# Optimizing a Trainium2 kernel written in Bass

```python
import jax, jax.numpy as jnp
from jax import lax
import numpy as np

D_MODEL = 2048
BATCH = 1
SEQ = 256
DEPTH = 1

PLE_DIM = 256
EPS = 1e-6
GM_CHUNK = 128
GM_GROUP_DIM = 128
GM_GROUPS = D_MODEL // 256
GM_WIDTH = GM_GROUPS * GM_GROUP_DIM
DN_HEAD_DIM = 128
DN_HEADS = D_MODEL // DN_HEAD_DIM
DN_WIDTH = DN_HEADS * DN_HEAD_DIM
DN_CONV = 4
DN_CHUNK = 64
D_FF = ((-(-(8 * D_MODEL) // 3) + 255) // 256) * 256
IN_SIZES = (2 * GM_WIDTH, 3 * DN_WIDTH, DN_WIDTH, DN_HEADS, DN_HEADS, 2 * D_MODEL)
IN_WIDTH = sum(IN_SIZES)
IN_SPLIT_POINTS = tuple(int(c) for c in np.cumsum(IN_SIZES)[:-1])

kernel_name = "hybrid_gmlp_gated_deltanet_block"

def rms_norm(x, gain):
    xf = x.astype(jnp.float32)
    xf = xf * lax.rsqrt(jnp.mean(xf * xf, axis=-1, keepdims=True) + EPS)
    return (xf * gain.astype(jnp.float32)).astype(x.dtype)

def l2norm(x):
    return x * lax.rsqrt(jnp.sum(x * x, axis=-1, keepdims=True) + EPS)

def chunked_spatial_gating(uv, v_gain, w_s, b_s):
    b, s, _ = uv.shape
    u, v = jnp.split(uv, 2, axis=-1)
    v = rms_norm(v, v_gain)
    v = v.reshape(b, s // GM_CHUNK, GM_CHUNK, GM_GROUPS, GM_GROUP_DIM)
    causal = jnp.tril(jnp.ones((GM_CHUNK, GM_CHUNK), dtype=bool))
    w = jnp.where(causal[None], w_s, 0.0)
    sv = jnp.einsum('gts,bnsgc->bntgc', w, v) + jnp.transpose(b_s)[None, None, :, :, None]
    return u * sv.reshape(b, s, GM_WIDTH)

def causal_short_conv(x, w):
    c = x.shape[-1]
    y = lax.conv_general_dilated(
        x, w[:, None, :].astype(x.dtype), window_strides=(1,),
        padding=((DN_CONV - 1, 0),), dimension_numbers=('NWC', 'WIO', 'NWC'),
        feature_group_count=c)
    return jax.nn.silu(y)

def gated_delta_rule(q, k, v, g, beta):
    out_dtype = v.dtype
    f32 = jnp.float32
    b, s, h, dk = q.shape
    dv = v.shape[-1]
    n = s // DN_CHUNK
    q = l2norm(q.astype(f32)) * (dk ** -0.5)
    k = l2norm(k.astype(f32))
    v = v.astype(f32)

    def chunks(t):
        t = t.reshape((b, n, DN_CHUNK, h) + t.shape[3:])
        return jnp.moveaxis(t, 3, 1)

    q, k, v = chunks(q), chunks(k), chunks(v)
    g = jnp.cumsum(chunks(g.astype(f32)), axis=-1)
    beta = chunks(beta.astype(f32))
    tril = jnp.tril(jnp.ones((DN_CHUNK, DN_CHUNK), dtype=bool))
    strict = jnp.tril(jnp.ones((DN_CHUNK, DN_CHUNK), dtype=bool), -1)
    diff = g[..., :, None] - g[..., None, :]
    decay = jnp.where(tril, jnp.exp(jnp.where(tril, diff, 0.0)), 0.0)
    k_beta = k * beta[..., None]
    m = jnp.where(strict, jnp.einsum('bhnid,bhnjd->bhnij', k_beta, k) * decay, 0.0)
    rhs = jnp.concatenate([v * beta[..., None], k_beta * jnp.exp(g)[..., None]], axis=-1)
    sol = lax.linalg.triangular_solve(m, rhs, left_side=True, lower=True, unit_diagonal=True)
    u_c, w_c = sol[..., :dv], sol[..., dv:]
    qk = jnp.einsum('bhnid,bhnjd->bhnij', q, k) * decay
    g_last = g[..., -1]
    q_dec = q * jnp.exp(g)[..., None]
    k_tail = k * jnp.exp(g_last[..., None] - g)[..., None]

    def step(state, xs):
        qk_i, u_i, w_i, qd_i, kt_i, gl_i = xs
        v_new = u_i - jnp.einsum('bhcd,bhde->bhce', w_i, state)
        o = jnp.einsum('bhcd,bhde->bhce', qd_i, state) + jnp.einsum('bhij,bhje->bhie', qk_i, v_new)
        state = state * jnp.exp(gl_i)[..., None, None] + jnp.einsum('bhcd,bhce->bhde', kt_i, v_new)
        return state, o

    xs = tuple(jnp.moveaxis(t, 2, 0) for t in (qk, u_c, w_c, q_dec, k_tail, g_last))
    state0 = jnp.zeros((b, h, dk, dv), f32)
    _, o = lax.scan(step, state0, xs)
    o = jnp.transpose(o, (1, 0, 3, 2, 4)).reshape(b, s, h, dv)
    return o.astype(out_dtype)

def setup_inputs(seed: int = 0) -> dict:
    key = jax.random.key(seed)
    ks = jax.random.split(key, 24)
    f32 = jnp.float32

    def normal(k, shape, scale):
        return jax.random.normal(k, shape, f32) * scale

    def gain(k, shape):
        return 1.0 + 0.02 * jax.random.normal(k, shape, f32)

    L = DEPTH
    x = jax.random.normal(ks[0], (BATCH, SEQ, D_MODEL), f32)
    p = jax.random.normal(ks[1], (DEPTH, BATCH, SEQ, PLE_DIM), f32)
    norm_mix = gain(ks[2], (L, D_MODEL))
    w_in = normal(ks[3], (L, D_MODEL, IN_WIDTH), D_MODEL ** -0.5)
    gm_v_norm = gain(ks[4], (L, GM_WIDTH))
    gm_w_s = normal(ks[5], (L, GM_GROUPS, GM_CHUNK, GM_CHUNK), GM_CHUNK ** -0.5)
    gm_b_s = 1.0 + 0.1 * jax.random.normal(ks[6], (L, GM_GROUPS, GM_CHUNK), f32)
    dn_conv_w = normal(ks[7], (L, DN_CONV, 3 * DN_WIDTH), DN_CONV ** -0.5)
    dn_a_log = jnp.log(jax.random.uniform(ks[8], (L, DN_HEADS), f32, 1.0, 16.0))
    dt = jnp.exp(jax.random.uniform(ks[9], (L, DN_HEADS), f32, np.log(1e-3), np.log(1e-1)))
    dn_dt_bias = dt + jnp.log(-jnp.expm1(-dt))
    dn_out_norm = gain(ks[10], (L, DN_HEAD_DIM))
    w_branch_a = normal(ks[11], (L, GM_WIDTH, D_MODEL), GM_WIDTH ** -0.5)
    w_branch_b = normal(ks[12], (L, DN_WIDTH, D_MODEL), DN_WIDTH ** -0.5)
    w_out = normal(ks[13], (L, D_MODEL, D_MODEL), D_MODEL ** -0.5)
    norm_ffn = gain(ks[14], (L, D_MODEL))
    w_gate_up = normal(ks[15], (L, D_MODEL, 2 * D_FF), D_MODEL ** -0.5)
    w_down = normal(ks[16], (L, D_FF, D_MODEL), D_FF ** -0.5)
    ple_norm = gain(ks[17], (L, D_MODEL))
    w_ple_gate = normal(ks[18], (L, D_MODEL, D_MODEL), D_MODEL ** -0.5)
    w_ple_proj = normal(ks[19], (L, PLE_DIM, D_MODEL), PLE_DIM ** -0.5)
    norm_final = gain(ks[20], (D_MODEL,))
    return {"x": x, "p": p, "norm_mix": norm_mix, "w_in": w_in, "gm_v_norm": gm_v_norm,
            "gm_w_s": gm_w_s, "gm_b_s": gm_b_s, "dn_conv_w": dn_conv_w, "dn_a_log": dn_a_log,
            "dn_dt_bias": dn_dt_bias, "dn_out_norm": dn_out_norm, "w_branch_a": w_branch_a,
            "w_branch_b": w_branch_b, "w_out": w_out, "norm_ffn": norm_ffn, "w_gate_up": w_gate_up,
            "w_down": w_down, "ple_norm": ple_norm, "w_ple_gate": w_ple_gate,
            "w_ple_proj": w_ple_proj, "norm_final": norm_final}

def reference(x, p, norm_mix, w_in, gm_v_norm, gm_w_s, gm_b_s, dn_conv_w, dn_a_log, dn_dt_bias,
              dn_out_norm, w_branch_a, w_branch_b, w_out, norm_ffn, w_gate_up, w_down,
              ple_norm, w_ple_gate, w_ple_proj, norm_final):
    b, s, _ = x.shape
    for i in range(DEPTH):
        h = rms_norm(x, norm_mix[i])
        proj = h @ w_in[i]
        gm_uv, dn_qkv, dn_z, dn_beta, dn_a, gate_logits = jnp.split(proj, IN_SPLIT_POINTS, axis=-1)
        y_a = chunked_spatial_gating(jax.nn.gelu(gm_uv, approximate=False), gm_v_norm[i], gm_w_s[i], gm_b_s[i])
        qkv = causal_short_conv(dn_qkv, dn_conv_w[i])
        q, k, v = jnp.split(qkv, 3, axis=-1)
        q = q.reshape(b, s, DN_HEADS, DN_HEAD_DIM)
        k = k.reshape(b, s, DN_HEADS, DN_HEAD_DIM)
        v = v.reshape(b, s, DN_HEADS, DN_HEAD_DIM)
        beta = jax.nn.sigmoid(dn_beta)
        g = -jnp.exp(dn_a_log[i].astype(jnp.float32)) * jax.nn.softplus(
            dn_a.astype(jnp.float32) + dn_dt_bias[i].astype(jnp.float32))
        o = gated_delta_rule(q, k, v, g, beta)
        o = rms_norm(o, dn_out_norm[i]) * jax.nn.silu(dn_z.reshape(b, s, DN_HEADS, DN_HEAD_DIM))
        y_b = o.reshape(b, s, DN_WIDTH)
        gate_a, gate_b = jnp.split(jax.nn.sigmoid(gate_logits), 2, axis=-1)
        merged = gate_a * (y_a @ w_branch_a[i]) + gate_b * (y_b @ w_branch_b[i])
        x = x + merged @ w_out[i]
        h = rms_norm(x, norm_ffn[i])
        f_gate, f_up = jnp.split(h @ w_gate_up[i], 2, axis=-1)
        x = x + (jax.nn.silu(f_gate) * f_up) @ w_down[i]
        ple_gate = jax.nn.sigmoid(rms_norm(x, ple_norm[i]) @ w_ple_gate[i])
        x = x + ple_gate * (p[i] @ w_ple_proj[i])
    return rms_norm(x, norm_final)


_drawn_inputs = setup_inputs


def setup_inputs(seed=0):
    import zlib

    import numpy as np

    out = dict(_drawn_inputs(seed))
    spreads = {}
    factors = {'norm_mix': 3.931,
     'gm_v_norm': 34.712,
     'dn_out_norm': 38.169,
     'norm_ffn': 13.637,
     'ple_norm': 200.0,
     'norm_final': 23.832,
     'gm_b_s': 4.299,
     'w_ple_gate': 21.872,
     'p': 8.0,
     'w_ple_proj': 8.0}
    for name, (base, spread) in spreads.items():
        noise = np.random.default_rng([zlib.crc32(name.encode()), seed]).standard_normal(out[name].shape)
        drawn = base * np.exp(spread * noise) if base else spread * noise
        out[name] = __import__('jax').numpy.asarray(drawn.astype(out[name].dtype))
    for name, factor in factors.items():
        out[name] = (out[name] * factor).astype(out[name].dtype)
    return out
```

```python
import numpy as np

import concourse.bass as bass
from concourse import mybir

F32 = mybir.dt.float32
F32R = mybir.dt.float32r
ACT = mybir.ActivationFunctionType
ALU = mybir.AluOpType
ds = bass.ds

P = 128
SEQ = 256
D = 2048
TILES = SEQ // P
KD = D // P
HEADS = 16
GROUP = 4
NGROUPS = HEADS // GROUP
GM = 1024
GMT = GM // P
FF = 5632
KF = FF // P
PLE = 256
COLS = 512
HALF_K = 2
RING = 4
LEAD = 3
EPS = 1e-6
BIG = 1e30
HID = D // P // HALF_K
HGM = GM // P // HALF_K
HFF = KF // HALF_K
NB = D // COLS
FB = FF // COLS

BLK_U, BLK_V, BLK_Q, BLK_K, BLK_DV, BLK_Z, BLK_GA, BLK_GB = 0, 2, 4, 8, 12, 16, 20, 24

C_MIX, C_FFN, C_PLE, C_FIN, C_GMV, C_DNO, C_CONV = 0, 16, 32, 48, 64, 72, 73
NCOL = C_CONV + 4 * 48

PLAN = [("qkv", 4, 3 * HID, (2, 1)), ("uv", 1, 4 * HID, (2, 2)), ("z", 2, 2 * HID, (1, 1)),
        ("mix", NB, 3 * HID + HGM, (2, 2)), ("out", 2, 2 * HID, (1, 1)), ("ffn", FB, 2 * HID, (1, 1)),
        ("down", 2, 2 * HFF, (1, 1)), ("proj", 1, 4, (2, 2)), ("ple", 2, 2 * HID, (1, 1))]
H0, PER, U0 = {}, {}, {}
_h, _u = 0, [0, 0]
for _name, _n, _per, _uses in PLAN:
    H0[_name], PER[_name], U0[_name] = _h, _per, (tuple(_u), _uses)
    _h += _n * _per
    _u = [_u[0] + _n * _uses[0], _u[1] + _n * _uses[1]]
TOTAL = _h


def half_of(phase, i, n):
    return H0[phase] + PER[phase] * i + n


def use_of(phase, i, buf, n):
    base, per = U0[phase]
    return base[buf] + per[buf] * i + n


def build(nc, win, wba, wa, wb, wo, wgu, wd, wpg, wpp, xT_d, pT_d, cols_d, hv_d, gmw_d, gmb_d, out_d):
    scratch_m = nc.dram_tensor("inv_in", (4, 8, 32, 32), F32, kind="Internal").ap()
    scratch_x = nc.dram_tensor("inv_out", (2, 4, 8, 32, 32), F32, kind="Internal").ap()

    cursor = [(nc.sbuf_base + 63) // 64 * 64]

    def at(name, shape, dt, offset=None):
        size = int(np.prod(shape[1:])) * 4
        if offset is None:
            offset = cursor[0]
            cursor[0] += (size + 31) // 32 * 32
        return nc.alloc_sbuf_tensor_at(name, shape, dt, offset=offset)

    def sem(name):
        return nc.alloc_semaphore(name)

    raw = at("raw", [P, RING, HALF_K, COLS], F32)
    whi = at("whi", [P, RING, HALF_K, COLS], F32R)
    wlo = at("wlo", [P, RING, HALF_K, COLS], F32R)
    xT = at("xT", [P, KD, SEQ], F32)
    ahi = at("ahi", [P, KD, SEQ], F32R)
    alo = at("alo", [P, KD, SEQ], F32R)
    region = cursor[0]
    cursor[0] += 2 * KF * SEQ * 4

    def shared(name, shape, dt, kib):
        return at(name, shape, dt, offset=region + int(kib * 1024))

    oT = shared("oT", [P, HEADS, SEQ], F32, 0)
    conv = [shared(f"conv_{c}", [P, GROUP, SEQ], F32, 16 + 4 * n) for n, c in enumerate("qkv")]
    qn = shared("qn", [P, GROUP, SEQ], F32, 28)
    kn = shared("kn", [P, GROUP, SEQ], F32, 32)
    vbeta = shared("vbeta", [P, 8, P], F32, 36)
    kbeg = shared("kbeg", [P, GROUP, P], F32, 40)
    ktail = shared("ktail", [P, GROUP, P], F32, 42)
    qdec = shared("qdec", [P, GROUP, P], F32, 44)
    negm = shared("negm", [P, 8, P], F32, 46)
    qkT = shared("qkT", [P, 8, P], F32, 50)
    inv = shared("inv", [P, 8, P], F32, 54)
    invT = shared("invT", [P, 8, P], F32, 58)
    blk_m = shared("blk_m", [32, 32, 32], F32, 62)
    blk_x = shared("blk_x", [32, 32, 32], F32, 66)
    blk_t = shared("blk_t", [32, 32, 32], F32, 70)
    vnew = shared("vnew", [P, 8, P], F32, 74)
    p32 = shared("p32", [P, 8, 32], F32, 78)
    p64 = shared("p64", [64, 8, 64], F32, 79)
    nwT = shared("nwT", [P, GROUP, P], F32, 81)
    state = shared("state", [P, GROUP, P], F32, 83)
    vg = shared("vg", [P, TILES, GM], F32, 16)
    uT = shared("uT", [P, GMT, SEQ], F32, 28)
    gmw = shared("gmw", [P, GMT, P], F32, 62)
    gmb = shared("gmb", [P, GMT, P], F32, 66)
    ytmp = shared("ytmp", [P, GMT, SEQ], F32, 16)
    wba_sb = shared("wba_sb", [P, KD, 48], F32, 62)
    g1 = shared("g1", [48, SEQ], F32, 66)
    g2 = shared("g2", [48, SEQ], F32, 67)
    praw = shared("praw", [P, PLE // P, SEQ], F32, 70)
    mask_m = shared("mask_m", [P, P], F32, 85)
    mask_q = shared("mask_q", [P, P], F32, 85.5)
    bg = shared("bg", [80, SEQ], F32, 86)
    ident = shared("ident", [P, P], F32, 87)
    yahi = shared("yahi", [P, GMT, SEQ], F32R, 72)
    yalo = shared("yalo", [P, GMT, SEQ], F32R, 80)
    ybhi = shared("ybhi", [P, KD, SEQ], F32R, 40)
    yblo = shared("yblo", [P, KD, SEQ], F32R, 56)
    mhi = shared("mhi", [P, KD, SEQ], F32R, 0)
    mlo = shared("mlo", [P, KD, SEQ], F32R, 16)
    fhi = shared("fhi", [P, KF, SEQ], F32R, 0)
    flo = shared("flo", [P, KF, SEQ], F32R, 44)
    pw = shared("pw", [P, KD, SEQ], F32, 0)

    cols = at("cols", [P, NCOL], F32)
    ones = at("ones", [P, P], F32)
    R = at("R", [P, SEQ], F32)
    Rt = at("Rt", [P, SEQ], F32)
    hv = at("hv", [48, 3], F32)
    tok = at("tok", [P, 5, TILES, HEADS], F32)
    selg = at("selg", [48, GROUP], F32)
    rcol = at("rcol", [P, TILES], F32)
    vsum = at("vsum", [P, 2, TILES], F32)
    vrms = at("vrms", [P, TILES], F32)
    sqsum = at("sqsum", [P, 2, SEQ], F32)
    t = [at(f"t{n}", [P, GROUP, SEQ], F32) for n in range(3)]
    pre_at = cursor[0]
    pre = at("pre", [P, GROUP, SEQ + 4], F32)
    phi = at("phi", [P, PLE // P, SEQ], F32R, offset=pre_at)
    plo = at("plo", [P, PLE // P, SEQ], F32R, offset=pre_at + 2048)

    acc = [nc.alloc_psum_tensor(f"acc{n}", [P, 2, COLS], F32) for n in range(2)]
    ps = [nc.alloc_psum_tensor(f"ps{n}", [P, 2, COLS], F32) for n in range(2)]
    psf = [x[:].rearrange("p a n -> p (a n)") for x in ps]

    def heads(flat, width):
        return flat.rearrange("p (h n) -> p h n", n=width)

    accv = [heads(a[:].rearrange("p a n -> p (a n)"), SEQ) for a in acc]
    psv = [heads(x, SEQ) for x in psf]
    psq = [heads(x, P) for x in psf]

    raw_in = [sem(f"raw_in{n}") for n in range(RING)]
    hi_done, lo_done, half_used = sem("hi_done"), sem("lo_done"), sem("half_used")
    acc_read = [sem(f"acc_read{n}") for n in range(2)]
    cols_in, x_in, ba_in, gm_in = sem("cols_in"), [sem(f"x_in{n}") for n in range(4)], sem("ba_in"), sem("gm_in")
    pool_step, waits_carried = sem("pool_step"), sem("waits_carried")
    consts_made, wba_scaled = sem("consts_made"), sem("wba_scaled")
    sq_added, sq_summed, mean_inv, r_done = sem("sq_added"), sem("sq_summed"), sem("mean_inv"), sem("r_done")
    x0_gain, x0_sq, x0_hi, x0_lo = sem("x0_gain"), sem("x0_sq"), sem("x0_hi"), sem("x0_lo")
    ba_out, rcol_out, rcol_done = sem("ba_out"), sem("rcol_out"), sem("rcol_done")
    ba_dve, ba_act, tok_T, tok_done = sem("ba_dve"), sem("ba_act"), sem("tok_T"), sem("tok_done")
    tok_eg = sem("tok_eg")
    pre_done, conv_mac, conv_done, conv_silu = sem("pre_done"), sem("conv_mac"), sem("conv_done"), sem("conv_silu")
    convv_done, convv_silu = sem("convv_done"), sem("convv_silu")
    qk_sq, sel_done, g_out = sem("qk_sq"), sem("sel_done"), sem("g_out")
    k_len, q_len, qk_mean, qk_inv, qk_root = sem("k_len"), sem("q_len"), sem("qk_mean"), sem("qk_inv"), sem("qk_root")
    qk_normed, diff_done, decay_done, qdec_done = sem("qk_normed"), sem("diff_done"), sem("decay_done"), sem("qdec_done")
    gram_m_out, gram_q_out, negm_done, qkT_done = sem("gram_m_out"), sem("gram_q_out"), sem("negm_done"), sem("qkT_done")
    kT_out, vT_out, kv_scaled = sem("kT_out"), sem("vT_out"), sem("kv_scaled")
    m_stored, m_in, x_inv, x_stored, x_placed, inv_zero = (sem("m_stored"), sem("m_in"), sem("x_inv"), sem("x_stored"),
                                                           sem("x_placed"), sem("inv_zero"))
    merge_out, merge_act, merge_dve = sem("merge_out"), sem("merge_act"), sem("merge_dve")
    delta_out, delta_act, delta_dve = sem("delta_out"), sem("delta_act"), sem("delta_dve")
    o_len, o_mean, o_root, ps_free = sem("o_len"), sem("o_mean"), sem("o_root"), sem("ps_free")
    gm_masked, v_gelu, v_mean, v_root, v_normed = sem("gm_masked"), sem("v_gelu"), sem("v_mean"), sem("v_root"), sem("v_normed")
    u_scaled, u_gelu, sv_out, sv_biased, ya_dve, ya_hi, ya_lo = (sem("u_scaled"), sem("u_gelu"), sem("sv_out"), sem("sv_biased"),
                                                               sem("ya_dve"), sem("ya_hi"), sem("ya_lo"))
    z_scaled, z_silu, z_gated, yb_hi, yb_lo = sem("z_scaled"), sem("z_silu"), sem("z_gated"), sem("yb_hi"), sem("yb_lo")
    gate_scaled, gate_sig, mix_prod, mix_hi, mix_lo = sem("gate_scaled"), sem("gate_sig"), sem("mix_prod"), sem("mix_hi"), sem("mix_lo")
    res = [{k: sem(f"{k}{n}") for k in ("x", "sq", "gain", "added", "hi", "lo")} for n in range(2)]
    ff_scaled, ff_silu, ff_gate, ff_prod, ff_hi, ff_lo = (sem("ff_scaled"), sem("ff_silu"), sem("ff_gate"), sem("ff_prod"),
                                                        sem("ff_hi"), sem("ff_lo"))
    p_in, p_hi, p_lo, pw_done = sem("p_in"), sem("p_hi"), sem("p_lo"), sem("pw_done")
    ple_scaled, ple_sig, ple_prod, ple_x, ple_sq, ple_gain = (sem("ple_scaled"), sem("ple_sig"), sem("ple_prod"), sem("ple_x"),
                                                            sem("ple_sq"), sem("ple_gain"))
    out_dve, out_pool, stored = sem("out_dve"), sem("out_pool"), sem("stored")

    def load_half(sp, src, row, h, n):
        if not (isinstance(h, int) and h < RING):
            sp.wait_ge(lo_done, h - RING + 1)
        sp.dma_start(raw[:, n % RING], src[ds(row, P), :].rearrange("p (k n) -> p k n", k=HALF_K)).then_inc(raw_in[n % RING], 16)

    def split_hi(act, phase, i, n):
        h, s = half_of(phase, i, n + LEAD), (n + LEAD) % RING
        if isinstance(h, int) and h >= TOTAL:
            return
        act.wait_ge(raw_in[s], i * (16 * PER[phase] // RING) + 16 * (H0[phase] // RING + (n + LEAD) // RING + 1))
        if not (isinstance(h, int) and h < RING):
            act.wait_ge(half_used, h - RING + 1)
        nc.scalar.activation(whi[:, s], raw[:, s], ACT.Copy).then_inc(hi_done, 1)

    def split_lo(dve, phase, i, n):
        h, s = half_of(phase, i, n + LEAD), (n + LEAD) % RING
        if isinstance(h, int) and h >= TOTAL:
            return
        dve.wait_ge(hi_done, h + 1)
        nc.vector.tensor_tensor(wlo[:, s], raw[:, s], whi[:, s].bitcast(F32), ALU.subtract).then_inc(lo_done, 1)

    def use_half(pe, phase, i, n, buf, first, last, kt0, xhi, xlo, rows=False):
        s = n % RING
        pe.wait_ge(lo_done, half_of(phase, i, n) + 1)
        for kt in range(HALF_K):
            k = kt0 + kt
            begin, end = first and kt == 0, last and kt == HALF_K - 1
            if rows:
                for m in range(TILES):
                    xh, xl = xhi[:, k, m * P:(m + 1) * P], xlo[:, k, m * P:(m + 1) * P]
                    o = acc[buf][:, m]
                    nc.tensor.matmul(o, xh, whi[:, s, kt], start=begin, stop=False, skip_group_check=True)
                    nc.tensor.matmul(o, xh, wlo[:, s, kt], start=False, stop=False, skip_group_check=True)
                    mm = nc.tensor.matmul(o, xl, whi[:, s, kt], start=False, stop=end, skip_group_check=True)
            else:
                for m in range(4):
                    o = accv[buf][:, m]
                    wh, wl = whi[:, s, kt, m * P:(m + 1) * P], wlo[:, s, kt, m * P:(m + 1) * P]
                    nc.tensor.matmul(o, wh, xhi[:, k], start=begin and m % 2 == 0, stop=False, skip_group_check=True)
                    nc.tensor.matmul(o, wh, xlo[:, k], start=False, stop=False, skip_group_check=True)
                    mm = nc.tensor.matmul(o, wl, xhi[:, k], start=False, stop=end, skip_group_check=True)
        mm.then_inc(half_used, 1)

    def acc_free(pe, phase, i, buf, n):
        u = use_of(phase, i, buf, n)
        if not (isinstance(u, int) and u == 0):
            pe.wait_ge(acc_read[buf], u)

    def acc_full(eng, phase, i, end):
        eng.wait_ge(half_used, half_of(phase, i, end))

    def carry_wait(eng):
        eng.sem_inc(waits_carried, 1)

    def bc(ap, n):
        return ap.unsqueeze(2).to_broadcast([ap.shape[0], ap.shape[1], n])

    def over(r, n):
        return r.unsqueeze(1).to_broadcast([r.shape[0], n, r.shape[1]])

    def piece(ap, j):
        return ap[:, 2 * j:2 * j + 2]

    def tiles(ap, blk, j):
        return ap[:, ds(4 * blk + 2 * j, 2)]

    with nc.Block() as block:

        @block.sync
        def _(sp):
            sp.dma_start(cols[:], cols_d).then_inc(cols_in, 16)
            for c in range(4):
                sp.dma_start(xT[:, 4 * c:4 * c + 4], xT_d[:, 4 * c:4 * c + 4]).then_inc(x_in[c], 16)
                load_half(sp, win, (BLK_Q * HID + c) * P, c, c)
            sp.dma_start(wba_sb[:], wba).then_inc(ba_in, 16)
            sp.dma_start(hv[32:48, 0:2], hv_d).then_inc(ba_in, 16)

            def w_in_block(phase, i, blk, n0, skip=0):
                for n in range(skip, HID):
                    load_half(sp, win, (blk * HID + n) * P, half_of(phase, i, n0 + n), n0 + n)

            w_in_block("qkv", 0, BLK_Q, 0, RING)
            w_in_block("qkv", 0, BLK_K, HID)
            w_in_block("qkv", 0, BLK_DV, 2 * HID)
            with sp.Fori(1, NGROUPS) as g:
                w_in_block("qkv", g, BLK_Q + g, 0)
                w_in_block("qkv", g, BLK_K + g, HID)
                w_in_block("qkv", g, BLK_DV + g, 2 * HID)
            w_in_block("uv", 0, BLK_V, 0)
            w_in_block("uv", 0, BLK_V + 1, HID)
            w_in_block("uv", 0, BLK_U, 2 * HID)
            w_in_block("uv", 0, BLK_U + 1, 3 * HID)
            with sp.Fori(0, 2) as i:
                for b in range(2):
                    w_in_block("z", i, BLK_Z + 2 * i + b, b * HID)
            with sp.Fori(0, NB) as i:
                w_in_block("mix", i, BLK_GA + i, 0)
                w_in_block("mix", i, BLK_GB + i, HID)
                for n in range(HGM):
                    load_half(sp, wa, (i * HGM + n) * P, half_of("mix", i, 2 * HID + n), 2 * HID + n)
                for n in range(HID):
                    load_half(sp, wb, (i * HID + n) * P, half_of("mix", i, 2 * HID + HGM + n), 2 * HID + HGM + n)
            with sp.Fori(0, 2) as i:
                for n in range(2 * HID):
                    load_half(sp, wo, (i * (2 * HID) + n) * P, half_of("out", i, n), n)
            with sp.Fori(0, FB) as i:
                for b in range(2):
                    for n in range(HID):
                        load_half(sp, wgu, ((i + b * FB) * HID + n) * P, half_of("ffn", i, b * HID + n), b * HID + n)
            with sp.Fori(0, 2) as i:
                for n in range(2 * HFF):
                    load_half(sp, wd, (i * (2 * HFF) + n) * P, half_of("down", i, n), n)
            for n in range(NB):
                load_half(sp, wpp, n * P, half_of("proj", 0, n), n)
            with sp.Fori(0, 2) as i:
                for n in range(2 * HID):
                    load_half(sp, wpg, (i * (2 * HID) + n) * P, half_of("ple", i, n), n)
            for c in range(4):
                if c == 3:
                    sp.wait_ge(out_pool, 1)
                else:
                    sp.wait_ge(out_dve, c + 1)
                sp.dma_start(out_d[:, 4 * c:4 * c + 4], xT[:, 4 * c:4 * c + 4]).then_inc(stored, 16)
            sp.wait_ge(stored, 64)

        @block.gpsimd
        def _(pool):
            g = nc.gpsimd

            def chain(ins, value):
                ins.then_inc(pool_step, 1)
                pool.wait_ge(pool_step, value)

            g.memset(ones[:], 1.0).then_inc(consts_made, 1)
            chain(g.memset(ident[:], 0.0), 1)
            g.affine_select(out=ident[:], in_=ident[:], compare_op=ALU.not_equal, fill=1.0, base=0,
                            pattern=[[-1, P]], channel_multiplier=1).then_inc(consts_made, 1)
            chain(g.memset(mask_m[:], 0.0), 2)
            g.affine_select(out=mask_m[:], in_=mask_m[:], compare_op=ALU.is_gt, fill=BIG, base=0,
                            pattern=[[-1, P]], channel_multiplier=1).then_inc(consts_made, 1)
            chain(g.memset(mask_q[:], 0.0), 3)
            g.affine_select(out=mask_q[:], in_=mask_q[:], compare_op=ALU.is_ge, fill=-BIG, base=0,
                            pattern=[[1, P]], channel_multiplier=-1).then_inc(consts_made, 1)
            g.memset(bg[:], 0.0).then_inc(consts_made, 1)
            g.memset(pre[:, :, 0:4], 0.0).then_inc(consts_made, 1)
            chain(g.memset(sqsum[:], 0.0), 4)
            for c in range(4):
                pool.wait_ge(x0_sq, c + 1)
                chain(g.tensor_tensor(sqsum[:], sqsum[:], piece(t[1], 0), ALU.add), 5 + c)
                g.tensor_tensor(sqsum[:], sqsum[:], piece(t[1], 1), ALU.add).then_inc(sq_added, 1)
                pool.wait_ge(sq_added, c + 1)
            pool.wait_ge(cols_in, 16)
            pool.wait_ge(ba_in, 32)
            g.tensor_tensor(wba_sb[:], wba_sb[:], bc(cols[:, C_MIX:C_MIX + KD], 48), ALU.mult).then_inc(wba_scaled, 1)

            CONV_STEPS, INV_STEPS = 6, 64

            def convolve_v(g_, v):
                pool.wait_ge(pre_done, 3 * g_ + 3)
                y = conv[2]
                for tap in range(4):
                    w = bc(cols[:, ds(C_CONV + tap * 48 + 2 * HEADS + GROUP * g_, GROUP)], SEQ)
                    src = pre[:, :, 1 + tap:1 + tap + SEQ]
                    if tap == 0:
                        chain(g.tensor_tensor(y[:], src, w, ALU.mult), v + 1)
                        continue
                    chain(g.tensor_tensor(t[2][:], src, w, ALU.mult), v + 2 * tap)
                    last = g.tensor_tensor(y[:], y[:], t[2][:], ALU.add)
                    if tap < 3:
                        chain(last, v + 2 * tap + 1)
                last.then_inc(convv_done, 1)

            def before_inverse(d):
                for n, (src, dst, r) in enumerate(((conv[1], kn, t[1]), (conv[0], qn, t[0]))):
                    pool.wait_ge(qk_root, 2 * d + n + 1)
                    g.tensor_tensor(dst[:], src[:], r[:], ALU.mult).then_inc(qk_normed, 1)
                    if n == 0:
                        g.memset(inv[:], 0.0)
                        g.memset(invT[:], 0.0).then_inc(inv_zero, 1)
                pool.wait_ge(decay_done, 3 * d + 1)
                pool.wait_ge(qk_normed, 2 * d + 2)
                g.tensor_tensor(qdec[:], qn[:, :, P:SEQ], vnew[:, 4:8, :], ALU.mult).then_inc(qdec_done, 1)

            def invert(d, v):
                pool.wait_ge(negm_done, d + 1)
                carry_wait(pool)
                for a in range(4):
                    pool.dma_start(scratch_m[a].rearrange("h i j -> i h j"),
                                   negm[32 * a:32 * a + 32, :, 32 * a:32 * a + 32]).then_inc(m_stored, 16)
                chain(g.memset(blk_x[:], 0.0), v + 1)
                carry_wait(pool)
                chain(g.memset(blk_x[:].rearrange("p i j -> p (i j)")[:, 0:1024:33], 1.0), v + 2)
                pool.wait_ge(m_stored, 64 * (d + 1))
                carry_wait(pool)
                pool.dma_start(blk_m[:], scratch_m.rearrange("a h i j -> (a h) i j")).then_inc(m_in, 16)
                pool.wait_ge(m_in, 16 * (d + 1))
                for j in range(31):
                    r, c = 31 - j, j + 1
                    tmp = blk_t[:, 0:r, 0:c]
                    chain(g.tensor_tensor(tmp, blk_m[:, j + 1:32, j:j + 1].to_broadcast([32, r, c]),
                                          blk_x[:, j:j + 1, 0:c].to_broadcast([32, r, c]), ALU.mult), v + 3 + 2 * j)
                    chain(g.tensor_tensor(blk_x[:, j + 1:32, 0:c], blk_x[:, j + 1:32, 0:c], tmp, ALU.add), v + 4 + 2 * j)
                carry_wait(pool)
                g.tensor_copy(blk_t[:], blk_x[:].rearrange("p i j -> p j i")).then_inc(x_inv, 1)
                pool.wait_ge(x_inv, d + 1)
                carry_wait(pool)
                pool.dma_start(scratch_x[0].rearrange("a h i j -> (a h) i j"), blk_x[:]).then_inc(x_stored, 16)
                pool.dma_start(scratch_x[1].rearrange("a h i j -> (a h) i j"), blk_t[:]).then_inc(x_stored, 16)
                pool.wait_ge(x_stored, 32 * (d + 1))
                pool.wait_ge(inv_zero, d + 1)
                carry_wait(pool)
                for a in range(4):
                    for which, dst in enumerate((inv, invT)):
                        pool.dma_start(dst[32 * a:32 * a + 32, :, 32 * a:32 * a + 32],
                                       scratch_x[which, a].rearrange("h i j -> i h j")).then_inc(x_placed, 16)

            v0 = 8
            convolve_v(0, v0)
            v0 += CONV_STEPS

            with pool.Fori(1, NGROUPS) as g_:
                v = v0 + (g_ - 1) * (INV_STEPS + CONV_STEPS)
                before_inverse(g_ - 1)
                invert(g_ - 1, v)
                convolve_v(g_, v + INV_STEPS)
            v0 += (NGROUPS - 1) * (INV_STEPS + CONV_STEPS)
            before_inverse(NGROUPS - 1)
            invert(NGROUPS - 1, v0)
            v0 += INV_STEPS
            pool.wait_ge(x_placed, 128 * NGROUPS)
            pool.dma_start(gmw[:], gmw_d).then_inc(gm_in, 16)
            pool.dma_start(gmb[:].rearrange("p g n -> p (g n)"), gmb_d.to_broadcast([P, GM])).then_inc(gm_in, 16)
            pool.dma_start(praw[:], pT_d).then_inc(p_in, 16)
            pool.wait_ge(gm_in, 32)
            g.affine_select(out=gmw[:], in_=gmw[:], compare_op=ALU.is_ge, fill=0.0, base=0,
                            pattern=[[0, GMT], [1, P]], channel_multiplier=-1).then_inc(gm_masked, 1)

            def residual(n, gain):
                s = res[n]
                pool.wait_ge(sq_summed, n + 1)
                g.memset(sqsum[:], 0.0).then_inc(s["added"], 1)
                pool.wait_ge(s["added"], 1)
                with pool.Fori(0, 2) as i:
                    for b in range(2):
                        for j in range(2):
                            q = 4 * i + 2 * b + j
                            pool.wait_ge(s["x"], q + 1)
                            g.tensor_tensor(piece(t[0], j), tiles(xT, 2 * i + b, j),
                                            bc(cols[:, ds(gain + 4 * (2 * i + b) + 2 * j, 2)], SEQ), ALU.mult).then_inc(s["gain"], 1)
                            pool.wait_ge(s["sq"], q + 1)
                            g.tensor_tensor(sqsum[:], sqsum[:], piece(t[1], j), ALU.add).then_inc(s["added"], 1)
                            pool.wait_ge(s["added"], q + 2)

            residual(0, C_FFN)
            with pool.Fori(0, FB) as i:
                for j in range(2):
                    pool.wait_ge(ff_silu, 2 * i + j + 1)
                    g.tensor_tensor(piece(t[1], j), piece(t[0], j), over(R[:], 2), ALU.mult).then_inc(ff_gate, 1)
            residual(1, C_PLE)
            pool.wait_ge(sq_summed, 3)
            chain(g.memset(sqsum[:], 0.0), v0 + 1)
            for b in range(NB):
                for j in range(2):
                    q = 2 * b + j
                    pool.wait_ge(ple_sig, q + 1)
                    if b == 0:
                        pool.wait_ge(pw_done, NB)
                    g.tensor_tensor(piece(t[0], j), piece(t[0], j), tiles(pw, b, j), ALU.mult).then_inc(ple_prod, 1)
                for j in range(2):
                    q = 2 * b + j
                    pool.wait_ge(ple_sq, q + 1)
                    g.tensor_tensor(sqsum[:], sqsum[:], piece(t[1], j), ALU.add).then_inc(sq_added, 1)
                    g.tensor_tensor(tiles(xT, b, j), tiles(xT, b, j),
                                    bc(cols[:, C_FIN + 4 * b + 2 * j:C_FIN + 4 * b + 2 * j + 2], SEQ), ALU.mult).then_inc(ple_gain, 1)
                    pool.wait_ge(sq_added, 5 + q)
            pool.wait_ge(r_done, 4)
            pool.wait_ge(ple_gain, 8)
            g.tensor_tensor(xT[:, 12:16], xT[:, 12:16], over(R[:], 4), ALU.mult).then_inc(out_pool, 1)

        @block.tensor
        def _(pe):
            mm = nc.tensor.matmul

            def gemm(phase, i, n0, halves, buf, use, xhi, xlo, rows=False, after=None):
                acc_free(pe, phase, i, buf, use)
                for n in range(halves):
                    use_half(pe, phase, i, n0 + n, buf, n == 0, n == halves - 1, HALF_K * n, xhi, xlo, rows)
                    if after and n in after:
                        after[n]()

            def sum_squares(n):
                for k in range(2):
                    last = mm(psf[0][:, 0:SEQ], ones[:], sqsum[:, k], start=(k == 0), stop=(k == 1))
                last.then_inc(sq_summed, 1)

            def beta_a():
                pe.wait_ge(wba_scaled, 1)
                for k in range(KD):
                    last = mm(psf[1][0:48, 0:SEQ], wba_sb[:, k], xT[:, k], start=(k == 0), stop=(k == KD - 1))
                last.then_inc(ba_out, 1)
                pe.wait_ge(r_done, 1)
                for m in range(TILES):
                    last = mm(psf[0][:, COLS + m:COLS + m + 1], R[0:1, m * P:(m + 1) * P], ones[0:1, 0:1], start=True, stop=True)
                last.then_inc(rcol_out, 1)

            def tok_columns():
                pe.wait_ge(ba_act, 5)
                pe.wait_ge(ba_dve, 7)
                pe.wait_ge(rcol_done, 1)
                for m in range(TILES):
                    last = nc.tensor.transpose(psf[0][:, m * 80:m * 80 + 80], bg[:, m * P:(m + 1) * P], ident[0:80, 0:80])
                last.then_inc(tok_T, 1)

            def first_sum():
                pe.wait_ge(sq_added, 4)
                sum_squares(0)

            pe.wait_ge(consts_made, 6)
            def x_part(c):
                return lambda: pe.wait_ge(x0_lo, c + 1)
            x_part(0)()
            gemm("qkv", 0, 0, HID, 0, 0, ahi, alo,
                 after={1: lambda: (x_part(1)(), first_sum()), 3: x_part(2), 4: beta_a, 5: x_part(3)})
            gemm("qkv", 0, HID, HID, 1, 0, ahi, alo, after={4: tok_columns})
            gemm("qkv", 0, 2 * HID, HID, 0, 1, ahi, alo)

            def tok_tile(ap, h, m):
                return ap[:, h, m * P:(m + 1) * P]

            def lengths(n, bank, signal, d):
                for b in range(2):
                    last = mm(ps[bank][:, b], ones[:], piece(t[n], b).rearrange("p h n -> p (h n)"), start=True, stop=True)
                last.then_inc(signal, 1)

            def start_group(d):
                pe.wait_ge(sel_done, d + 1)
                pe.wait_ge(ps_free, d + 1)
                for h in range(GROUP):
                    last = mm(psv[1][:, h], selg[32:48, h:h + 1].to_broadcast([16, P]), bg[32:48, :], start=True, stop=True)
                last.then_inc(g_out, 1)
                pe.wait_ge(qk_sq, 2 * d + 2)
                lengths(1, 0, k_len, d)

            def q_lengths(d):
                pe.wait_ge(diff_done, 2 * d + 2)
                pe.wait_ge(decay_done, 3 * d + 1)
                lengths(0, 1, q_len, d)

            def gram_m(d):
                pe.wait_ge(qk_normed, 2 * d + 1)
                pe.wait_ge(qk_mean, 2 * d + 1)
                for m in range(TILES):
                    for h in range(GROUP):
                        last = mm(psq[0][:, 4 * m + h], tok_tile(kn, h, m), tok_tile(kn, h, m), start=True, stop=True)
                last.then_inc(gram_m_out, 1)

            def transposes(d):
                pe.wait_ge(qk_mean, 2 * d + 2)
                pe.wait_ge(convv_silu, d + 1)
                for m in range(TILES):
                    for h in range(GROUP):
                        last = nc.tensor.transpose(psq[1][:, 4 * m + h], tok_tile(conv[2], h, m), ident[:])
                last.then_inc(vT_out, 1)
                pe.wait_ge(negm_done, d + 1)
                for m in range(TILES):
                    for h in range(GROUP):
                        last = nc.tensor.transpose(psq[0][:, 4 * m + h], tok_tile(kn, h, m), ident[:])
                last.then_inc(kT_out, 1)

            def gram_q(d):
                pe.wait_ge(qk_normed, 2 * d + 2)
                pe.wait_ge(kv_scaled, 4 * d + 2)
                for m in range(TILES):
                    for h in range(GROUP):
                        last = mm(psq[1][:, 4 * m + h], tok_tile(kn, h, m), tok_tile(qn, h, m), start=True, stop=True)
                last.then_inc(gram_q_out, 1)

            PAIRS = ((0, 32), (64, 96))

            def merge32_a(d):
                pe.wait_ge(x_placed, 128 * (d + 1))
                pe.wait_ge(kv_scaled, 4 * d + 4)
                carry_wait(pe)
                for a, (top, low) in enumerate(PAIRS):
                    for x in range(8):
                        last = mm(ps[0][top:top + 32, a, 32 * x:32 * x + 32], negm[low:low + 32, x, top:top + 32],
                                  invT[low:low + 32, x, low:low + 32], start=True, stop=True)
                last.then_inc(merge_out, 1)

            def merge32_b(d):
                pe.wait_ge(merge_act, 3 * d + 2)
                pe.wait_ge(qkT_done, d + 1)
                carry_wait(pe)
                for a, (top, low) in enumerate(PAIRS):
                    for x in range(8):
                        last = mm(ps[1][top:top + 32, a, 32 * x:32 * x + 32], inv[top:top + 32, x, top:top + 32],
                                  p32[top:top + 32, x], start=True, stop=True)
                for x in range(8):
                    last = mm(ps[1][32:64, 0, 256 + 32 * x:288 + 32 * x], p32[0:32, x], inv[0:32, x, 0:32], start=True, stop=True)
                last.then_inc(merge_out, 1)

            def merge64_a(d):
                pe.wait_ge(merge_dve, 4 * d + 2)
                pe.wait_ge(merge_act, 3 * d + 3)
                carry_wait(pe)
                for x in range(8):
                    last = mm(ps[0][0:64, 0, 64 * x:64 * x + 64], negm[64:128, x, 0:64], invT[64:128, x, 64:128], start=True, stop=True)
                last.then_inc(merge_out, 1)

            def merge64_b(d):
                pe.wait_ge(merge_dve, 4 * d + 3)
                carry_wait(pe)
                for x in range(8):
                    last = mm(ps[0][0:64, 1, 64 * x:64 * x + 64], inv[0:64, x, 0:64], p64[:, x], start=True, stop=True)
                last.then_inc(merge_out, 1)

            def first_tile(d):
                pe.wait_ge(merge_dve, 4 * d + 4)
                for h in range(GROUP):
                    last = mm(psq[1][:, h], invT[:, h], vbeta[:, h], start=True, stop=True)
                last.then_inc(delta_out, 1)
                for h in range(GROUP):
                    last = mm(psq[1][:, 4 + h], kbeg[:, h], invT[:, 4 + h], start=True, stop=True)
                last.then_inc(delta_out, 1)

            def carry(d):
                pe.wait_ge(delta_act, 3 * d + 1)
                for h in range(GROUP):
                    last = mm(psq[0][:, h], ktail[:, h], vnew[:, h], start=True, stop=True)
                last.then_inc(delta_out, 1)

            def second_tile(d):
                pe.wait_ge(delta_dve, 2 * d + 2)
                for h in range(GROUP):
                    mm(psq[0][:, 4 + h], invT[:, 4 + h], vbeta[:, 4 + h], start=True, stop=False)
                    last = mm(psq[0][:, 4 + h], nwT[:, h], state[:, h], start=False, stop=True)
                last.then_inc(delta_out, 1)

            def outputs(d):
                pe.wait_ge(delta_act, 3 * d + 2)
                pe.wait_ge(qdec_done, d + 1)
                for h in range(GROUP):
                    mm(psv[1][:, h, 0:P], vnew[:, h], qkT[:, h], start=True, stop=True)
                    mm(psv[1][:, h, P:SEQ], vnew[:, 4 + h], qkT[:, 4 + h], start=True, stop=False)
                    last = mm(psv[1][:, h, P:SEQ], state[:, h], qdec[:, h], start=False, stop=True)
                last.then_inc(delta_out, 1)

            def out_lengths(d):
                pe.wait_ge(delta_act, 3 * d + 3)
                for b in range(2):
                    last = mm(ps[0][:, b], ones[:], piece(qn, b).rearrange("p h n -> p (h n)"), start=True, stop=True)
                last.then_inc(o_len, 1)

            def stages(d, n0):
                all_ = {1: q_lengths, 2: gram_m, 5: transposes, 7: gram_q, 15: merge32_a, 16: merge32_b, 17: merge64_a,
                        18: merge64_b, 19: first_tile, 20: carry, 21: second_tile, 22: outputs, 23: out_lengths}

                def step(f):
                    return lambda: f(d)
                return {n - n0: step(f) for n, f in all_.items() if n0 <= n < n0 + HID}

            def group(g, d):
                start_group(d)
                gemm("qkv", g, 0, HID, 0, 0, ahi, alo, after=stages(d, 0))
                gemm("qkv", g, HID, HID, 1, 0, ahi, alo, after=stages(d, HID))
                gemm("qkv", g, 2 * HID, HID, 0, 1, ahi, alo, after=stages(d, 2 * HID))

            with pe.Fori(1, NGROUPS) as g:
                group(g, g - 1)

            def spatial():
                pe.wait_ge(v_normed, TILES)
                pe.wait_ge(gm_masked, 1)
                pe.wait_ge(ps_free, NGROUPS + 1)
                for x in range(GMT):
                    for m in range(TILES):
                        last = mm(psv[x // 4][:, x % 4, m * P:(m + 1) * P], vg[:, m, x * P:(x + 1) * P], gmw[:, x], start=True, stop=True)
                last.then_inc(sv_out, 1)

            d = NGROUPS - 1
            start_group(d)
            gemm("uv", 0, 0, HID, 0, 0, ahi, alo, rows=True, after=stages(d, 0))
            gemm("uv", 0, HID, HID, 1, 0, ahi, alo, rows=True, after=stages(d, HID))
            gemm("uv", 0, 2 * HID, HID, 0, 1, ahi, alo, after=stages(d, 2 * HID))
            gemm("uv", 0, 3 * HID, HID, 1, 1, ahi, alo, after={4: spatial})

            with pe.Fori(0, 2) as i:
                for b in range(2):
                    gemm("z", i, b * HID, HID, b, 0, ahi, alo)
            with pe.Fori(0, NB) as i:
                gemm("mix", i, 0, HID, 0, 0, ahi, alo)
                gemm("mix", i, HID, HID, 1, 0, ahi, alo)
                pe.wait_ge(ya_lo, 2)
                gemm("mix", i, 2 * HID, HGM, 0, 1, yahi, yalo)
                pe.wait_ge(yb_lo, 8)
                gemm("mix", i, 2 * HID + HGM, HID, 1, 1, ybhi, yblo)

            def operand_ready(done, last):
                return lambda: pe.wait_ge(done, last)

            pe.wait_ge(mix_lo, 6)
            gemm("out", 0, 0, HID, 0, 0, mhi, mlo, after={5: operand_ready(mix_lo, 8)})
            gemm("out", 0, HID, HID, 1, 0, mhi, mlo)
            with pe.Fori(1, 2) as i:
                for b in range(2):
                    gemm("out", i, b * HID, HID, b, 0, mhi, mlo)

            def next_sum(n):
                def f():
                    pe.wait_ge(res[n]["added"], 9)
                    sum_squares(n + 1)
                return f

            pe.wait_ge(res[0]["lo"], 6)
            gemm("ffn", 0, 0, HID, 0, 0, ahi, alo, after={1: next_sum(0), 5: operand_ready(res[0]["lo"], 8)})
            gemm("ffn", 0, HID, HID, 1, 0, ahi, alo)
            with pe.Fori(1, FB) as i:
                for b in range(2):
                    gemm("ffn", i, b * HID, HID, b, 0, ahi, alo)
            pe.wait_ge(ff_lo, 2 * FB - 2)
            gemm("down", 0, 0, HFF, 0, 0, fhi, flo, after={HFF - 3: operand_ready(ff_lo, 2 * FB)})
            gemm("down", 0, HFF, HFF, 1, 0, fhi, flo)
            with pe.Fori(1, 2) as i:
                for b in range(2):
                    gemm("down", i, b * HFF, HFF, b, 0, fhi, flo)
            pe.wait_ge(p_lo, 1)
            for b in range(NB):
                gemm("proj", 0, b, 1, b % 2, b // 2, phi, plo, after={0: next_sum(1)} if b == 1 else None)
            pe.wait_ge(res[1]["lo"], 8)
            for i in range(2):
                for b in range(2):
                    gemm("ple", i, b * HID, HID, b, 0, ahi, alo)
            pe.wait_ge(sq_added, 12)
            sum_squares(3)

        @block.scalar
        def _(act):
            f = nc.scalar.activation

            def split(phase, i, a, b):
                for n in range(a, b):
                    split_hi(act, phase, i, n)

            def root(n):
                act.wait_ge(mean_inv, 2 * n + 2)
                f(R[:], Rt[:], ACT.Sqrt).then_inc(r_done, 1)

            for n in range(-LEAD, 0):
                split_hi(act, "qkv", 0, n)
                c = n + LEAD
                act.wait_ge(x_in[c], 16)
                if c:
                    act.wait_ge(sq_added, c)
                f(t[1][:], xT[:, 4 * c:4 * c + 4], ACT.Square).then_inc(x0_sq, 1)
                act.wait_ge(x0_gain, c + 1)
                f(ahi[:, 4 * c:4 * c + 4], t[2 * (c % 2)][:], ACT.Copy).then_inc(x0_hi, 1)
            act.wait_ge(x_in[3], 16)
            act.wait_ge(sq_added, 3)
            f(t[1][:], xT[:, 12:16], ACT.Square).then_inc(x0_sq, 1)
            act.wait_ge(x0_gain, 4)
            f(ahi[:, 12:16], t[2][:], ACT.Copy).then_inc(x0_hi, 1)

            def silu_qk(c, g):
                act.wait_ge(conv_done, 8 * g + 4 * (c + 1))
                f(conv[c][:], conv[c][:], ACT.Silu).then_inc(conv_silu, 1)
                act.wait_ge(conv_silu, 2 * g + c + 1)
                f(t[c][:], conv[c][:], ACT.Square).then_inc(qk_sq, 1)

            def k_root(d):
                act.wait_ge(qk_inv, 2 * d + 1)
                f(t[1][:], t[1][:], ACT.Sqrt).then_inc(qk_root, 1)

            def q_root(d):
                act.wait_ge(qk_inv, 2 * d + 2)
                f(t[0][:], t[0][:], ACT.Sqrt).then_inc(qk_root, 1)

            def g_exp(d):
                act.wait_ge(g_out, d + 1)
                f(vnew[:, 4:8], psv[1][:, :, P:SEQ], ACT.Exp).then_inc(decay_done, 1)

            def decay_m(d):
                act.wait_ge(diff_done, 2 * d + 1)
                f(negm[:], negm[:], ACT.Exp, scale=-1.0).then_inc(decay_done, 1)

            def decay_q(d):
                act.wait_ge(diff_done, 2 * d + 2)
                f(qkT[:], qkT[:], ACT.Exp).then_inc(decay_done, 1)

            def silu_v(d):
                act.wait_ge(convv_done, d + 1)
                f(conv[2][:], conv[2][:], ACT.Silu).then_inc(convv_silu, 1)

            def copy_p32(d):
                act.wait_ge(merge_out, 4 * d + 1)
                for a, top in enumerate((0, 64)):
                    f(p32[top:top + 32], heads(ps[0][top:top + 32, a, 0:256], 32), ACT.Copy).then_inc(merge_act, 1)

            def copy_inv(d):
                act.wait_ge(merge_out, 4 * d + 2)
                f(inv[32:64, :, 0:32], heads(ps[1][32:64, 0, 256:512], 32), ACT.Copy).then_inc(merge_act, 1)

            def copy_v0(d):
                act.wait_ge(delta_out, 5 * d + 1)
                f(vnew[:, 0:4], psq[1][:, 0:4], ACT.Copy).then_inc(delta_act, 1)

            def copy_v1(d):
                act.wait_ge(delta_out, 5 * d + 4)
                f(vnew[:, 4:8], psq[0][:, 4:8], ACT.Copy).then_inc(delta_act, 1)

            def square_o(d):
                act.wait_ge(delta_out, 5 * d + 5)
                f(qn[:], psv[1], ACT.Square).then_inc(delta_act, 1)

            def o_rt(d):
                act.wait_ge(o_mean, 2 * d + 2)
                f(kn[:], kn[:], ACT.Sqrt).then_inc(o_root, 1)

            STAGES = {0: (g_exp, k_root), 2: (decay_m,), 3: (decay_q,), 4: (q_root, silu_v), 16: (copy_p32,),
                      17: (copy_inv,), 20: (copy_v0,), 22: (copy_v1,), 23: (square_o, o_rt)}

            def beta_g():
                act.wait_ge(ba_dve, 1)
                f(bg[0:16, :], g1[0:16, :], ACT.Sigmoid).then_inc(ba_act, 1)
                f(hv[32:48, 2:3], hv[32:48, 1:2], ACT.Exp).then_inc(ba_act, 1)
                act.wait_ge(ba_dve, 3)
                f(g2[32:48, :], g2[32:48, :], ACT.Exp, scale=-1.0).then_inc(ba_act, 1)
                act.wait_ge(ba_act, 3)
                f(g2[32:48, :], g2[32:48, :], ACT.Ln, bias=1.0).then_inc(ba_act, 1)

            def tails():
                act.wait_ge(ba_dve, 7)
                f(bg[64:80, 0:P], bg[32:48, 0:P], ACT.Exp, bias=bg[32:48, P - 1:P], scale=-1.0).then_inc(ba_act, 1)

            def tok_exp():
                act.wait_ge(tok_done, 2)
                f(tok[:, 3], tok[:, 1], ACT.Exp).then_inc(tok_eg, 1)

            for n in range(3 * HID):
                split_hi(act, "qkv", 0, n)
                if n == 2:
                    root(0)
                if n == 6:
                    beta_g()
                if n == 7:
                    tails()
                if n == 14:
                    tok_exp()
                if n in (11, 19):
                    silu_qk(n // 8 - 1, 0)
            with act.Fori(1, NGROUPS) as g:
                for n in range(3 * HID):
                    split_hi(act, "qkv", g, n)
                    for stage in STAGES.get(n, ()):
                        stage(g - 1)
                    if n in (11, 19):
                        silu_qk(n // 8 - 1, g)

            def v_block(b):
                acc_full(act, "uv", 0, HID * (b + 1))
                if b == 0:
                    act.wait_ge(qk_normed, 2 * NGROUPS)
                for m in range(TILES):
                    x = f(vg[:, m, COLS * b:COLS * (b + 1)], acc[b][:, m], ACT.Gelu, scale=rcol[:, m:m + 1])
                    x.then_inc(v_gelu, 1)
                    if m == TILES - 1:
                        act.wait_ge(v_gelu, 4 * b + 3)
                        act.sem_inc(acc_read[b], 1)
                    else:
                        act.wait_ge(v_gelu, 4 * b + 2 * m + 1)
                    f(t[2][:, 0:2].rearrange("p a n -> p (a n)"), vg[:, m, COLS * b:COLS * (b + 1)], ACT.Square,
                      accum_out=vsum[:, b, m:m + 1]).then_inc(v_gelu, 1)
                    act.wait_ge(v_gelu, 4 * b + 2 * m + 2)

            def u_block(b):
                act.wait_ge(ps_free, NGROUPS + 1)
                for j in range(2):
                    act.wait_ge(u_scaled, 2 * b + j + 1)
                    f(uT[:, 4 * b + 2 * j:4 * b + 2 * j + 2], piece(t[0], j), ACT.Gelu).then_inc(u_gelu, 1)

            for n in range(4 * HID):
                split_hi(act, "uv", 0, n)
                for stage in STAGES.get(n, ()):
                    stage(NGROUPS - 1)
                if n in (7, 15):
                    v_block(n // 8)
                if n == 18:
                    act.wait_ge(v_mean, 3)
                    f(vrms[:], vrms[:], ACT.Sqrt).then_inc(v_root, 1)
                if n in (23, 31):
                    u_block(n // 8 - 2)
            for j in range(2):
                act.wait_ge(ya_dve, j + 1)
                f(yahi[:, 4 * j:4 * j + 4], ytmp[:, 4 * j:4 * j + 4], ACT.Copy).then_inc(ya_hi, 1)
            act.wait_ge(p_in, 16)
            f(phi[:], praw[:], ACT.Copy).then_inc(p_hi, 1)

            with act.Fori(0, 2) as i:
                for b in range(2):
                    split(("z"), i, b * HID, (b + 1) * HID)
                    for j in range(2):
                        act.wait_ge(z_scaled, 4 * i + 2 * b + j + 1)
                        f(piece(t[0], j), piece(t[0], j), ACT.Silu).then_inc(z_silu, 1)
                    for j in range(2):
                        act.wait_ge(z_gated, 4 * i + 2 * b + j + 1)
                        f(tiles(ybhi, 2 * i + b, j), piece(t[1], j), ACT.Copy).then_inc(yb_hi, 1)
            with act.Fori(0, NB) as i:
                for b in range(2):
                    split("mix", i, b * HID, (b + 1) * HID)
                    for j in range(2):
                        act.wait_ge(gate_scaled, 4 * i + 2 * b + j + 1)
                        f(piece(t[b], j), piece(t[b], j), ACT.Sigmoid).then_inc(gate_sig, 1)
                split("mix", i, 2 * HID, PER["mix"])
                for j in range(2):
                    act.wait_ge(mix_prod, 6 * i + 5 + j)
                    f(tiles(mhi, i, j), piece(t[2], j), ACT.Copy).then_inc(mix_hi, 1)

            def residual(n, phase, halves):
                s = res[n]
                with act.Fori(0, 2) as i:
                    for b in range(2):
                        split(phase, i, b * halves, (b + 1) * halves)
                        for j in range(2):
                            q = 4 * i + 2 * b + j
                            act.wait_ge(s["x"], q + 1)
                            act.wait_ge(s["added"], 1 + 4 * i + (0, 0, 1, 2)[2 * b + j])
                            f(piece(t[1], j), tiles(xT, 2 * i + b, j), ACT.Square).then_inc(s["sq"], 1)
                        for j in range(2):
                            act.wait_ge(s["gain"], 4 * i + 2 * b + j + 1)
                            f(tiles(ahi, 2 * i + b, j), piece(t[0], j), ACT.Copy).then_inc(s["hi"], 1)

            residual(0, "out", HID)
            root(1)
            with act.Fori(0, FB) as i:
                split("ffn", i, 0, HID)
                for j in range(2):
                    act.wait_ge(ff_scaled, 2 * i + j + 1)
                    f(piece(t[0], j), piece(t[0], j), ACT.Silu).then_inc(ff_silu, 1)
                split("ffn", i, HID, 2 * HID)
                for j in range(2):
                    act.wait_ge(ff_prod, 2 * i + j + 1)
                    f(tiles(fhi, i, j), piece(t[2], j), ACT.Copy).then_inc(ff_hi, 1)
            residual(1, "down", HFF)
            split("proj", 0, 0, NB)
            root(2)
            for i in range(2):
                for b in range(2):
                    split("ple", i, b * HID, (b + 1) * HID)
                    for j in range(2):
                        act.wait_ge(ple_scaled, 4 * i + 2 * b + j + 1)
                        f(piece(t[0], j), piece(t[0], j), ACT.Sigmoid).then_inc(ple_sig, 1)
                    for j in range(2):
                        q = 4 * i + 2 * b + j
                        act.wait_ge(ple_x, q + 1)
                        if q >= 2:
                            act.wait_ge(sq_added, 4 + q - 1)
                        f(piece(t[1], j), tiles(xT, 2 * i + b, j), ACT.Square).then_inc(ple_sq, 1)
            root(3)

        @block.vector
        def _(dve):
            v = nc.vector

            def split(phase, i, a, b):
                for n in range(a, b):
                    split_lo(dve, phase, i, n)

            def mean(n):
                dve.wait_ge(sq_summed, n + 1)
                v.tensor_scalar(Rt[:], psf[0][:, 0:SEQ], 1.0 / D, EPS, ALU.mult, ALU.add).then_inc(mean_inv, 1)
                dve.wait_ge(mean_inv, 2 * n + 1)
                v.reciprocal(Rt[:], Rt[:]).then_inc(mean_inv, 1)

            def x_gain(c):
                dve.wait_ge(x_in[c], 16)
                if c >= 2:
                    dve.wait_ge(x0_lo, c - 1)
                v.tensor_tensor(t[2 * (c % 2)][:], xT[:, 4 * c:4 * c + 4], bc(cols[:, C_MIX + 4 * c:C_MIX + 4 * c + 4], SEQ),
                                ALU.mult).then_inc(x0_gain, 1)

            def x_lo(c):
                dve.wait_ge(x0_hi, c + 1)
                v.tensor_tensor(alo[:, 4 * c:4 * c + 4], t[2 * (c % 2)][:], ahi[:, 4 * c:4 * c + 4].bitcast(F32),
                                ALU.subtract).then_inc(x0_lo, 1)

            dve.wait_ge(cols_in, 16)
            for n in range(-LEAD, 0):
                c = n + LEAD
                x_gain(c)
                split_lo(dve, "qkv", 0, n)
                x_lo(c)
            x_gain(3)
            x_lo(3)

            def evac_qkv(c, g):
                acc_full(dve, "qkv", g, (c + 1) * HID)
                if c == 0:
                    if not (isinstance(g, int) and g == 0):
                        dve.wait_ge(convv_done, g)
                else:
                    dve.wait_ge(conv_done, 8 * g + 4 * c)
                buf = c % 2
                v.tensor_tensor(pre[:, :, 4:], accv[buf], over(R[:], 4), ALU.mult).then_inc(pre_done, 1)
                dve.wait_ge(pre_done, 3 * g + c + 1)
                dve.sem_inc(acc_read[buf], 1)

            def convolve(c, g, h):
                y = conv[c][:, h]
                for tap in range(4):
                    w = cols[:, ds(C_CONV + tap * 48 + c * HEADS + GROUP * g + h, 1)]
                    src = pre[:, h, 1 + tap:1 + tap + SEQ]
                    if tap == 0:
                        ins = v.tensor_scalar(y, src, w, None, ALU.mult)
                    else:
                        ins = v.scalar_tensor_tensor(y, src, w, y, ALU.mult, ALU.add)
                    if tap == 3:
                        ins.then_inc(conv_done, 1)
                    else:
                        ins.then_inc(conv_mac, 1)
                        dve.wait_ge(conv_mac, 24 * g + 12 * c + 3 * h + tap + 1)

            def invert_mean(n, src, dst, factor, wait, value, d):
                dve.wait_ge(wait, value)
                v.tensor_scalar(dst, src, EPS, factor, ALU.add, ALU.mult).then_inc(qk_mean, 1)
                dve.wait_ge(qk_mean, 2 * d + n)
                v.reciprocal(dst, dst).then_inc(qk_inv, 1)

            def k_mean(d):
                invert_mean(1, psv[0], t[1][:], 1.0, k_len, d + 1, d)

            def q_mean(d):
                invert_mean(2, psv[1], t[0][:], float(P), q_len, d + 1, d)

            def token(k, m, h, d):
                return tok[:, k, m, ds(GROUP * d + h, 1)]

            def tokens(k, m, d):
                return bc(tok[:, k, m, ds(GROUP * d, GROUP)], P)

            def diff_m(d):
                dve.wait_ge(decay_done, 3 * d + 1)
                for m in range(TILES):
                    for h in range(GROUP):
                        x = v.scalar_tensor_tensor(negm[:, 4 * m + h], psv[1][:, h, m * P:(m + 1) * P], token(1, m, h, d), mask_m[:],
                                                   ALU.subtract, ALU.max)
                x.then_inc(diff_done, 1)

            def diff_q(d):
                for m in range(TILES):
                    for h in range(GROUP):
                        x = v.scalar_tensor_tensor(qkT[:, 4 * m + h], psv[1][:, h, m * P:(m + 1) * P], token(1, m, h, d), mask_q[:],
                                                   ALU.subtract, ALU.min)
                x.then_inc(diff_done, 1)

            def make_negm(d):
                dve.wait_ge(gram_m_out, d + 1)
                dve.wait_ge(decay_done, 3 * d + 2)
                for m in range(TILES):
                    for h in range(GROUP):
                        x = v.scalar_tensor_tensor(negm[:, 4 * m + h], psq[0][:, 4 * m + h], token(4, m, h, d), negm[:, 4 * m + h],
                                                   ALU.mult, ALU.mult)
                x.then_inc(negm_done, 1)

            def scale_kv(d):
                dve.wait_ge(vT_out, d + 1)
                for m in range(TILES):
                    v.tensor_tensor(vbeta[:, 4 * m:4 * m + 4], psq[1][:, 4 * m:4 * m + 4], tokens(0, m, d), ALU.mult).then_inc(kv_scaled, 1)
                dve.wait_ge(kT_out, d + 1)
                v.tensor_tensor(ktail[:], psq[0][:, 0:4], tokens(2, 0, d), ALU.mult).then_inc(kv_scaled, 1)
                v.tensor_tensor(kbeg[:], psq[0][:, 4:8], tokens(3, 1, d), ALU.mult).then_inc(kv_scaled, 1)

            def make_qkT(d):
                dve.wait_ge(gram_q_out, d + 1)
                dve.wait_ge(decay_done, 3 * d + 3)
                v.tensor_tensor(qkT[:], psq[1], qkT[:], ALU.mult).then_inc(qkT_done, 1)

            def copy_invT32(d):
                dve.wait_ge(merge_out, 4 * d + 2)
                for a, (top, low) in enumerate(((0, 32), (64, 96))):
                    v.tensor_copy(invT[top:top + 32, :, low:low + 32], heads(ps[1][top:top + 32, a, 0:256], 32)).then_inc(merge_dve, 1)

            def copy_p64(d):
                dve.wait_ge(merge_out, 4 * d + 3)
                v.tensor_copy(p64[:], heads(ps[0][0:64, 0], 64)).then_inc(merge_dve, 1)

            def copy_invT64(d):
                dve.wait_ge(merge_out, 4 * d + 4)
                v.tensor_copy(invT[0:64, :, 64:128], heads(ps[0][0:64, 1], 64)).then_inc(merge_dve, 1)

            def copy_nwT(d):
                dve.wait_ge(delta_out, 5 * d + 2)
                v.tensor_scalar(nwT[:], psq[1][:, 4:8], -1.0, None, ALU.mult).then_inc(delta_dve, 1)

            def copy_state(d):
                dve.wait_ge(delta_out, 5 * d + 3)
                v.tensor_copy(state[:], psq[0][:, 0:4]).then_inc(delta_dve, 1)

            def norm_o(d):
                dve.wait_ge(o_len, d + 1)
                v.tensor_scalar(kn[:], psv[0], 1.0 / P, EPS, ALU.mult, ALU.add).then_inc(o_mean, 1)
                dve.wait_ge(o_mean, 2 * d + 1)
                v.reciprocal(kn[:], kn[:]).then_inc(o_mean, 1)
                dve.wait_ge(o_root, d + 1)
                v.scalar_tensor_tensor(oT[:, ds(GROUP * d, GROUP)], psv[1], cols[:, C_DNO:C_DNO + 1], kn[:], ALU.mult, ALU.mult).then_inc(ps_free, 1)

            STAGES = {0: (k_mean,), 1: (diff_m,), 2: (diff_q,), 3: (q_mean,), 4: (make_negm,), 6: (scale_kv,), 8: (make_qkT,),
                      17: (copy_invT32,), 18: (copy_p64,), 19: (copy_invT64,), 20: (copy_nwT,), 21: (copy_state,)}

            def select_heads(g):
                v.tensor_copy(selg[32:48, :], ident[32:48, ds(32 + GROUP * g, GROUP)]).then_inc(sel_done, 1)

            def beta_g():
                dve.wait_ge(ba_out, 1)
                v.tensor_tensor(g1[:], psf[1][0:48, 0:SEQ], R[0:48, :], ALU.mult).then_inc(ba_dve, 1)
                dve.wait_ge(ba_dve, 1)
                v.tensor_scalar(g1[32:48, :], g1[32:48, :], hv[32:48, 0:1], None, ALU.add).then_inc(ba_dve, 1)
                dve.wait_ge(ba_dve, 2)
                v.scalar_tensor_tensor(g2[32:48, :], g1[32:48, :], -1.0, g1[32:48, :], ALU.mult, ALU.max).then_inc(ba_dve, 1)
                dve.wait_ge(rcol_out, 1)
                v.tensor_copy(rcol[:], psf[0][:, COLS:COLS + TILES]).then_inc(rcol_done, 1)
                dve.wait_ge(ba_act, 4)
                v.scalar_tensor_tensor(g1[32:48, :], g1[32:48, :], 0.0, g2[32:48, :], ALU.max, ALU.add).then_inc(ba_dve, 1)
                dve.wait_ge(ba_dve, 4)
                v.tensor_scalar(g2[32:48, :], g1[32:48, :], hv[32:48, 2:3], -1.0, ALU.mult, ALU.mult).then_inc(ba_dve, 1)
                dve.wait_ge(ba_dve, 5)
                for m in range(TILES):
                    v.tensor_tensor_scan(bg[32:48, m * P:(m + 1) * P], ones[32:48, :], g2[32:48, m * P:(m + 1) * P], 0.0,
                                         ALU.mult, ALU.add).then_inc(ba_dve, 1)

            def tok_copy():
                dve.wait_ge(tok_T, 1)
                src = psf[0][:, 0:160].rearrange("p (m c) -> p m c", m=TILES)
                for k in (1, 0, 2):
                    v.tensor_copy(tok[:, k], src[:, :, 32 * k:32 * k + 16]).then_inc(tok_done, 1)
                dve.wait_ge(tok_done, 3)
                v.tensor_scalar(tok[:, 4], tok[:, 0], -1.0, None, ALU.mult).then_inc(tok_done, 1)
                dve.wait_ge(tok_eg, 1)
                v.tensor_tensor(tok[:, 3], tok[:, 3], tok[:, 0], ALU.mult).then_inc(tok_done, 1)
                dve.wait_ge(tok_done, 5)
                dve.sem_inc(ps_free, 1)

            def conv_stage(n, g):
                for c in range(2):
                    if n == 8 * c + 7:
                        evac_qkv(c, g)
                    if 8 * c + 9 <= n < 8 * c + 11:
                        for h in (0, 1):
                            convolve(c, g, 2 * (n - 8 * c - 9) + h)
                if n == 20:
                    select_heads(g)

            for n in range(3 * HID):
                split_lo(dve, "qkv", 0, n)
                if n == 2:
                    mean(0)
                if n == 6:
                    beta_g()
                if n == 14:
                    tok_copy()
                conv_stage(n, 0)
            evac_qkv(2, 0)
            with dve.Fori(1, NGROUPS) as g:
                for n in range(3 * HID):
                    split_lo(dve, "qkv", g, n)
                    for stage in STAGES.get(n, ()):
                        stage(g - 1)
                    conv_stage(n, g)
                evac_qkv(2, g)
                norm_o(g - 1)

            def v_norm():
                dve.wait_ge(v_gelu, 8)
                v.tensor_tensor(vrms[:], vsum[:, 0], vsum[:, 1], ALU.add).then_inc(v_mean, 1)
                dve.wait_ge(v_mean, 1)
                v.tensor_scalar(vrms[:], vrms[:], 1.0 / GM, EPS, ALU.mult, ALU.add).then_inc(v_mean, 1)
                dve.wait_ge(v_mean, 2)
                v.reciprocal(vrms[:], vrms[:]).then_inc(v_mean, 1)

            def v_scale():
                dve.wait_ge(v_root, 1)
                for m in range(TILES):
                    v.tensor_scalar(vg[:, m], vg[:, m], vrms[:, m:m + 1], None, ALU.mult).then_inc(v_normed, 1)

            def u_block(b):
                acc_full(dve, "uv", 0, (b + 3) * HID)
                for j in range(2):
                    if b:
                        dve.wait_ge(u_gelu, j + 1)
                    v.tensor_tensor(piece(t[0], j), piece(accv[b], j), over(R[:], 2), ALU.mult).then_inc(u_scaled, 1)
                dve.wait_ge(u_scaled, 2 * b + 2)
                dve.sem_inc(acc_read[b], 1)

            def sv_bias():
                dve.wait_ge(sv_out, 1)
                for x in range(GMT):
                    ins = v.scalar_tensor_tensor(ytmp[:, x].rearrange("p (m t) -> p m t", m=TILES),
                                                 psv[x // 4][:, x % 4].rearrange("p (m t) -> p m t", m=TILES), cols[:, C_GMV + x:C_GMV + x + 1],
                                                 over(gmb[:, x], TILES), ALU.mult, ALU.add)
                ins.then_inc(sv_biased, 1)

            for n in range(4 * HID):
                split_lo(dve, "uv", 0, n)
                for stage in STAGES.get(n, ()):
                    stage(NGROUPS - 1)
                if n == 16:
                    v_norm()
                if n == 19:
                    v_scale()
                if n == 23:
                    u_block(0)
                    norm_o(NGROUPS - 1)
                if n == 29:
                    sv_bias()
            u_block(1)
            dve.wait_ge(sv_biased, 1)
            for j in range(2):
                dve.wait_ge(u_gelu, 2 * j + 2)
                v.tensor_tensor(ytmp[:, 4 * j:4 * j + 4], ytmp[:, 4 * j:4 * j + 4], uT[:, 4 * j:4 * j + 4], ALU.mult).then_inc(ya_dve, 1)
            for j in range(2):
                dve.wait_ge(ya_hi, j + 1)
                v.tensor_tensor(yalo[:, 4 * j:4 * j + 4], ytmp[:, 4 * j:4 * j + 4], yahi[:, 4 * j:4 * j + 4].bitcast(F32), ALU.subtract).then_inc(ya_lo, 1)
            dve.wait_ge(p_hi, 1)
            v.tensor_tensor(plo[:], praw[:], phi[:].bitcast(F32), ALU.subtract).then_inc(p_lo, 1)

            def times_row(phase, i, end, buf, dst, signal, value):
                acc_full(dve, phase, i, end)
                for j in range(2):
                    x = v.tensor_tensor(piece(dst, j), piece(accv[buf], j), over(R[:], 2), ALU.mult)
                    x.then_inc(signal, 1)
                dve.wait_ge(signal, value + 2)
                dve.sem_inc(acc_read[buf], 1)

            def take_lo(hi, lo, src, blk, done, signal, value):
                for j in range(2):
                    dve.wait_ge(done, value + j + 1)
                    v.tensor_tensor(tiles(lo, blk, j), piece(src, j), tiles(hi, blk, j).bitcast(F32), ALU.subtract).then_inc(signal, 1)

            with dve.Fori(0, 2) as i:
                for b in range(2):
                    split("z", i, b * HID, (b + 1) * HID)
                    times_row("z", i, (b + 1) * HID, b, t[0], z_scaled, 4 * i + 2 * b)
                    for j in range(2):
                        dve.wait_ge(z_silu, 4 * i + 2 * b + j + 1)
                        v.tensor_tensor(piece(t[1], j), tiles(oT, 2 * i + b, j), piece(t[0], j), ALU.mult).then_inc(z_gated, 1)
                    take_lo(ybhi, yblo, t[1], 2 * i + b, yb_hi, yb_lo, 4 * i + 2 * b)
            with dve.Fori(0, NB) as i:
                for b in range(2):
                    split("mix", i, b * HID, (b + 1) * HID)
                    times_row("mix", i, (b + 1) * HID, b, t[b], gate_scaled, 4 * i + 2 * b)
                split("mix", i, 2 * HID, 2 * HID + HGM)
                for b in range(2):
                    if b:
                        split("mix", i, 2 * HID + HGM, PER["mix"])
                    acc_full(dve, "mix", i, 2 * HID + HGM + b * HID)
                    for j in range(2):
                        dve.wait_ge(gate_sig, 4 * i + 2 * b + j + 1)
                        v.tensor_tensor(piece(t[b], j), piece(accv[b], j), piece(t[b], j), ALU.mult).then_inc(mix_prod, 1)
                    dve.wait_ge(mix_prod, 6 * i + 2 * b + 2)
                    dve.sem_inc(acc_read[b], 1)
                for j in range(2):
                    v.tensor_tensor(piece(t[2], j), piece(t[0], j), piece(t[1], j), ALU.add).then_inc(mix_prod, 1)
                take_lo(mhi, mlo, t[2], i, mix_hi, mix_lo, 2 * i)

            def residual(n, phase, halves):
                s = res[n]
                with dve.Fori(0, 2) as i:
                    for b in range(2):
                        split(phase, i, b * halves, (b + 1) * halves)
                        acc_full(dve, phase, i, (b + 1) * halves)
                        q = 4 * i + 2 * b
                        for j in range(2):
                            v.tensor_tensor(tiles(xT, 2 * i + b, j), piece(accv[b], j), tiles(xT, 2 * i + b, j), ALU.add).then_inc(s["x"], 1)
                        dve.wait_ge(s["x"], q + 2)
                        dve.sem_inc(acc_read[b], 1)
                        take_lo(ahi, alo, t[0], 2 * i + b, s["hi"], s["lo"], q)

            residual(0, "out", HID)
            mean(1)
            dve.wait_ge(r_done, 2)
            with dve.Fori(0, FB) as i:
                split("ffn", i, 0, HID)
                times_row("ffn", i, HID, 0, t[0], ff_scaled, 2 * i)
                split("ffn", i, HID, 2 * HID)
                acc_full(dve, "ffn", i, 2 * HID)
                for j in range(2):
                    dve.wait_ge(ff_gate, 2 * i + j + 1)
                    v.tensor_tensor(piece(t[2], j), piece(accv[1], j), piece(t[1], j), ALU.mult).then_inc(ff_prod, 1)
                dve.wait_ge(ff_prod, 2 * i + 2)
                dve.sem_inc(acc_read[1], 1)
                take_lo(fhi, flo, t[2], i, ff_hi, ff_lo, 2 * i)
            residual(1, "down", HFF)
            for b in range(NB):
                split("proj", 0, b, b + 1)
                acc_full(dve, "proj", 0, b + 1)
                v.tensor_copy(pw[:, 4 * b:4 * b + 4], accv[b % 2]).then_inc(pw_done, 1)
                dve.wait_ge(pw_done, b + 1)
                dve.sem_inc(acc_read[b % 2], 1)
                if b == 1:
                    mean(2)
            dve.wait_ge(r_done, 3)
            for i in range(2):
                for b in range(2):
                    split("ple", i, b * HID, (b + 1) * HID)
                    times_row("ple", i, (b + 1) * HID, b, t[0], ple_scaled, 4 * i + 2 * b)
                    for j in range(2):
                        dve.wait_ge(ple_prod, 4 * i + 2 * b + j + 1)
                        v.tensor_tensor(tiles(xT, 2 * i + b, j), tiles(xT, 2 * i + b, j), piece(t[0], j), ALU.add).then_inc(ple_x, 1)
            mean(3)
            dve.wait_ge(r_done, 4)
            dve.wait_ge(ple_gain, 8)
            for c in range(3):
                v.tensor_tensor(xT[:, 4 * c:4 * c + 4], xT[:, 4 * c:4 * c + 4], over(R[:], 4), ALU.mult).then_inc(out_dve, 1)


def halves(w):
    k, n = w.shape
    x = w.reshape(k // (HALF_K * P), HALF_K, P, n // COLS, COLS).transpose(3, 0, 2, 1, 4)
    return np.ascontiguousarray(x.reshape(-1, HALF_K * COLS))


def features(a, n):
    return np.ascontiguousarray(a.reshape(SEQ, n, P).transpose(2, 1, 0))


def kernel(**inputs):
    from concourse import bacc
    from concourse.bass_utils import run_bass_kernel_spmd

    a = {k: np.asarray(v) for k, v in inputs.items()}
    w_in = a["w_in"][0]
    ba0 = 2 * GM + 4 * D
    wba = np.zeros((D, 48), np.float32)
    wba[:, 0:16] = w_in[:, ba0:ba0 + HEADS]
    wba[:, 32:48] = w_in[:, ba0 + HEADS:ba0 + 2 * HEADS]

    def per_feature(x):
        return x.reshape(-1, P).T

    conv_w = a["dn_conv_w"][0]
    arrays = {
        "win": halves(np.concatenate([w_in[:, :ba0], w_in[:, ba0 + 2 * HEADS:]], axis=1)),
        "wba": np.ascontiguousarray(wba.reshape(KD, P, 48).transpose(1, 0, 2)),
        "wa": halves(a["w_branch_a"][0]), "wb": halves(a["w_branch_b"][0]), "wo": halves(a["w_out"][0]),
        "wgu": halves(a["w_gate_up"][0]), "wd": halves(a["w_down"][0]), "wpg": halves(a["w_ple_gate"][0]),
        "wpp": halves(a["w_ple_proj"][0]),
        "xT": features(a["x"][0], KD), "pT": features(a["p"][0, 0], PLE // P),
        "cols": np.ascontiguousarray(np.concatenate([
            per_feature(a["norm_mix"][0]), per_feature(a["norm_ffn"][0]), per_feature(a["ple_norm"][0]),
            per_feature(a["norm_final"]), per_feature(a["gm_v_norm"][0]), per_feature(a["dn_out_norm"][0])]
            + [per_feature(conv_w[t]) for t in range(4)], axis=1)),
        "hv": np.ascontiguousarray(np.stack([a["dn_dt_bias"][0], a["dn_a_log"][0]], axis=1)),
        "gmw": np.ascontiguousarray(a["gm_w_s"][0].transpose(2, 0, 1)),
        "gmb": np.ascontiguousarray(a["gm_b_s"][0].reshape(1, GM)),
    }
    nc = bacc.Bacc("TRN2", target_bir_lowering=False, num_devices=1)
    args = [nc.dram_tensor(f"in_{k}", x.shape, mybir.dt.from_np(x.dtype), kind="ExternalInput").ap() for k, x in arrays.items()]
    out = nc.dram_tensor("out_T", (P, KD, SEQ), F32, kind="ExternalOutput").ap()
    build(nc, *args, out)
    r = run_bass_kernel_spmd(nc, [{f"in_{k}": x for k, x in arrays.items()}], core_ids=[0])
    got = np.asarray(r.results[0]["out_T"])
    return np.ascontiguousarray(got.transpose(2, 1, 0)).reshape(1, SEQ, D)
```

```python
import numpy as np

import concourse.bass as bass
from concourse import mybir

F32 = mybir.dt.float32
F32R = mybir.dt.float32r
ACT = mybir.ActivationFunctionType
ALU = mybir.AluOpType
ds = bass.ds

P = 128
SEQ = 256
D = 2048
TILES = SEQ // P
KD = D // P
HEADS = 16
GROUP = 4
NGROUPS = HEADS // GROUP
GM = 1024
GMT = GM // P
FF = 5632
KF = FF // P
PLE = 256
COLS = 512
HALF_K = 2
RING = 4
LEAD = 3
EPS = 1e-6
BIG = 1e30
HID = D // P // HALF_K
HGM = GM // P // HALF_K
HFF = KF // HALF_K
NB = D // COLS
FB = FF // COLS

BLK_U, BLK_V, BLK_Q, BLK_K, BLK_DV, BLK_Z, BLK_GA, BLK_GB = 0, 2, 4, 8, 12, 16, 20, 24

C_MIX, C_FFN, C_PLE, C_FIN, C_GMV, C_DNO, C_CONV = 0, 16, 32, 48, 64, 72, 73
NCOL = C_CONV + 4 * 48

PLAN = [("qkv", 4, 3 * HID, (2, 1)), ("uv", 1, 4 * HID, (2, 2)), ("z", 2, 2 * HID, (1, 1)),
        ("mix", NB, 3 * HID + HGM, (2, 2)), ("out", 2, 2 * HID, (1, 1)), ("ffn", FB, 2 * HID, (1, 1)),
        ("down", 2, 2 * HFF, (1, 1)), ("proj", 1, 4, (2, 2)), ("ple", 2, 2 * HID, (1, 1))]
H0, PER, U0 = {}, {}, {}
_h, _u = 0, [0, 0]
for _name, _n, _per, _uses in PLAN:
    H0[_name], PER[_name], U0[_name] = _h, _per, (tuple(_u), _uses)
    _h += _n * _per
    _u = [_u[0] + _n * _uses[0], _u[1] + _n * _uses[1]]
TOTAL = _h


def half_of(phase, i, n):
    return H0[phase] + PER[phase] * i + n


def use_of(phase, i, buf, n):
    base, per = U0[phase]
    return base[buf] + per[buf] * i + n


def build(nc, win, wba, wa, wb, wo, wgu, wd, wpg, wpp, xT_d, pT_d, cols_d, hv_d, gmw_d, gmb_d, out_d):
    scratch_m = nc.dram_tensor("inv_in", (4, 8, 32, 32), F32, kind="Internal").ap()
    scratch_x = nc.dram_tensor("inv_out", (2, 4, 8, 32, 32), F32, kind="Internal").ap()

    cursor = [(nc.sbuf_base + 63) // 64 * 64]

    def at(name, shape, dt, offset=None):
        size = int(np.prod(shape[1:])) * 4
        if offset is None:
            offset = cursor[0]
            cursor[0] += (size + 31) // 32 * 32
        return nc.alloc_sbuf_tensor_at(name, shape, dt, offset=offset)

    def sem(name):
        return nc.alloc_semaphore(name)

    raw = at("raw", [P, RING, HALF_K, COLS], F32)
    whi = at("whi", [P, RING, HALF_K, COLS], F32R)
    wlo = at("wlo", [P, RING, HALF_K, COLS], F32R)
    xT = at("xT", [P, KD, SEQ], F32)
    ahi = at("ahi", [P, KD, SEQ], F32R)
    alo = at("alo", [P, KD, SEQ], F32R)
    region = cursor[0]
    cursor[0] += 2 * KF * SEQ * 4

    def shared(name, shape, dt, kib):
        return at(name, shape, dt, offset=region + int(kib * 1024))

    oT = shared("oT", [P, HEADS, SEQ], F32, 0)
    conv = [shared(f"conv_{c}", [P, GROUP, SEQ], F32, 16 + 4 * n) for n, c in enumerate("qkv")]
    qn = shared("qn", [P, GROUP, SEQ], F32, 28)
    kn = shared("kn", [P, GROUP, SEQ], F32, 32)
    vbeta = shared("vbeta", [P, 8, P], F32, 36)
    kbeg = shared("kbeg", [P, GROUP, P], F32, 40)
    ktail = shared("ktail", [P, GROUP, P], F32, 42)
    qdec = shared("qdec", [P, GROUP, P], F32, 44)
    negm = shared("negm", [P, 8, P], F32, 46)
    qkT = shared("qkT", [P, 8, P], F32, 50)
    inv = shared("inv", [P, 8, P], F32, 54)
    invT = shared("invT", [P, 8, P], F32, 58)
    blk_m = shared("blk_m", [32, 32, 32], F32, 62)
    blk_x = shared("blk_x", [32, 32, 32], F32, 66)
    blk_t = shared("blk_t", [32, 32, 32], F32, 70)
    vnew = shared("vnew", [P, 8, P], F32, 74)
    p32 = shared("p32", [P, 8, 32], F32, 78)
    p64 = shared("p64", [64, 8, 64], F32, 79)
    nwT = shared("nwT", [P, GROUP, P], F32, 81)
    state = shared("state", [P, GROUP, P], F32, 83)
    vg = shared("vg", [P, TILES, GM], F32, 16)
    uT = shared("uT", [P, GMT, SEQ], F32, 28)
    gmw = shared("gmw", [P, GMT, P], F32, 62)
    gmb = shared("gmb", [P, GMT, P], F32, 66)
    ytmp = shared("ytmp", [P, GMT, SEQ], F32, 16)
    wba_sb = shared("wba_sb", [P, KD, 48], F32, 62)
    g1 = shared("g1", [48, SEQ], F32, 66)
    g2 = shared("g2", [48, SEQ], F32, 67)
    praw = shared("praw", [P, PLE // P, SEQ], F32, 70)
    mask_m = shared("mask_m", [P, P], F32, 85)
    mask_q = shared("mask_q", [P, P], F32, 85.5)
    bg = shared("bg", [80, SEQ], F32, 86)
    ident = shared("ident", [P, P], F32, 87)
    yahi = shared("yahi", [P, GMT, SEQ], F32R, 72)
    yalo = shared("yalo", [P, GMT, SEQ], F32R, 80)
    ybhi = shared("ybhi", [P, KD, SEQ], F32R, 40)
    yblo = shared("yblo", [P, KD, SEQ], F32R, 56)
    mhi = shared("mhi", [P, KD, SEQ], F32R, 0)
    mlo = shared("mlo", [P, KD, SEQ], F32R, 16)
    fhi = shared("fhi", [P, KF, SEQ], F32R, 0)
    flo = shared("flo", [P, KF, SEQ], F32R, 44)
    pw = shared("pw", [P, KD, SEQ], F32, 0)

    cols = at("cols", [P, NCOL], F32)
    ones = at("ones", [P, P], F32)
    R = at("R", [P, SEQ], F32)
    Rt = at("Rt", [P, SEQ], F32)
    hv = at("hv", [48, 3], F32)
    tok = at("tok", [P, 5, TILES, HEADS], F32)
    selg = at("selg", [48, GROUP], F32)
    length = at("length", [P, 3, 8], F32)
    rcol = at("rcol", [P, TILES], F32)
    vsum = at("vsum", [P, 2, TILES], F32)
    vrms = at("vrms", [P, TILES], F32)
    sqsum = at("sqsum", [P, 2, SEQ], F32)
    t = [at(f"t{n}", [P, GROUP, SEQ], F32) for n in range(3)]
    pre_at = cursor[0]
    pre = at("pre", [P, GROUP, SEQ + 4], F32)
    phi = at("phi", [P, PLE // P, SEQ], F32R, offset=pre_at)
    plo = at("plo", [P, PLE // P, SEQ], F32R, offset=pre_at + 2048)

    acc = [nc.alloc_psum_tensor(f"acc{n}", [P, 2, COLS], F32) for n in range(2)]
    ps = [nc.alloc_psum_tensor(f"ps{n}", [P, 2, COLS], F32) for n in range(2)]
    psf = [x[:].rearrange("p a n -> p (a n)") for x in ps]

    def heads(flat, width):
        return flat.rearrange("p (h n) -> p h n", n=width)

    accv = [heads(a[:].rearrange("p a n -> p (a n)"), SEQ) for a in acc]
    psv = [heads(x, SEQ) for x in psf]
    psq = [heads(x, P) for x in psf]

    raw_in = [sem(f"raw_in{n}") for n in range(RING)]
    hi_done, lo_done, half_used = sem("hi_done"), sem("lo_done"), sem("half_used")
    acc_read = [sem(f"acc_read{n}") for n in range(2)]
    cols_in, x_in, ba_in, gm_in = sem("cols_in"), [sem(f"x_in{n}") for n in range(4)], sem("ba_in"), sem("gm_in")
    pool_step, waits_carried = sem("pool_step"), sem("waits_carried")
    consts_made, wba_scaled = sem("consts_made"), sem("wba_scaled")
    sq_added, sq_summed, mean_inv, r_done = sem("sq_added"), sem("sq_summed"), sem("mean_inv"), sem("r_done")
    x0_gain, x0_sq, x0_hi, x0_lo = sem("x0_gain"), sem("x0_sq"), sem("x0_hi"), sem("x0_lo")
    ba_out, rcol_out, rcol_done = sem("ba_out"), sem("rcol_out"), sem("rcol_done")
    ba_dve, ba_act, tok_T, tok_done = sem("ba_dve"), sem("ba_act"), sem("tok_T"), sem("tok_done")
    tok_eg = sem("tok_eg")
    pre_done, conv_mac, conv_done, conv_silu = sem("pre_done"), sem("conv_mac"), sem("conv_done"), sem("conv_silu")
    convv_silu = sem("convv_silu")
    qk_sq, sel_done, g_out = sem("qk_sq"), sem("sel_done"), sem("g_out")
    qk_len, qk_mean, qk_inv, qk_root, qk_diag, qk_rows = (sem("qk_len"), sem("qk_mean"), sem("qk_inv"), sem("qk_root"),
                                                          sem("qk_diag"), sem("qk_rows"))
    qk_normed, diff_done, decay_done, qdec_done = sem("qk_normed"), sem("diff_done"), sem("decay_done"), sem("qdec_done")
    gram_m_out, gram_q_out, negm_done, qkT_done = sem("gram_m_out"), sem("gram_q_out"), sem("negm_done"), sem("qkT_done")
    kT_out, vT_out, k_scaled, v_scaled = sem("kT_out"), sem("vT_out"), sem("k_scaled"), sem("v_scaled")
    m_stored, m_in, x_inv, x_stored, invT_placed, inv_zero = (sem("m_stored"), sem("m_in"), sem("x_inv"), sem("x_stored"),
                                                           sem("invT_placed"), sem("inv_zero"))
    merge_out, merge_act, merge_dve = sem("merge_out"), sem("merge_act"), sem("merge_dve")
    delta_out, delta_act, delta_dve = sem("delta_out"), sem("delta_act"), sem("delta_dve")
    o_len, o_mean, o_root, o_diag, o_rows, ps_free = (sem("o_len"), sem("o_mean"), sem("o_root"), sem("o_diag"), sem("o_rows"),
                                                      sem("ps_free"))
    o_gained, inv_placed = sem("o_gained"), sem("inv_placed")
    gm_masked, v_gelu, v_mean, v_root, v_normed = sem("gm_masked"), sem("v_gelu"), sem("v_mean"), sem("v_root"), sem("v_normed")
    u_scaled, u_gelu, sv_out, sv_biased, ya_dve, ya_hi, ya_lo = (sem("u_scaled"), sem("u_gelu"), sem("sv_out"), sem("sv_biased"),
                                                               sem("ya_dve"), sem("ya_hi"), sem("ya_lo"))
    z_scaled, z_silu, z_gated, yb_hi, yb_lo = sem("z_scaled"), sem("z_silu"), sem("z_gated"), sem("yb_hi"), sem("yb_lo")
    gate_scaled, gate_sig, mix_prod, mix_hi, mix_lo = sem("gate_scaled"), sem("gate_sig"), sem("mix_prod"), sem("mix_hi"), sem("mix_lo")
    res = [{k: sem(f"{k}{n}") for k in ("x", "sq", "gain", "added", "hi", "lo")} for n in range(2)]
    ff_scaled, ff_silu, ff_gate, ff_prod, ff_hi, ff_lo = (sem("ff_scaled"), sem("ff_silu"), sem("ff_gate"), sem("ff_prod"),
                                                        sem("ff_hi"), sem("ff_lo"))
    p_in, p_hi, p_lo, pw_done = sem("p_in"), sem("p_hi"), sem("p_lo"), sem("pw_done")
    ple_scaled, ple_sig, ple_prod, ple_x, ple_sq, ple_gain = (sem("ple_scaled"), sem("ple_sig"), sem("ple_prod"), sem("ple_x"),
                                                            sem("ple_sq"), sem("ple_gain"))
    out_dve, out_pool, stored = sem("out_dve"), sem("out_pool"), sem("stored")

    def load_half(sp, src, row, h, n):
        if not (isinstance(h, int) and h < RING):
            sp.wait_ge(lo_done, h - RING + 1)
        sp.dma_start(raw[:, n % RING], src[ds(row, P), :].rearrange("p (k n) -> p k n", k=HALF_K)).then_inc(raw_in[n % RING], 16)

    def split_hi(act, phase, i, n):
        h, s = half_of(phase, i, n + LEAD), (n + LEAD) % RING
        if isinstance(h, int) and h >= TOTAL:
            return
        act.wait_ge(raw_in[s], i * (16 * PER[phase] // RING) + 16 * (H0[phase] // RING + (n + LEAD) // RING + 1))
        if not (isinstance(h, int) and h < RING):
            act.wait_ge(half_used, h - RING + 1)
        nc.scalar.activation(whi[:, s], raw[:, s], ACT.Copy).then_inc(hi_done, 1)

    def split_lo(dve, phase, i, n):
        h, s = half_of(phase, i, n + LEAD), (n + LEAD) % RING
        if isinstance(h, int) and h >= TOTAL:
            return
        dve.wait_ge(hi_done, h + 1)
        nc.vector.tensor_tensor(wlo[:, s], raw[:, s], whi[:, s].bitcast(F32), ALU.subtract).then_inc(lo_done, 1)

    def use_half(pe, phase, i, n, buf, first, last, kt0, xhi, xlo, rows=False):
        s = n % RING
        pe.wait_ge(lo_done, half_of(phase, i, n) + 1)
        for kt in range(HALF_K):
            k = kt0 + kt
            begin, end = first and kt == 0, last and kt == HALF_K - 1
            if rows:
                for m in range(TILES):
                    xh, xl = xhi[:, k, m * P:(m + 1) * P], xlo[:, k, m * P:(m + 1) * P]
                    o = acc[buf][:, m]
                    nc.tensor.matmul(o, xh, whi[:, s, kt], start=begin, stop=False, skip_group_check=True)
                    nc.tensor.matmul(o, xh, wlo[:, s, kt], start=False, stop=False, skip_group_check=True)
                    mm = nc.tensor.matmul(o, xl, whi[:, s, kt], start=False, stop=end, skip_group_check=True)
            else:
                for m in range(4):
                    o = accv[buf][:, m]
                    wh, wl = whi[:, s, kt, m * P:(m + 1) * P], wlo[:, s, kt, m * P:(m + 1) * P]
                    nc.tensor.matmul(o, wh, xhi[:, k], start=begin and m % 2 == 0, stop=False, skip_group_check=True)
                    nc.tensor.matmul(o, wh, xlo[:, k], start=False, stop=False, skip_group_check=True)
                    mm = nc.tensor.matmul(o, wl, xhi[:, k], start=False, stop=end, skip_group_check=True)
        mm.then_inc(half_used, 1)

    def acc_free(pe, phase, i, buf, n):
        u = use_of(phase, i, buf, n)
        if not (isinstance(u, int) and u == 0):
            pe.wait_ge(acc_read[buf], u)

    def acc_full(eng, phase, i, end):
        eng.wait_ge(half_used, half_of(phase, i, end))

    def carry_wait(eng):
        eng.sem_inc(waits_carried, 1)

    def bc(ap, n):
        return ap.unsqueeze(2).to_broadcast([ap.shape[0], ap.shape[1], n])

    def over(r, n):
        return r.unsqueeze(1).to_broadcast([r.shape[0], n, r.shape[1]])

    def piece(ap, j):
        return ap[:, 2 * j:2 * j + 2]

    def tiles(ap, blk, j):
        return ap[:, ds(4 * blk + 2 * j, 2)]

    with nc.Block() as block:

        @block.sync
        def _(sp):
            sp.dma_start(cols[:], cols_d).then_inc(cols_in, 16)
            for c in range(4):
                sp.dma_start(xT[:, 4 * c:4 * c + 4], xT_d[:, 4 * c:4 * c + 4]).then_inc(x_in[c], 16)
                load_half(sp, win, (BLK_K * HID + c) * P, c, c)
            sp.dma_start(wba_sb[:], wba).then_inc(ba_in, 16)
            sp.dma_start(hv[32:48, 0:2], hv_d).then_inc(ba_in, 16)

            def w_in_block(phase, i, blk, n0, skip=0):
                for n in range(skip, HID):
                    load_half(sp, win, (blk * HID + n) * P, half_of(phase, i, n0 + n), n0 + n)

            w_in_block("qkv", 0, BLK_K, 0, RING)
            w_in_block("qkv", 0, BLK_Q, HID)
            w_in_block("qkv", 0, BLK_DV, 2 * HID)
            with sp.Fori(1, NGROUPS) as g:
                w_in_block("qkv", g, BLK_K + g, 0)
                w_in_block("qkv", g, BLK_Q + g, HID)
                w_in_block("qkv", g, BLK_DV + g, 2 * HID)
            w_in_block("uv", 0, BLK_V, 0)
            w_in_block("uv", 0, BLK_V + 1, HID)
            w_in_block("uv", 0, BLK_U, 2 * HID)
            w_in_block("uv", 0, BLK_U + 1, 3 * HID)
            with sp.Fori(0, 2) as i:
                for b in range(2):
                    w_in_block("z", i, BLK_Z + 2 * i + b, b * HID)
            with sp.Fori(0, NB) as i:
                w_in_block("mix", i, BLK_GA + i, 0)
                w_in_block("mix", i, BLK_GB + i, HID)
                for n in range(HGM):
                    load_half(sp, wa, (i * HGM + n) * P, half_of("mix", i, 2 * HID + n), 2 * HID + n)
                for n in range(HID):
                    load_half(sp, wb, (i * HID + n) * P, half_of("mix", i, 2 * HID + HGM + n), 2 * HID + HGM + n)
            with sp.Fori(0, 2) as i:
                for n in range(2 * HID):
                    load_half(sp, wo, (i * (2 * HID) + n) * P, half_of("out", i, n), n)
            with sp.Fori(0, FB) as i:
                for b in range(2):
                    for n in range(HID):
                        load_half(sp, wgu, ((i + b * FB) * HID + n) * P, half_of("ffn", i, b * HID + n), b * HID + n)
            with sp.Fori(0, 2) as i:
                for n in range(2 * HFF):
                    load_half(sp, wd, (i * (2 * HFF) + n) * P, half_of("down", i, n), n)
            for n in range(NB):
                load_half(sp, wpp, n * P, half_of("proj", 0, n), n)
            with sp.Fori(0, 2) as i:
                for n in range(2 * HID):
                    load_half(sp, wpg, (i * (2 * HID) + n) * P, half_of("ple", i, n), n)
            for c in range(4):
                if c == 3:
                    sp.wait_ge(out_pool, 1)
                else:
                    sp.wait_ge(out_dve, c + 1)
                sp.dma_start(out_d[:, 4 * c:4 * c + 4], xT[:, 4 * c:4 * c + 4]).then_inc(stored, 16)
            sp.wait_ge(stored, 64)

        @block.gpsimd
        def _(pool):
            g = nc.gpsimd

            def chain(ins, value):
                ins.then_inc(pool_step, 1)
                pool.wait_ge(pool_step, value)

            g.memset(ones[:], 1.0).then_inc(consts_made, 1)
            chain(g.memset(ident[:], 0.0), 1)
            g.affine_select(out=ident[:], in_=ident[:], compare_op=ALU.not_equal, fill=1.0, base=0,
                            pattern=[[-1, P]], channel_multiplier=1).then_inc(consts_made, 1)
            chain(g.memset(mask_m[:], 0.0), 2)
            g.affine_select(out=mask_m[:], in_=mask_m[:], compare_op=ALU.is_gt, fill=BIG, base=0,
                            pattern=[[-1, P]], channel_multiplier=1).then_inc(consts_made, 1)
            chain(g.memset(mask_q[:], 0.0), 3)
            g.affine_select(out=mask_q[:], in_=mask_q[:], compare_op=ALU.is_ge, fill=-BIG, base=0,
                            pattern=[[1, P]], channel_multiplier=-1).then_inc(consts_made, 1)
            g.memset(bg[:], 0.0).then_inc(consts_made, 1)
            g.memset(pre[:, :, 0:4], 0.0).then_inc(consts_made, 1)
            chain(g.memset(sqsum[:], 0.0), 4)
            for c in range(4):
                pool.wait_ge(x0_sq, c + 1)
                chain(g.tensor_tensor(sqsum[:], sqsum[:], piece(t[1], 0), ALU.add), 5 + c)
                g.tensor_tensor(sqsum[:], sqsum[:], piece(t[1], 1), ALU.add).then_inc(sq_added, 1)
                pool.wait_ge(sq_added, c + 1)
            pool.wait_ge(cols_in, 16)
            pool.wait_ge(ba_in, 32)
            g.tensor_tensor(wba_sb[:], wba_sb[:], bc(cols[:, C_MIX:C_MIX + KD], 48), ALU.mult).then_inc(wba_scaled, 1)

            INV_STEPS = 64

            def invert(d, v):
                pool.wait_ge(negm_done, d + 1)
                carry_wait(pool)
                chain(g.memset(blk_x[:], 0.0), v + 1)
                carry_wait(pool)
                chain(g.memset(blk_x[:].rearrange("p i j -> p (i j)")[:, 0:1024:33], 1.0), v + 2)
                pool.wait_ge(m_stored, 64 * (d + 1))
                carry_wait(pool)
                pool.dma_start(blk_m[:], scratch_m.rearrange("a h i j -> (a h) i j")).then_inc(m_in, 16)
                g.memset(inv[:], 0.0)
                g.memset(invT[:], 0.0).then_inc(inv_zero, 1)
                pool.wait_ge(m_in, 16 * (d + 1))
                for j in range(31):
                    r, c = 31 - j, j + 1
                    tmp = blk_t[:, 0:r, 0:c]
                    chain(g.tensor_tensor(tmp, blk_m[:, j + 1:32, j:j + 1].to_broadcast([32, r, c]),
                                          blk_x[:, j:j + 1, 0:c].to_broadcast([32, r, c]), ALU.mult), v + 3 + 2 * j)
                    chain(g.tensor_tensor(blk_x[:, j + 1:32, 0:c], blk_x[:, j + 1:32, 0:c], tmp, ALU.add), v + 4 + 2 * j)
                carry_wait(pool)
                g.tensor_copy(blk_t[:], blk_x[:].rearrange("p i j -> p j i")).then_inc(x_inv, 1)
                pool.wait_ge(x_inv, d + 1)
                carry_wait(pool)
                pool.dma_start(scratch_x[1].rearrange("a h i j -> (a h) i j"), blk_t[:]).then_inc(x_stored, 16)
                pool.dma_start(scratch_x[0].rearrange("a h i j -> (a h) i j"), blk_x[:]).then_inc(x_stored, 16)
                pool.wait_ge(x_stored, 32 * (d + 1))
                pool.wait_ge(inv_zero, d + 1)
                carry_wait(pool)
                for a in range(4):
                    pool.dma_start(invT[32 * a:32 * a + 32, :, 32 * a:32 * a + 32],
                                   scratch_x[1, a].rearrange("h i j -> i h j")).then_inc(invT_placed, 16)

            v0 = 8
            with pool.Fori(0, NGROUPS) as d:
                invert(d, v0 + d * INV_STEPS)
            v0 += NGROUPS * INV_STEPS
            pool.wait_ge(invT_placed, 64 * NGROUPS)
            pool.dma_start(gmw[:], gmw_d).then_inc(gm_in, 16)
            pool.dma_start(gmb[:].rearrange("p g n -> p (g n)"), gmb_d.to_broadcast([P, GM])).then_inc(gm_in, 16)
            pool.dma_start(praw[:], pT_d).then_inc(p_in, 16)
            pool.wait_ge(gm_in, 32)
            g.affine_select(out=gmw[:], in_=gmw[:], compare_op=ALU.is_ge, fill=0.0, base=0,
                            pattern=[[0, GMT], [1, P]], channel_multiplier=-1).then_inc(gm_masked, 1)

            def residual(n, gain):
                s = res[n]
                pool.wait_ge(sq_summed, n + 1)
                g.memset(sqsum[:], 0.0).then_inc(s["added"], 1)
                pool.wait_ge(s["added"], 1)
                with pool.Fori(0, 2) as i:
                    for b in range(2):
                        for j in range(2):
                            q = 4 * i + 2 * b + j
                            pool.wait_ge(s["x"], q + 1)
                            g.tensor_tensor(piece(t[0], j), tiles(xT, 2 * i + b, j),
                                            bc(cols[:, ds(gain + 4 * (2 * i + b) + 2 * j, 2)], SEQ), ALU.mult).then_inc(s["gain"], 1)
                            pool.wait_ge(s["sq"], q + 1)
                            g.tensor_tensor(sqsum[:], sqsum[:], piece(t[1], j), ALU.add).then_inc(s["added"], 1)
                            pool.wait_ge(s["added"], q + 2)

            residual(0, C_FFN)
            with pool.Fori(0, FB) as i:
                for j in range(2):
                    pool.wait_ge(ff_silu, 2 * i + j + 1)
                    g.tensor_tensor(piece(t[1], j), piece(t[0], j), over(R[:], 2), ALU.mult).then_inc(ff_gate, 1)
            residual(1, C_PLE)
            pool.wait_ge(sq_summed, 3)
            chain(g.memset(sqsum[:], 0.0), v0 + 1)
            for b in range(NB):
                for j in range(2):
                    q = 2 * b + j
                    pool.wait_ge(ple_sig, q + 1)
                    if b == 0:
                        pool.wait_ge(pw_done, NB)
                    g.tensor_tensor(piece(t[0], j), piece(t[0], j), tiles(pw, b, j), ALU.mult).then_inc(ple_prod, 1)
                for j in range(2):
                    q = 2 * b + j
                    pool.wait_ge(ple_sq, q + 1)
                    g.tensor_tensor(sqsum[:], sqsum[:], piece(t[1], j), ALU.add).then_inc(sq_added, 1)
                    g.tensor_tensor(tiles(xT, b, j), tiles(xT, b, j),
                                    bc(cols[:, C_FIN + 4 * b + 2 * j:C_FIN + 4 * b + 2 * j + 2], SEQ), ALU.mult).then_inc(ple_gain, 1)
                    pool.wait_ge(sq_added, 5 + q)
            pool.wait_ge(r_done, 4)
            pool.wait_ge(ple_gain, 8)
            g.tensor_tensor(xT[:, 12:16], xT[:, 12:16], over(R[:], 4), ALU.mult).then_inc(out_pool, 1)

        @block.tensor
        def _(pe):
            mm = nc.tensor.matmul

            def gemm(phase, i, n0, halves, buf, use, xhi, xlo, rows=False, after=None):
                acc_free(pe, phase, i, buf, use)
                for n in range(halves):
                    use_half(pe, phase, i, n0 + n, buf, n == 0, n == halves - 1, HALF_K * n, xhi, xlo, rows)
                    if after and n in after:
                        after[n]()

            def sum_squares(n):
                for k in range(2):
                    last = mm(psf[0][:, 0:SEQ], ones[:], sqsum[:, k], start=(k == 0), stop=(k == 1))
                last.then_inc(sq_summed, 1)

            def beta_a():
                pe.wait_ge(wba_scaled, 1)
                for k in range(KD):
                    last = mm(psf[1][0:48, 0:SEQ], wba_sb[:, k], xT[:, k], start=(k == 0), stop=(k == KD - 1))
                last.then_inc(ba_out, 1)
                pe.wait_ge(r_done, 1)
                for m in range(TILES):
                    last = mm(psf[0][:, COLS + m:COLS + m + 1], R[0:1, m * P:(m + 1) * P], ones[0:1, 0:1], start=True, stop=True)
                last.then_inc(rcol_out, 1)

            def tok_columns():
                pe.wait_ge(ba_act, 5)
                pe.wait_ge(ba_dve, 7)
                pe.wait_ge(rcol_done, 1)
                for m in range(TILES):
                    last = nc.tensor.transpose(psf[0][:, m * 80:m * 80 + 80], bg[:, m * P:(m + 1) * P], ident[0:80, 0:80])
                last.then_inc(tok_T, 1)

            def first_sum():
                pe.wait_ge(sq_added, 4)
                sum_squares(0)

            pe.wait_ge(consts_made, 6)
            def x_part(c):
                return lambda: pe.wait_ge(x0_lo, c + 1)
            x_part(0)()
            def tok_tile(ap, h, m):
                return ap[:, h, m * P:(m + 1) * P]

            def columns(src, n, signal):
                for h in range(GROUP):
                    for m in range(TILES):
                        c = 8 * n + 2 * h + m
                        last = mm(psf[0][:, c:c + 1], tok_tile(src, h, m), ones[:, 0:1], start=True, stop=True)
                last.then_inc(signal, 1)

            def rows(src, signal):
                for b in range(2):
                    last = mm(ps[0][:, b], ones[:], piece(src, b).rearrange("p h n -> p (h n)"), start=True, stop=True)
                last.then_inc(signal, 1)

            def k_columns(g, first=False):
                pe.wait_ge(qk_sq, 2 * g + 1)
                if first:
                    pe.wait_ge(ps_free, 1)
                columns(t[1], 1, qk_len)

            def k_rows(g):
                pe.wait_ge(qk_diag, 2 * g + 1)
                rows(t[1], qk_rows)

            def q_columns(g):
                pe.wait_ge(qk_sq, 2 * g + 2)
                pe.wait_ge(negm_done, g + 1)
                columns(t[0], 0, qk_len)

            def q_rows(g):
                pe.wait_ge(qk_diag, 2 * g + 2)
                rows(t[0], qk_rows)

            def grams(g):
                pe.wait_ge(ps_free, g + 1)
                pe.wait_ge(sel_done, g + 1)
                for h in range(GROUP):
                    last = mm(psv[1][:, h], selg[32:48, h:h + 1].to_broadcast([16, P]), bg[32:48, :], start=True, stop=True)
                last.then_inc(g_out, 1)
                pe.wait_ge(qk_normed, 2 * g + 1)
                for m in range(TILES):
                    for h in range(GROUP):
                        last = mm(psq[0][:, 4 * m + h], tok_tile(kn, h, m), tok_tile(kn, h, m), start=True, stop=True)
                last.then_inc(gram_m_out, 1)

            def transpose_k(g):
                pe.wait_ge(diff_done, 2 * g + 2)
                for m in range(TILES):
                    for h in range(GROUP):
                        last = nc.tensor.transpose(psq[1][:, 4 * m + h], tok_tile(kn, h, m), ident[:])
                last.then_inc(kT_out, 1)

            def gram_q(g):
                pe.wait_ge(qk_normed, 2 * g + 2)
                pe.wait_ge(k_scaled, 2 * g + 2)
                for m in range(TILES):
                    for h in range(GROUP):
                        last = mm(psq[1][:, 4 * m + h], tok_tile(kn, h, m), tok_tile(qn, h, m), start=True, stop=True)
                last.then_inc(gram_q_out, 1)

            def transpose_v(d):
                pe.wait_ge(convv_silu, d + 1)
                pe.wait_ge(qkT_done, d + 1)
                for m in range(TILES):
                    for h in range(GROUP):
                        last = nc.tensor.transpose(psq[1][:, 4 * m + h], tok_tile(conv[2], h, m), ident[:])
                last.then_inc(vT_out, 1)

            PAIRS = ((0, 32), (64, 96))

            def merge32_a(d):
                pe.wait_ge(invT_placed, 64 * (d + 1))
                pe.wait_ge(qk_normed, 2 * d + 2)
                carry_wait(pe)
                for a, (top, low) in enumerate(PAIRS):
                    for x in range(8):
                        last = mm(ps[0][top:top + 32, a, 32 * x:32 * x + 32], negm[low:low + 32, x, top:top + 32],
                                  invT[low:low + 32, x, low:low + 32], start=True, stop=True)
                last.then_inc(merge_out, 1)

            def merge32_b(d):
                pe.wait_ge(merge_act, 3 * d + 2)
                pe.wait_ge(v_scaled, 2 * d + 2)
                pe.wait_ge(inv_placed, 64 * (d + 1))
                carry_wait(pe)
                for a, (top, low) in enumerate(PAIRS):
                    for x in range(8):
                        last = mm(ps[1][top:top + 32, a, 32 * x:32 * x + 32], inv[top:top + 32, x, top:top + 32],
                                  p32[top:top + 32, x], start=True, stop=True)
                for x in range(8):
                    last = mm(ps[1][32:64, 0, 256 + 32 * x:288 + 32 * x], p32[0:32, x], inv[0:32, x, 0:32], start=True, stop=True)
                last.then_inc(merge_out, 1)

            def merge64_a(d):
                pe.wait_ge(merge_dve, 4 * d + 2)
                pe.wait_ge(merge_act, 3 * d + 3)
                carry_wait(pe)
                for x in range(8):
                    last = mm(ps[0][0:64, 0, 64 * x:64 * x + 64], negm[64:128, x, 0:64], invT[64:128, x, 64:128], start=True, stop=True)
                last.then_inc(merge_out, 1)

            def merge64_b(d):
                pe.wait_ge(merge_dve, 4 * d + 3)
                carry_wait(pe)
                for x in range(8):
                    last = mm(ps[0][0:64, 1, 64 * x:64 * x + 64], inv[0:64, x, 0:64], p64[:, x], start=True, stop=True)
                last.then_inc(merge_out, 1)

            def first_tile(d):
                pe.wait_ge(merge_dve, 4 * d + 4)
                for h in range(GROUP):
                    last = mm(psq[1][:, h], invT[:, h], vbeta[:, h], start=True, stop=True)
                last.then_inc(delta_out, 1)
                for h in range(GROUP):
                    last = mm(psq[1][:, 4 + h], kbeg[:, h], invT[:, 4 + h], start=True, stop=True)
                last.then_inc(delta_out, 1)

            def carry(d):
                pe.wait_ge(delta_act, 3 * d + 1)
                for h in range(GROUP):
                    last = mm(psq[0][:, h], ktail[:, h], vnew[:, h], start=True, stop=True)
                last.then_inc(delta_out, 1)

            def second_tile(d):
                pe.wait_ge(delta_dve, 2 * d + 2)
                for h in range(GROUP):
                    mm(psq[0][:, 4 + h], invT[:, 4 + h], vbeta[:, 4 + h], start=True, stop=False)
                    last = mm(psq[0][:, 4 + h], nwT[:, h], state[:, h], start=False, stop=True)
                last.then_inc(delta_out, 1)

            def outputs(d):
                pe.wait_ge(delta_act, 3 * d + 2)
                pe.wait_ge(qdec_done, d + 1)
                for h in range(GROUP):
                    mm(psv[1][:, h, 0:P], vnew[:, h], qkT[:, h], start=True, stop=True)
                    mm(psv[1][:, h, P:SEQ], vnew[:, 4 + h], qkT[:, 4 + h], start=True, stop=False)
                    last = mm(psv[1][:, h, P:SEQ], state[:, h], qdec[:, h], start=False, stop=True)
                last.then_inc(delta_out, 1)

            def o_columns(d, g=None):
                pe.wait_ge(delta_act, 3 * d + 3)
                if g is not None:
                    pe.wait_ge(qk_mean, 2 * g + 1)
                columns(t[2], 2, o_len)

            def k_rows_after_o(g):
                pe.wait_ge(o_mean, 2 * g - 1)
                k_rows(g)

            def o_row(d, g=None):
                pe.wait_ge(o_diag, d + 1)
                if g is not None:
                    pe.wait_ge(qk_normed, 2 * g + 1)
                rows(t[2], o_rows)

            FINISH = {3: transpose_v, 4: merge32_a, 5: merge32_b, 6: merge64_a, 7: merge64_b, 8: first_tile, 9: carry,
                      10: second_tile, 11: outputs}
            START = {15: grams, 18: transpose_k, 19: q_columns, 21: q_rows, 22: gram_q}

            def stages(d, g, n0):
                steps = {}

                def put(n, f, *a):
                    if n0 <= n < n0 + HID:
                        steps.setdefault(n - n0, []).append(lambda: f(*a))
                if d is not None:
                    for n, f in FINISH.items():
                        put(n, f, d)
                    put(12, o_columns, d, g)
                    put(14, o_row, d, g)
                if g is not None:
                    put(11, k_columns, g, d is None)
                    put(13, k_rows if d is None else k_rows_after_o, g)
                    for n, f in START.items():
                        put(n, f, g)
                return steps

            def group(g, d, extra=({}, {})):
                for p, buf, use in ((0, 0, 0), (1, 1, 0), (2, 0, 1)):
                    after = {n: (lambda fs: lambda: [f() for f in fs])(fs) for n, fs in stages(d, g, p * HID).items()}
                    if p < 2:
                        after.update(extra[p])
                    gemm("qkv", g, p * HID, HID, buf, use, ahi, alo, after=after)

            group(0, None, extra=({1: lambda: (x_part(1)(), first_sum()), 3: x_part(2), 4: beta_a, 5: x_part(3)},
                                  {0: tok_columns}))
            with pe.Fori(1, NGROUPS) as g:
                group(g, g - 1)

            def spatial():
                pe.wait_ge(v_normed, TILES)
                pe.wait_ge(gm_masked, 1)
                pe.wait_ge(ps_free, NGROUPS + 1)
                for x in range(GMT):
                    for m in range(TILES):
                        last = mm(psv[x // 4][:, x % 4, m * P:(m + 1) * P], vg[:, m, x * P:(x + 1) * P], gmw[:, x], start=True, stop=True)
                last.then_inc(sv_out, 1)

            for p, buf in ((0, 0), (1, 1)):
                last_steps = {n: (lambda fs: lambda: [f() for f in fs])(fs) for n, fs in stages(NGROUPS - 1, None, p * HID).items()}
                gemm("uv", 0, p * HID, HID, buf, 0, ahi, alo, rows=True, after=last_steps)
            gemm("uv", 0, 2 * HID, HID, 0, 1, ahi, alo)
            gemm("uv", 0, 3 * HID, HID, 1, 1, ahi, alo, after={4: spatial})

            with pe.Fori(0, 2) as i:
                for b in range(2):
                    gemm("z", i, b * HID, HID, b, 0, ahi, alo)
            with pe.Fori(0, NB) as i:
                gemm("mix", i, 0, HID, 0, 0, ahi, alo)
                gemm("mix", i, HID, HID, 1, 0, ahi, alo)
                pe.wait_ge(ya_lo, 2)
                gemm("mix", i, 2 * HID, HGM, 0, 1, yahi, yalo)
                pe.wait_ge(yb_lo, 8)
                gemm("mix", i, 2 * HID + HGM, HID, 1, 1, ybhi, yblo)

            def operand_ready(done, last):
                return lambda: pe.wait_ge(done, last)

            pe.wait_ge(mix_lo, 6)
            gemm("out", 0, 0, HID, 0, 0, mhi, mlo, after={5: operand_ready(mix_lo, 8)})
            gemm("out", 0, HID, HID, 1, 0, mhi, mlo)
            with pe.Fori(1, 2) as i:
                for b in range(2):
                    gemm("out", i, b * HID, HID, b, 0, mhi, mlo)

            def next_sum(n):
                def f():
                    pe.wait_ge(res[n]["added"], 9)
                    sum_squares(n + 1)
                return f

            pe.wait_ge(res[0]["lo"], 6)
            gemm("ffn", 0, 0, HID, 0, 0, ahi, alo, after={1: next_sum(0), 5: operand_ready(res[0]["lo"], 8)})
            gemm("ffn", 0, HID, HID, 1, 0, ahi, alo)
            with pe.Fori(1, FB) as i:
                for b in range(2):
                    gemm("ffn", i, b * HID, HID, b, 0, ahi, alo)
            pe.wait_ge(ff_lo, 2 * FB - 2)
            gemm("down", 0, 0, HFF, 0, 0, fhi, flo, after={HFF - 3: operand_ready(ff_lo, 2 * FB)})
            gemm("down", 0, HFF, HFF, 1, 0, fhi, flo)
            with pe.Fori(1, 2) as i:
                for b in range(2):
                    gemm("down", i, b * HFF, HFF, b, 0, fhi, flo)
            pe.wait_ge(p_lo, 1)
            for b in range(NB):
                gemm("proj", 0, b, 1, b % 2, b // 2, phi, plo, after={0: next_sum(1)} if b == 1 else None)
            pe.wait_ge(res[1]["lo"], 8)
            for i in range(2):
                for b in range(2):
                    gemm("ple", i, b * HID, HID, b, 0, ahi, alo)
            pe.wait_ge(sq_added, 12)
            sum_squares(3)

        @block.scalar
        def _(act):
            f = nc.scalar.activation

            def split(phase, i, a, b):
                for n in range(a, b):
                    split_hi(act, phase, i, n)

            def root(n):
                act.wait_ge(mean_inv, 2 * n + 2)
                f(R[:], Rt[:], ACT.Sqrt).then_inc(r_done, 1)

            for n in range(-LEAD, 0):
                split_hi(act, "qkv", 0, n)
                c = n + LEAD
                act.wait_ge(x_in[c], 16)
                if c:
                    act.wait_ge(sq_added, c)
                f(t[1][:], xT[:, 4 * c:4 * c + 4], ACT.Square).then_inc(x0_sq, 1)
                act.wait_ge(x0_gain, c + 1)
                f(ahi[:, 4 * c:4 * c + 4], t[2 * (c % 2)][:], ACT.Copy).then_inc(x0_hi, 1)
            act.wait_ge(x_in[3], 16)
            act.wait_ge(sq_added, 3)
            f(t[1][:], xT[:, 12:16], ACT.Square).then_inc(x0_sq, 1)
            act.wait_ge(x0_gain, 4)
            f(ahi[:, 12:16], t[2][:], ACT.Copy).then_inc(x0_hi, 1)

            def silu_qk(c, p, g):
                act.wait_ge(conv_done, 12 * g + 4 * (p + 1))
                f(conv[c][:], conv[c][:], ACT.Silu).then_inc(conv_silu, 1)
                act.wait_ge(conv_silu, 2 * g + p + 1)
                f(t[c][:], conv[c][:], ACT.Square).then_inc(qk_sq, 1)

            def silu_k(g):
                silu_qk(1, 0, g)

            def silu_q(g):
                silu_qk(0, 1, g)

            def k_root(d):
                act.wait_ge(qk_inv, 2 * d + 1)
                f(length[:, 1], length[:, 1], ACT.Sqrt).then_inc(qk_root, 1)

            def q_root(d):
                act.wait_ge(qk_inv, 2 * d + 2)
                f(length[:, 0], length[:, 0], ACT.Sqrt).then_inc(qk_root, 1)

            def g_exp(d):
                act.wait_ge(g_out, d + 1)
                f(vnew[:, 4:8], psv[1][:, :, P:SEQ], ACT.Exp).then_inc(decay_done, 1)

            def decay_m(d):
                act.wait_ge(diff_done, 2 * d + 1)
                f(negm[:], negm[:], ACT.Exp, scale=-1.0).then_inc(decay_done, 1)

            def decay_q(d):
                act.wait_ge(diff_done, 2 * d + 2)
                f(qkT[:], qkT[:], ACT.Exp).then_inc(decay_done, 1)

            def silu_v(d):
                act.wait_ge(conv_done, 12 * d + 12)
                f(conv[2][:], conv[2][:], ACT.Silu).then_inc(convv_silu, 1)

            def copy_p32(d):
                act.wait_ge(merge_out, 4 * d + 1)
                for a, top in enumerate((0, 64)):
                    f(p32[top:top + 32], heads(ps[0][top:top + 32, a, 0:256], 32), ACT.Copy).then_inc(merge_act, 1)

            def copy_inv(d):
                act.wait_ge(merge_out, 4 * d + 2)
                f(inv[32:64, :, 0:32], heads(ps[1][32:64, 0, 256:512], 32), ACT.Copy).then_inc(merge_act, 1)

            def copy_v0(d):
                act.wait_ge(delta_out, 5 * d + 1)
                f(vnew[:, 0:4], psq[1][:, 0:4], ACT.Copy).then_inc(delta_act, 1)

            def copy_v1(d):
                act.wait_ge(delta_out, 5 * d + 4)
                f(vnew[:, 4:8], psq[0][:, 4:8], ACT.Copy).then_inc(delta_act, 1)

            def square_o(d):
                act.wait_ge(delta_out, 5 * d + 5)
                f(t[2][:], psv[1], ACT.Square).then_inc(delta_act, 1)

            def o_rt(d):
                act.wait_ge(o_mean, 2 * d + 2)
                f(length[:, 2], length[:, 2], ACT.Sqrt).then_inc(o_root, 1)

            def store_m(g):
                act.wait_ge(negm_done, g + 1)
                carry_wait(act)
                for a in range(4):
                    act.dma_start(scratch_m[a].rearrange("h i j -> i h j"),
                                  negm[32 * a:32 * a + 32, :, 32 * a:32 * a + 32]).then_inc(m_stored, 16)

            def place_inv(d):
                act.wait_ge(x_stored, 32 * (d + 1))
                act.wait_ge(inv_zero, d + 1)
                carry_wait(act)
                for a in range(4):
                    act.dma_start(inv[32 * a:32 * a + 32, :, 32 * a:32 * a + 32],
                                  scratch_x[0, a].rearrange("h i j -> i h j")).then_inc(inv_placed, 16)

            FINISH = {2: (silu_v,), 4: (place_inv,), 5: (copy_p32,), 6: (copy_inv,), 9: (copy_v0,), 11: (copy_v1,),
                      12: (square_o,), 13: (o_rt,)}
            START = {10: (silu_k,), 12: (k_root,), 16: (g_exp, decay_m), 17: (decay_q, store_m), 18: (silu_q,), 20: (q_root,)}

            def beta_g():
                act.wait_ge(ba_dve, 1)
                f(bg[0:16, :], g1[0:16, :], ACT.Sigmoid).then_inc(ba_act, 1)
                f(hv[32:48, 2:3], hv[32:48, 1:2], ACT.Exp).then_inc(ba_act, 1)
                act.wait_ge(ba_dve, 3)
                f(g2[32:48, :], g2[32:48, :], ACT.Exp, scale=-1.0).then_inc(ba_act, 1)
                act.wait_ge(ba_act, 3)
                f(g2[32:48, :], g2[32:48, :], ACT.Ln, bias=1.0).then_inc(ba_act, 1)

            def tails():
                act.wait_ge(ba_dve, 7)
                f(bg[64:80, 0:P], bg[32:48, 0:P], ACT.Exp, bias=bg[32:48, P - 1:P], scale=-1.0).then_inc(ba_act, 1)

            def tok_exp():
                act.wait_ge(tok_done, 2)
                f(tok[:, 3], tok[:, 1], ACT.Exp).then_inc(tok_eg, 1)

            for n in range(3 * HID):
                split_hi(act, "qkv", 0, n)
                if n == 2:
                    root(0)
                if n == 6:
                    beta_g()
                if n == 7:
                    tails()
                if n == 9:
                    tok_exp()
                for stage in START.get(n, ()):
                    stage(0)
            with act.Fori(1, NGROUPS) as g:
                for n in range(3 * HID):
                    split_hi(act, "qkv", g, n)
                    for stage in FINISH.get(n, ()):
                        stage(g - 1)
                    for stage in START.get(n, ()):
                        stage(g)

            def v_block(b):
                acc_full(act, "uv", 0, HID * (b + 1))
                if b == 0:
                    act.wait_ge(qk_normed, 2 * NGROUPS)
                for m in range(TILES):
                    x = f(vg[:, m, COLS * b:COLS * (b + 1)], acc[b][:, m], ACT.Gelu, scale=rcol[:, m:m + 1])
                    x.then_inc(v_gelu, 1)
                    if m == TILES - 1:
                        act.wait_ge(v_gelu, 4 * b + 3)
                        act.sem_inc(acc_read[b], 1)
                    else:
                        act.wait_ge(v_gelu, 4 * b + 2 * m + 1)
                    f(t[2][:, 0:2].rearrange("p a n -> p (a n)"), vg[:, m, COLS * b:COLS * (b + 1)], ACT.Square,
                      accum_out=vsum[:, b, m:m + 1]).then_inc(v_gelu, 1)
                    act.wait_ge(v_gelu, 4 * b + 2 * m + 2)

            def u_block(b):
                act.wait_ge(ps_free, NGROUPS + 1)
                for j in range(2):
                    act.wait_ge(u_scaled, 2 * b + j + 1)
                    f(uT[:, 4 * b + 2 * j:4 * b + 2 * j + 2], piece(t[0], j), ACT.Gelu).then_inc(u_gelu, 1)

            for n in range(4 * HID):
                split_hi(act, "uv", 0, n)
                for stage in FINISH.get(n, ()):
                    stage(NGROUPS - 1)
                if n in (7, 15):
                    v_block(n // 8)
                if n == 18:
                    act.wait_ge(v_mean, 3)
                    f(vrms[:], vrms[:], ACT.Sqrt).then_inc(v_root, 1)
                if n in (23, 31):
                    u_block(n // 8 - 2)
            for j in range(2):
                act.wait_ge(ya_dve, j + 1)
                f(yahi[:, 4 * j:4 * j + 4], ytmp[:, 4 * j:4 * j + 4], ACT.Copy).then_inc(ya_hi, 1)
            act.wait_ge(p_in, 16)
            f(phi[:], praw[:], ACT.Copy).then_inc(p_hi, 1)

            with act.Fori(0, 2) as i:
                for b in range(2):
                    split(("z"), i, b * HID, (b + 1) * HID)
                    for j in range(2):
                        act.wait_ge(z_scaled, 4 * i + 2 * b + j + 1)
                        f(piece(t[0], j), piece(t[0], j), ACT.Silu).then_inc(z_silu, 1)
                    for j in range(2):
                        act.wait_ge(z_gated, 4 * i + 2 * b + j + 1)
                        f(tiles(ybhi, 2 * i + b, j), piece(t[1], j), ACT.Copy).then_inc(yb_hi, 1)
            with act.Fori(0, NB) as i:
                for b in range(2):
                    split("mix", i, b * HID, (b + 1) * HID)
                    for j in range(2):
                        act.wait_ge(gate_scaled, 4 * i + 2 * b + j + 1)
                        f(piece(t[b], j), piece(t[b], j), ACT.Sigmoid).then_inc(gate_sig, 1)
                split("mix", i, 2 * HID, PER["mix"])
                for j in range(2):
                    act.wait_ge(mix_prod, 6 * i + 5 + j)
                    f(tiles(mhi, i, j), piece(t[2], j), ACT.Copy).then_inc(mix_hi, 1)

            def residual(n, phase, halves):
                s = res[n]
                with act.Fori(0, 2) as i:
                    for b in range(2):
                        split(phase, i, b * halves, (b + 1) * halves)
                        for j in range(2):
                            q = 4 * i + 2 * b + j
                            act.wait_ge(s["x"], q + 1)
                            act.wait_ge(s["added"], 1 + 4 * i + (0, 0, 1, 2)[2 * b + j])
                            f(piece(t[1], j), tiles(xT, 2 * i + b, j), ACT.Square).then_inc(s["sq"], 1)
                        for j in range(2):
                            act.wait_ge(s["gain"], 4 * i + 2 * b + j + 1)
                            f(tiles(ahi, 2 * i + b, j), piece(t[0], j), ACT.Copy).then_inc(s["hi"], 1)

            residual(0, "out", HID)
            root(1)
            with act.Fori(0, FB) as i:
                split("ffn", i, 0, HID)
                for j in range(2):
                    act.wait_ge(ff_scaled, 2 * i + j + 1)
                    f(piece(t[0], j), piece(t[0], j), ACT.Silu).then_inc(ff_silu, 1)
                split("ffn", i, HID, 2 * HID)
                for j in range(2):
                    act.wait_ge(ff_prod, 2 * i + j + 1)
                    f(tiles(fhi, i, j), piece(t[2], j), ACT.Copy).then_inc(ff_hi, 1)
            residual(1, "down", HFF)
            split("proj", 0, 0, NB)
            root(2)
            for i in range(2):
                for b in range(2):
                    split("ple", i, b * HID, (b + 1) * HID)
                    for j in range(2):
                        act.wait_ge(ple_scaled, 4 * i + 2 * b + j + 1)
                        f(piece(t[0], j), piece(t[0], j), ACT.Sigmoid).then_inc(ple_sig, 1)
                    for j in range(2):
                        q = 4 * i + 2 * b + j
                        act.wait_ge(ple_x, q + 1)
                        if q >= 2:
                            act.wait_ge(sq_added, 4 + q - 1)
                        f(piece(t[1], j), tiles(xT, 2 * i + b, j), ACT.Square).then_inc(ple_sq, 1)
            root(3)

        @block.vector
        def _(dve):
            v = nc.vector

            def split(phase, i, a, b):
                for n in range(a, b):
                    split_lo(dve, phase, i, n)

            def mean(n):
                dve.wait_ge(sq_summed, n + 1)
                v.tensor_scalar(Rt[:], psf[0][:, 0:SEQ], 1.0 / D, EPS, ALU.mult, ALU.add).then_inc(mean_inv, 1)
                dve.wait_ge(mean_inv, 2 * n + 1)
                v.reciprocal(Rt[:], Rt[:]).then_inc(mean_inv, 1)

            def x_gain(c):
                dve.wait_ge(x_in[c], 16)
                if c >= 2:
                    dve.wait_ge(x0_lo, c - 1)
                v.tensor_tensor(t[2 * (c % 2)][:], xT[:, 4 * c:4 * c + 4], bc(cols[:, C_MIX + 4 * c:C_MIX + 4 * c + 4], SEQ),
                                ALU.mult).then_inc(x0_gain, 1)

            def x_lo(c):
                dve.wait_ge(x0_hi, c + 1)
                v.tensor_tensor(alo[:, 4 * c:4 * c + 4], t[2 * (c % 2)][:], ahi[:, 4 * c:4 * c + 4].bitcast(F32),
                                ALU.subtract).then_inc(x0_lo, 1)

            dve.wait_ge(cols_in, 16)
            for n in range(-LEAD, 0):
                c = n + LEAD
                x_gain(c)
                split_lo(dve, "qkv", 0, n)
                x_lo(c)
            x_gain(3)
            x_lo(3)

            def evac(p, g):
                acc_full(dve, "qkv", g, (p + 1) * HID)
                if not (isinstance(g, int) and g == 0 and p == 0):
                    dve.wait_ge(conv_done, 12 * g + 4 * p)
                buf = p % 2
                v.tensor_tensor(pre[:, :, 4:], accv[buf], over(R[:], 4), ALU.mult).then_inc(pre_done, 1)
                dve.wait_ge(pre_done, 3 * g + p + 1)
                dve.sem_inc(acc_read[buf], 1)

            def convolve(c, p, g, pair):
                for tap in range(4):
                    for n in range(2):
                        h = 2 * pair + n
                        y = conv[c][:, h]
                        w = cols[:, ds(C_CONV + tap * 48 + c * HEADS + GROUP * g + h, 1)]
                        src = pre[:, h, 1 + tap:1 + tap + SEQ]
                        if tap == 0:
                            ins = v.tensor_scalar(y, src, w, None, ALU.mult)
                        else:
                            dve.wait_ge(conv_mac, 36 * g + 12 * p + 6 * pair + 2 * (tap - 1) + n + 1)
                            ins = v.scalar_tensor_tensor(y, src, w, y, ALU.mult, ALU.add)
                        ins.then_inc(conv_done if tap == 3 else conv_mac, 1)

            def conv_a(c, p):
                return lambda g: convolve(c, p, g, 0)

            def conv_b(c, p):
                return lambda g: convolve(c, p, g, 1)

            def invert_mean(n, c, eps, factor, d):
                dve.wait_ge(qk_len, 2 * d + n)
                x = length[:, c]
                v.tensor_scalar(x, psf[0][:, 8 * c:8 * c + 8], eps, factor, ALU.add, ALU.mult).then_inc(qk_mean, 1)
                dve.wait_ge(qk_mean, 2 * d + n)
                v.reciprocal(x, x).then_inc(qk_inv, 1)

            def k_mean(d):
                invert_mean(1, 1, EPS, 1.0, d)

            def q_mean(d):
                invert_mean(2, 0, EPS, float(P), d)

            def diagonal(c, signal):
                v.tensor_tensor(t[c][:].rearrange("p h (m n) -> p (h m) n", n=P), over(ident[:], 8), bc(length[:, c], P),
                                ALU.mult).then_inc(signal, 1)

            def k_diag(d):
                dve.wait_ge(qk_root, 2 * d + 1)
                diagonal(1, qk_diag)

            def q_diag(d):
                dve.wait_ge(qk_root, 2 * d + 2)
                diagonal(0, qk_diag)

            def norm_k(d):
                dve.wait_ge(qk_rows, 2 * d + 1)
                v.tensor_tensor(kn[:], psv[0], conv[1][:], ALU.mult).then_inc(qk_normed, 1)

            def norm_q(d):
                dve.wait_ge(qk_rows, 2 * d + 2)
                v.tensor_tensor(qn[:], psv[0], conv[0][:], ALU.mult).then_inc(qk_normed, 1)
                dve.wait_ge(qk_normed, 2 * d + 2)
                v.tensor_tensor(qdec[:], qn[:, :, P:SEQ], vnew[:, 4:8, :], ALU.mult).then_inc(qdec_done, 1)

            def token(k, m, h, d):
                return tok[:, k, m, ds(GROUP * d + h, 1)]

            def tokens(k, m, d):
                return bc(tok[:, k, m, ds(GROUP * d, GROUP)], P)

            def diff_m(d):
                dve.wait_ge(decay_done, 3 * d + 1)
                for m in range(TILES):
                    for h in range(GROUP):
                        x = v.scalar_tensor_tensor(negm[:, 4 * m + h], psv[1][:, h, m * P:(m + 1) * P], token(1, m, h, d), mask_m[:],
                                                   ALU.subtract, ALU.max)
                x.then_inc(diff_done, 1)

            def diff_q(d):
                for m in range(TILES):
                    for h in range(GROUP):
                        x = v.scalar_tensor_tensor(qkT[:, 4 * m + h], psv[1][:, h, m * P:(m + 1) * P], token(1, m, h, d), mask_q[:],
                                                   ALU.subtract, ALU.min)
                x.then_inc(diff_done, 1)

            def make_negm(d):
                dve.wait_ge(gram_m_out, d + 1)
                dve.wait_ge(decay_done, 3 * d + 2)
                for m in range(TILES):
                    for h in range(GROUP):
                        x = v.scalar_tensor_tensor(negm[:, 4 * m + h], psq[0][:, 4 * m + h], token(4, m, h, d), negm[:, 4 * m + h],
                                                   ALU.mult, ALU.mult)
                x.then_inc(negm_done, 1)

            def scale_v(d):
                dve.wait_ge(vT_out, d + 1)
                for m in range(TILES):
                    v.tensor_tensor(vbeta[:, 4 * m:4 * m + 4], psq[1][:, 4 * m:4 * m + 4], tokens(0, m, d), ALU.mult).then_inc(v_scaled, 1)

            def scale_k(d):
                dve.wait_ge(kT_out, d + 1)
                v.tensor_tensor(ktail[:], psq[1][:, 0:4], tokens(2, 0, d), ALU.mult).then_inc(k_scaled, 1)
                v.tensor_tensor(kbeg[:], psq[1][:, 4:8], tokens(3, 1, d), ALU.mult).then_inc(k_scaled, 1)

            def make_qkT(d):
                dve.wait_ge(gram_q_out, d + 1)
                dve.wait_ge(decay_done, 3 * d + 3)
                v.tensor_tensor(qkT[:], psq[1], qkT[:], ALU.mult).then_inc(qkT_done, 1)

            def copy_invT32(d):
                dve.wait_ge(merge_out, 4 * d + 2)
                for a, (top, low) in enumerate(((0, 32), (64, 96))):
                    v.tensor_copy(invT[top:top + 32, :, low:low + 32], heads(ps[1][top:top + 32, a, 0:256], 32)).then_inc(merge_dve, 1)

            def copy_p64(d):
                dve.wait_ge(merge_out, 4 * d + 3)
                v.tensor_copy(p64[:], heads(ps[0][0:64, 0], 64)).then_inc(merge_dve, 1)

            def copy_invT64(d):
                dve.wait_ge(merge_out, 4 * d + 4)
                v.tensor_copy(invT[0:64, :, 64:128], heads(ps[0][0:64, 1], 64)).then_inc(merge_dve, 1)

            def copy_nwT(d):
                dve.wait_ge(delta_out, 5 * d + 2)
                v.tensor_scalar(nwT[:], psq[1][:, 4:8], -1.0, None, ALU.mult).then_inc(delta_dve, 1)

            def copy_state(d):
                dve.wait_ge(delta_out, 5 * d + 3)
                v.tensor_copy(state[:], psq[0][:, 0:4]).then_inc(delta_dve, 1)

            def o_inv(d):
                dve.wait_ge(o_len, d + 1)
                v.tensor_scalar(length[:, 2], psf[0][:, 16:24], 1.0 / P, EPS, ALU.mult, ALU.add).then_inc(o_mean, 1)
                dve.wait_ge(o_mean, 2 * d + 1)
                v.reciprocal(length[:, 2], length[:, 2]).then_inc(o_mean, 1)
                dve.wait_ge(delta_act, 3 * d + 3)
                v.tensor_scalar(oT[:, ds(GROUP * d, GROUP)], psv[1], cols[:, C_DNO:C_DNO + 1], None, ALU.mult).then_inc(o_gained, 1)

            def o_diagonal(d):
                dve.wait_ge(o_root, d + 1)
                diagonal(2, o_diag)

            def norm_o(d):
                dve.wait_ge(o_gained, d + 1)
                dve.wait_ge(o_rows, d + 1)
                o = oT[:, ds(GROUP * d, GROUP)]
                v.tensor_tensor(o, o, psv[0], ALU.mult).then_inc(ps_free, 1)

            def select_heads(g):
                v.tensor_copy(selg[32:48, :], ident[32:48, ds(32 + GROUP * g, GROUP)]).then_inc(sel_done, 1)

            FINISH = {0: (make_qkT, conv_a(2, 2)), 1: (conv_b(2, 2),), 4: (scale_v,), 6: (copy_invT32,), 7: (copy_p64,),
                      8: (copy_invT64,), 9: (copy_nwT,), 10: (copy_state,), 13: (o_inv,), 14: (o_diagonal,), 15: (norm_o,)}
            START = {8: (conv_a(1, 0),), 9: (conv_b(1, 0),), 11: (select_heads,), 12: (k_mean,), 13: (k_diag,), 14: (norm_k,),
                     16: (diff_m, conv_a(0, 1)), 17: (make_negm, diff_q, conv_b(0, 1)), 19: (scale_k,), 20: (q_mean,),
                     21: (q_diag,), 22: (norm_q,)}

            def beta_g():
                dve.wait_ge(ba_out, 1)
                v.tensor_tensor(g1[:], psf[1][0:48, 0:SEQ], R[0:48, :], ALU.mult).then_inc(ba_dve, 1)
                dve.wait_ge(ba_dve, 1)
                v.tensor_scalar(g1[32:48, :], g1[32:48, :], hv[32:48, 0:1], None, ALU.add).then_inc(ba_dve, 1)
                dve.wait_ge(ba_dve, 2)
                v.scalar_tensor_tensor(g2[32:48, :], g1[32:48, :], -1.0, g1[32:48, :], ALU.mult, ALU.max).then_inc(ba_dve, 1)
                dve.wait_ge(rcol_out, 1)
                v.tensor_copy(rcol[:], psf[0][:, COLS:COLS + TILES]).then_inc(rcol_done, 1)
                dve.wait_ge(ba_act, 4)
                v.scalar_tensor_tensor(g1[32:48, :], g1[32:48, :], 0.0, g2[32:48, :], ALU.max, ALU.add).then_inc(ba_dve, 1)
                dve.wait_ge(ba_dve, 4)
                v.tensor_scalar(g2[32:48, :], g1[32:48, :], hv[32:48, 2:3], -1.0, ALU.mult, ALU.mult).then_inc(ba_dve, 1)
                dve.wait_ge(ba_dve, 5)
                for m in range(TILES):
                    v.tensor_tensor_scan(bg[32:48, m * P:(m + 1) * P], ones[32:48, :], g2[32:48, m * P:(m + 1) * P], 0.0,
                                         ALU.mult, ALU.add).then_inc(ba_dve, 1)

            def tok_copy():
                dve.wait_ge(tok_T, 1)
                src = psf[0][:, 0:160].rearrange("p (m c) -> p m c", m=TILES)
                for k in (1, 0, 2):
                    v.tensor_copy(tok[:, k], src[:, :, 32 * k:32 * k + 16]).then_inc(tok_done, 1)
                dve.wait_ge(tok_done, 3)
                v.tensor_scalar(tok[:, 4], tok[:, 0], -1.0, None, ALU.mult).then_inc(tok_done, 1)
                dve.wait_ge(tok_eg, 1)
                v.tensor_tensor(tok[:, 3], tok[:, 3], tok[:, 0], ALU.mult).then_inc(tok_done, 1)
                dve.wait_ge(tok_done, 5)
                dve.sem_inc(ps_free, 1)

            for n in range(3 * HID):
                split_lo(dve, "qkv", 0, n)
                if n == 2:
                    mean(0)
                if n == 6:
                    beta_g()
                if n == 9:
                    tok_copy()
                for stage in START.get(n, ()):
                    stage(0)
                if n in (7, 15, 23):
                    evac(n // 8, 0)
            with dve.Fori(1, NGROUPS) as g:
                for n in range(3 * HID):
                    split_lo(dve, "qkv", g, n)
                    for stage in START.get(n, ()):
                        stage(g)
                    for stage in FINISH.get(n, ()):
                        stage(g - 1)
                    if n in (7, 15, 23):
                        evac(n // 8, g)

            def v_norm():
                dve.wait_ge(v_gelu, 8)
                v.tensor_tensor(vrms[:], vsum[:, 0], vsum[:, 1], ALU.add).then_inc(v_mean, 1)
                dve.wait_ge(v_mean, 1)
                v.tensor_scalar(vrms[:], vrms[:], 1.0 / GM, EPS, ALU.mult, ALU.add).then_inc(v_mean, 1)
                dve.wait_ge(v_mean, 2)
                v.reciprocal(vrms[:], vrms[:]).then_inc(v_mean, 1)

            def v_scale():
                dve.wait_ge(v_root, 1)
                for m in range(TILES):
                    v.tensor_scalar(vg[:, m], vg[:, m], vrms[:, m:m + 1], None, ALU.mult).then_inc(v_normed, 1)

            def u_block(b):
                acc_full(dve, "uv", 0, (b + 3) * HID)
                for j in range(2):
                    if b:
                        dve.wait_ge(u_gelu, j + 1)
                    v.tensor_tensor(piece(t[0], j), piece(accv[b], j), over(R[:], 2), ALU.mult).then_inc(u_scaled, 1)
                dve.wait_ge(u_scaled, 2 * b + 2)
                dve.sem_inc(acc_read[b], 1)

            def sv_bias():
                dve.wait_ge(sv_out, 1)
                for x in range(GMT):
                    ins = v.scalar_tensor_tensor(ytmp[:, x].rearrange("p (m t) -> p m t", m=TILES),
                                                 psv[x // 4][:, x % 4].rearrange("p (m t) -> p m t", m=TILES), cols[:, C_GMV + x:C_GMV + x + 1],
                                                 over(gmb[:, x], TILES), ALU.mult, ALU.add)
                ins.then_inc(sv_biased, 1)

            for n in range(4 * HID):
                split_lo(dve, "uv", 0, n)
                for stage in FINISH.get(n, ()):
                    stage(NGROUPS - 1)
                if n == 16:
                    v_norm()
                if n == 19:
                    v_scale()
                if n == 23:
                    u_block(0)
                if n == 29:
                    sv_bias()
            u_block(1)
            dve.wait_ge(sv_biased, 1)
            for j in range(2):
                dve.wait_ge(u_gelu, 2 * j + 2)
                v.tensor_tensor(ytmp[:, 4 * j:4 * j + 4], ytmp[:, 4 * j:4 * j + 4], uT[:, 4 * j:4 * j + 4], ALU.mult).then_inc(ya_dve, 1)
            for j in range(2):
                dve.wait_ge(ya_hi, j + 1)
                v.tensor_tensor(yalo[:, 4 * j:4 * j + 4], ytmp[:, 4 * j:4 * j + 4], yahi[:, 4 * j:4 * j + 4].bitcast(F32), ALU.subtract).then_inc(ya_lo, 1)
            dve.wait_ge(p_hi, 1)
            v.tensor_tensor(plo[:], praw[:], phi[:].bitcast(F32), ALU.subtract).then_inc(p_lo, 1)

            def times_row(phase, i, end, buf, dst, signal, value):
                acc_full(dve, phase, i, end)
                for j in range(2):
                    x = v.tensor_tensor(piece(dst, j), piece(accv[buf], j), over(R[:], 2), ALU.mult)
                    x.then_inc(signal, 1)
                dve.wait_ge(signal, value + 2)
                dve.sem_inc(acc_read[buf], 1)

            def take_lo(hi, lo, src, blk, done, signal, value):
                for j in range(2):
                    dve.wait_ge(done, value + j + 1)
                    v.tensor_tensor(tiles(lo, blk, j), piece(src, j), tiles(hi, blk, j).bitcast(F32), ALU.subtract).then_inc(signal, 1)

            with dve.Fori(0, 2) as i:
                for b in range(2):
                    split("z", i, b * HID, (b + 1) * HID)
                    times_row("z", i, (b + 1) * HID, b, t[0], z_scaled, 4 * i + 2 * b)
                    for j in range(2):
                        dve.wait_ge(z_silu, 4 * i + 2 * b + j + 1)
                        v.tensor_tensor(piece(t[1], j), tiles(oT, 2 * i + b, j), piece(t[0], j), ALU.mult).then_inc(z_gated, 1)
                    take_lo(ybhi, yblo, t[1], 2 * i + b, yb_hi, yb_lo, 4 * i + 2 * b)
            with dve.Fori(0, NB) as i:
                for b in range(2):
                    split("mix", i, b * HID, (b + 1) * HID)
                    times_row("mix", i, (b + 1) * HID, b, t[b], gate_scaled, 4 * i + 2 * b)
                split("mix", i, 2 * HID, 2 * HID + HGM)
                for b in range(2):
                    if b:
                        split("mix", i, 2 * HID + HGM, PER["mix"])
                    acc_full(dve, "mix", i, 2 * HID + HGM + b * HID)
                    for j in range(2):
                        dve.wait_ge(gate_sig, 4 * i + 2 * b + j + 1)
                        v.tensor_tensor(piece(t[b], j), piece(accv[b], j), piece(t[b], j), ALU.mult).then_inc(mix_prod, 1)
                    dve.wait_ge(mix_prod, 6 * i + 2 * b + 2)
                    dve.sem_inc(acc_read[b], 1)
                for j in range(2):
                    v.tensor_tensor(piece(t[2], j), piece(t[0], j), piece(t[1], j), ALU.add).then_inc(mix_prod, 1)
                take_lo(mhi, mlo, t[2], i, mix_hi, mix_lo, 2 * i)

            def residual(n, phase, halves):
                s = res[n]
                with dve.Fori(0, 2) as i:
                    for b in range(2):
                        split(phase, i, b * halves, (b + 1) * halves)
                        acc_full(dve, phase, i, (b + 1) * halves)
                        q = 4 * i + 2 * b
                        for j in range(2):
                            v.tensor_tensor(tiles(xT, 2 * i + b, j), piece(accv[b], j), tiles(xT, 2 * i + b, j), ALU.add).then_inc(s["x"], 1)
                        dve.wait_ge(s["x"], q + 2)
                        dve.sem_inc(acc_read[b], 1)
                        take_lo(ahi, alo, t[0], 2 * i + b, s["hi"], s["lo"], q)

            residual(0, "out", HID)
            mean(1)
            dve.wait_ge(r_done, 2)
            with dve.Fori(0, FB) as i:
                split("ffn", i, 0, HID)
                times_row("ffn", i, HID, 0, t[0], ff_scaled, 2 * i)
                split("ffn", i, HID, 2 * HID)
                acc_full(dve, "ffn", i, 2 * HID)
                for j in range(2):
                    dve.wait_ge(ff_gate, 2 * i + j + 1)
                    v.tensor_tensor(piece(t[2], j), piece(accv[1], j), piece(t[1], j), ALU.mult).then_inc(ff_prod, 1)
                dve.wait_ge(ff_prod, 2 * i + 2)
                dve.sem_inc(acc_read[1], 1)
                take_lo(fhi, flo, t[2], i, ff_hi, ff_lo, 2 * i)
            residual(1, "down", HFF)
            for b in range(NB):
                split("proj", 0, b, b + 1)
                acc_full(dve, "proj", 0, b + 1)
                v.tensor_copy(pw[:, 4 * b:4 * b + 4], accv[b % 2]).then_inc(pw_done, 1)
                dve.wait_ge(pw_done, b + 1)
                dve.sem_inc(acc_read[b % 2], 1)
                if b == 1:
                    mean(2)
            dve.wait_ge(r_done, 3)
            for i in range(2):
                for b in range(2):
                    split("ple", i, b * HID, (b + 1) * HID)
                    times_row("ple", i, (b + 1) * HID, b, t[0], ple_scaled, 4 * i + 2 * b)
                    for j in range(2):
                        dve.wait_ge(ple_prod, 4 * i + 2 * b + j + 1)
                        v.tensor_tensor(tiles(xT, 2 * i + b, j), tiles(xT, 2 * i + b, j), piece(t[0], j), ALU.add).then_inc(ple_x, 1)
            mean(3)
            dve.wait_ge(r_done, 4)
            dve.wait_ge(ple_gain, 8)
            for c in range(3):
                v.tensor_tensor(xT[:, 4 * c:4 * c + 4], xT[:, 4 * c:4 * c + 4], over(R[:], 4), ALU.mult).then_inc(out_dve, 1)


def halves(w):
    k, n = w.shape
    x = w.reshape(k // (HALF_K * P), HALF_K, P, n // COLS, COLS).transpose(3, 0, 2, 1, 4)
    return np.ascontiguousarray(x.reshape(-1, HALF_K * COLS))


def features(a, n):
    return np.ascontiguousarray(a.reshape(SEQ, n, P).transpose(2, 1, 0))


def kernel(**inputs):
    from concourse import bacc
    from concourse.bass_utils import run_bass_kernel_spmd

    a = {k: np.asarray(v) for k, v in inputs.items()}
    w_in = a["w_in"][0]
    ba0 = 2 * GM + 4 * D
    wba = np.zeros((D, 48), np.float32)
    wba[:, 0:16] = w_in[:, ba0:ba0 + HEADS]
    wba[:, 32:48] = w_in[:, ba0 + HEADS:ba0 + 2 * HEADS]

    def per_feature(x):
        return x.reshape(-1, P).T

    conv_w = a["dn_conv_w"][0]
    arrays = {
        "win": halves(np.concatenate([w_in[:, :ba0], w_in[:, ba0 + 2 * HEADS:]], axis=1)),
        "wba": np.ascontiguousarray(wba.reshape(KD, P, 48).transpose(1, 0, 2)),
        "wa": halves(a["w_branch_a"][0]), "wb": halves(a["w_branch_b"][0]), "wo": halves(a["w_out"][0]),
        "wgu": halves(a["w_gate_up"][0]), "wd": halves(a["w_down"][0]), "wpg": halves(a["w_ple_gate"][0]),
        "wpp": halves(a["w_ple_proj"][0]),
        "xT": features(a["x"][0], KD), "pT": features(a["p"][0, 0], PLE // P),
        "cols": np.ascontiguousarray(np.concatenate([
            per_feature(a["norm_mix"][0]), per_feature(a["norm_ffn"][0]), per_feature(a["ple_norm"][0]),
            per_feature(a["norm_final"]), per_feature(a["gm_v_norm"][0]), per_feature(a["dn_out_norm"][0])]
            + [per_feature(conv_w[t]) for t in range(4)], axis=1)),
        "hv": np.ascontiguousarray(np.stack([a["dn_dt_bias"][0], a["dn_a_log"][0]], axis=1)),
        "gmw": np.ascontiguousarray(a["gm_w_s"][0].transpose(2, 0, 1)),
        "gmb": np.ascontiguousarray(a["gm_b_s"][0].reshape(1, GM)),
    }
    nc = bacc.Bacc("TRN2", target_bir_lowering=False, num_devices=1)
    args = [nc.dram_tensor(f"in_{k}", x.shape, mybir.dt.from_np(x.dtype), kind="ExternalInput").ap() for k, x in arrays.items()]
    out = nc.dram_tensor("out_T", (P, KD, SEQ), F32, kind="ExternalOutput").ap()
    build(nc, *args, out)
    r = run_bass_kernel_spmd(nc, [{f"in_{k}": x for k, x in arrays.items()}], core_ids=[0])
    got = np.asarray(r.results[0]["out_T"])
    return np.ascontiguousarray(got.transpose(2, 1, 0)).reshape(1, SEQ, D)
```

```python
import numpy as np

import concourse.bass as bass
from concourse import mybir

F32 = mybir.dt.float32
F32R = mybir.dt.float32r
ACT = mybir.ActivationFunctionType
ALU = mybir.AluOpType
ds = bass.ds

P = 128
SEQ = 256
D = 2048
TILES = SEQ // P
KD = D // P
HEADS = 16
GROUP = 4
NGROUPS = HEADS // GROUP
GM = 1024
GMT = GM // P
FF = 5632
KF = FF // P
PLE = 256
COLS = 512
HALF_K = 2
RING = 4
LEAD = 3
EPS = 1e-6
BIG = 1e30
HID = D // P // HALF_K
HGM = GM // P // HALF_K
HFF = KF // HALF_K
NB = D // COLS
FB = FF // COLS

BLK_U, BLK_V, BLK_Q, BLK_K, BLK_DV, BLK_Z, BLK_GA, BLK_GB = 0, 2, 4, 8, 12, 16, 20, 24

C_MIX, C_FFN, C_PLE, C_FIN, C_GMV, C_DNO, C_CONV = 0, 16, 32, 48, 64, 72, 73
NCOL = C_CONV + 4 * 48

PLAN = [("qkv", 4, 3 * HID, (2, 1)), ("uv", 1, 4 * HID, (2, 2)), ("z", 2, 2 * HID, (1, 1)),
        ("mix", NB, 3 * HID + HGM, (2, 2)), ("out", 2, 2 * HID, (1, 1)), ("ffn", FB, 2 * HID, (1, 1)),
        ("down", 2, 2 * HFF, (1, 1)), ("proj", 1, 4, (2, 2)), ("ple", 2, 2 * HID, (1, 1))]
H0, PER, U0 = {}, {}, {}
_h, _u = 0, [0, 0]
for _name, _n, _per, _uses in PLAN:
    H0[_name], PER[_name], U0[_name] = _h, _per, (tuple(_u), _uses)
    _h += _n * _per
    _u = [_u[0] + _n * _uses[0], _u[1] + _n * _uses[1]]
TOTAL = _h


def half_of(phase, i, n):
    return H0[phase] + PER[phase] * i + n


def use_of(phase, i, buf, n):
    base, per = U0[phase]
    return base[buf] + per[buf] * i + n


def build(nc, win, wba, wa, wb, wo, wgu, wd, wpg, wpp, xT_d, pT_d, cols_d, hv_d, gmw_d, gmb_d, out_d):
    scratch_m = nc.dram_tensor("inv_in", (8, 4, 32, 32), F32, kind="Internal").ap()
    scratch_x = nc.dram_tensor("inv_out", (8, 4, 8, 4, 32), F32, kind="Internal").ap()

    cursor = [(nc.sbuf_base + 63) // 64 * 64]

    def at(name, shape, dt, offset=None):
        size = int(np.prod(shape[1:])) * 4
        if offset is None:
            offset = cursor[0]
            cursor[0] += (size + 31) // 32 * 32
        return nc.alloc_sbuf_tensor_at(name, shape, dt, offset=offset)

    def sem(name):
        return nc.alloc_semaphore(name)

    raw = at("raw", [P, RING, HALF_K, COLS], F32)
    whi = at("whi", [P, RING, HALF_K, COLS], F32R)
    wlo = at("wlo", [P, RING, HALF_K, COLS], F32R)
    xT = at("xT", [P, KD, SEQ], F32)
    ahi = at("ahi", [P, KD, SEQ], F32R)
    alo = at("alo", [P, KD, SEQ], F32R)
    region = cursor[0]
    cursor[0] += 2 * KF * SEQ * 4

    def shared(name, shape, dt, kib):
        return at(name, shape, dt, offset=region + int(kib * 1024))

    oT = shared("oT", [P, HEADS, SEQ], F32, 0)
    conv = [shared(f"conv_{c}", [P, GROUP, SEQ], F32, 16 + 4 * n) for n, c in enumerate("qkv")]
    kn = shared("kn", [P, GROUP, SEQ], F32, 32)
    vbeta = shared("vbeta", [P, 8, P], F32, 36)
    kbeg = shared("kbeg", [P, GROUP, P], F32, 40)
    ktail = shared("ktail", [P, GROUP, P], F32, 42)
    qdec = shared("qdec", [P, GROUP, P], F32, 44)
    negm = shared("negm", [P, 8, P], F32, 46)
    qkT = shared("qkT", [P, 8, P], F32, 50)
    inv = shared("inv", [P, 8, P], F32, 54)
    invT = shared("invT", [P, 8, P], F32, 58)
    blk_m = shared("blk_m", [P, 32, 32], F32, 62)
    blk_x = shared("blk_x", [P, 32, 8], F32, 66)
    blk_eye = shared("blk_eye", [P, 32, 8], F32, 67)
    blk_t = shared("blk_t", [P, 32, 8], F32, 68)
    blk_xT = shared("blk_xT", [P, 8, 32], F32, 69)
    diagT = shared("diagT", [P, 8, 32], F32, 70)
    vnew = shared("vnew", [P, 8, P], F32, 74)
    p32 = shared("p32", [P, 8, 32], F32, 78)
    p64 = shared("p64", [64, 8, 64], F32, 79)
    nwT = shared("nwT", [P, GROUP, P], F32, 81)
    state = shared("state", [P, GROUP, P], F32, 83)
    vg = shared("vg", [P, TILES, GM], F32, 16)
    uT = shared("uT", [P, GMT, SEQ], F32, 28)
    gmw = shared("gmw", [P, GMT, P], F32, 62)
    gmb = shared("gmb", [P, GMT, P], F32, 66)
    ytmp = shared("ytmp", [P, GMT, SEQ], F32, 16)
    wba_sb = shared("wba_sb", [P, KD, 48], F32, 62)
    g1 = shared("g1", [48, SEQ], F32, 71)
    g2 = shared("g2", [48, SEQ], F32, 72)
    praw = shared("praw", [P, PLE // P, SEQ], F32, 70)
    mask_m = shared("mask_m", [P, P], F32, 85)
    mask_q = shared("mask_q", [P, P], F32, 85.5)
    bg = shared("bg", [80, SEQ], F32, 86)
    ident = shared("ident", [P, P], F32, 87)
    yahi = shared("yahi", [P, GMT, SEQ], F32R, 72)
    yalo = shared("yalo", [P, GMT, SEQ], F32R, 80)
    ybhi = shared("ybhi", [P, KD, SEQ], F32R, 40)
    yblo = shared("yblo", [P, KD, SEQ], F32R, 56)
    mhi = shared("mhi", [P, KD, SEQ], F32R, 0)
    mlo = shared("mlo", [P, KD, SEQ], F32R, 16)
    fhi = shared("fhi", [P, KF, SEQ], F32R, 0)
    flo = shared("flo", [P, KF, SEQ], F32R, 44)
    pw = shared("pw", [P, KD, SEQ], F32, 0)

    cols = at("cols", [P, NCOL], F32)
    ones = at("ones", [P, P], F32)
    R = at("R", [P, SEQ], F32)
    Rt = at("Rt", [P, SEQ], F32)
    hv = at("hv", [48, 3], F32)
    tok = at("tok", [P, 5, TILES, HEADS], F32)
    selg = at("selg", [48, GROUP], F32)
    length = at("length", [P, 3, 8], F32)
    rcol = at("rcol", [P, TILES], F32)
    vsum = at("vsum", [P, 2, TILES], F32)
    vrms = at("vrms", [P, TILES], F32)
    sqsum = at("sqsum", [P, 2, SEQ], F32)
    t = [at(f"t{n}", [P, GROUP, SEQ], F32) for n in range(3)]
    pre_at = cursor[0]
    pre = at("pre", [P, GROUP, SEQ + 4], F32)
    phi = at("phi", [P, PLE // P, SEQ], F32R, offset=pre_at)
    plo = at("plo", [P, PLE // P, SEQ], F32R, offset=pre_at + 2048)

    acc = [nc.alloc_psum_tensor(f"acc{n}", [P, 2, COLS], F32) for n in range(2)]
    ps = [nc.alloc_psum_tensor(f"ps{n}", [P, 2, COLS], F32) for n in range(2)]
    psf = [x[:].rearrange("p a n -> p (a n)") for x in ps]

    def heads(flat, width):
        return flat.rearrange("p (h n) -> p h n", n=width)

    accv = [heads(a[:].rearrange("p a n -> p (a n)"), SEQ) for a in acc]
    psv = [heads(x, SEQ) for x in psf]
    psq = [heads(x, P) for x in psf]

    raw_in = [sem(f"raw_in{n}") for n in range(RING)]
    hi_done, lo_done, half_used = sem("hi_done"), sem("lo_done"), sem("half_used")
    acc_read = [sem(f"acc_read{n}") for n in range(2)]
    cols_in, x_in, ba_in, gm_in = sem("cols_in"), [sem(f"x_in{n}") for n in range(4)], sem("ba_in"), sem("gm_in")
    pool_step, waits_carried = sem("pool_step"), sem("waits_carried")
    consts_made, wba_scaled = sem("consts_made"), sem("wba_scaled")
    sq_added, sq_summed, mean_inv, r_done = sem("sq_added"), sem("sq_summed"), sem("mean_inv"), sem("r_done")
    x0_gain, x0_sq, x0_hi, x0_lo = sem("x0_gain"), sem("x0_sq"), sem("x0_hi"), sem("x0_lo")
    ba_out, rcol_out, rcol_done = sem("ba_out"), sem("rcol_out"), sem("rcol_done")
    ba_dve, ba_act, tok_T, tok_done = sem("ba_dve"), sem("ba_act"), sem("tok_T"), sem("tok_done")
    tok_eg = sem("tok_eg")
    pre_done, conv_mac, conv_done, conv_silu = sem("pre_done"), sem("conv_mac"), sem("conv_done"), sem("conv_silu")
    convv_silu = sem("convv_silu")
    qk_sq, sel_done, g_out = sem("qk_sq"), sem("sel_done"), sem("g_out")
    qk_len, qk_mean, k_inv, k_rooted, k_diag_done, k_rows_out = (sem("qk_len"), sem("qk_mean"), sem("k_inv"), sem("k_rooted"),
                                                                 sem("k_diag_done"), sem("k_rows_out"))
    k_normed, diff_done, decay_done, qdec_done = sem("k_normed"), sem("diff_done"), sem("decay_done"), sem("qdec_done")
    gram_m_out, gram_q_out, negm_done, qkT_done = sem("gram_m_out"), sem("gram_q_out"), sem("negm_done"), sem("qkT_done")
    kT_out, vT_out, k_scaled, v_scaled = sem("kT_out"), sem("vT_out"), sem("k_scaled"), sem("v_scaled")
    m_stored, m_in, x_inv, x_stored, invT_placed, inv_zero = (sem("m_stored"), sem("m_in"), sem("x_inv"), sem("x_stored"),
                                                           sem("invT_placed"), sem("inv_zero"))
    merge_out, merge_act, merge_dve = sem("merge_out"), sem("merge_act"), sem("merge_dve")
    delta_out, delta_act, delta_dve = sem("delta_out"), sem("delta_act"), sem("delta_dve")
    o_len, o_mean, o_root, o_diag, o_rows, ps_free = (sem("o_len"), sem("o_mean"), sem("o_root"), sem("o_diag"), sem("o_rows"),
                                                      sem("ps_free"))
    o_gained, diagT_in, eye_made = sem("o_gained"), sem("diagT_in"), sem("eye_made")
    gm_masked, v_gelu, v_mean, v_root, v_normed = sem("gm_masked"), sem("v_gelu"), sem("v_mean"), sem("v_root"), sem("v_normed")
    u_scaled, u_gelu, sv_out, sv_biased, ya_dve, ya_hi, ya_lo = (sem("u_scaled"), sem("u_gelu"), sem("sv_out"), sem("sv_biased"),
                                                               sem("ya_dve"), sem("ya_hi"), sem("ya_lo"))
    z_scaled, z_silu, z_gated, yb_hi, yb_lo = sem("z_scaled"), sem("z_silu"), sem("z_gated"), sem("yb_hi"), sem("yb_lo")
    gate_scaled, gate_sig, mix_prod, mix_hi, mix_lo = sem("gate_scaled"), sem("gate_sig"), sem("mix_prod"), sem("mix_hi"), sem("mix_lo")
    res = [{k: sem(f"{k}{n}") for k in ("x", "sq", "gain", "added", "hi", "lo")} for n in range(2)]
    ff_scaled, ff_silu, ff_gate, ff_prod, ff_hi, ff_lo = (sem("ff_scaled"), sem("ff_silu"), sem("ff_gate"), sem("ff_prod"),
                                                        sem("ff_hi"), sem("ff_lo"))
    p_in, p_hi, p_lo, pw_done = sem("p_in"), sem("p_hi"), sem("p_lo"), sem("pw_done")
    ple_scaled, ple_sig, ple_prod, ple_x, ple_sq, ple_gain = (sem("ple_scaled"), sem("ple_sig"), sem("ple_prod"), sem("ple_x"),
                                                            sem("ple_sq"), sem("ple_gain"))
    out_dve, out_pool, stored = sem("out_dve"), sem("out_pool"), sem("stored")

    def load_half(sp, src, row, h, n):
        if not (isinstance(h, int) and h < RING):
            sp.wait_ge(lo_done, h - RING + 1)
        sp.dma_start(raw[:, n % RING], src[ds(row, P), :].rearrange("p (k n) -> p k n", k=HALF_K)).then_inc(raw_in[n % RING], 16)

    def split_hi(act, phase, i, n):
        h, s = half_of(phase, i, n + LEAD), (n + LEAD) % RING
        if isinstance(h, int) and h >= TOTAL:
            return
        act.wait_ge(raw_in[s], i * (16 * PER[phase] // RING) + 16 * (H0[phase] // RING + (n + LEAD) // RING + 1))
        if not (isinstance(h, int) and h < RING):
            act.wait_ge(half_used, h - RING + 1)
        nc.scalar.activation(whi[:, s], raw[:, s], ACT.Copy).then_inc(hi_done, 1)

    def split_lo(dve, phase, i, n):
        h, s = half_of(phase, i, n + LEAD), (n + LEAD) % RING
        if isinstance(h, int) and h >= TOTAL:
            return
        dve.wait_ge(hi_done, h + 1)
        nc.vector.tensor_tensor(wlo[:, s], raw[:, s], whi[:, s].bitcast(F32), ALU.subtract).then_inc(lo_done, 1)

    def use_half(pe, phase, i, n, buf, first, last, kt0, xhi, xlo, rows=False):
        s = n % RING
        pe.wait_ge(lo_done, half_of(phase, i, n) + 1)
        for kt in range(HALF_K):
            k = kt0 + kt
            begin, end = first and kt == 0, last and kt == HALF_K - 1
            if rows:
                for m in range(TILES):
                    xh, xl = xhi[:, k, m * P:(m + 1) * P], xlo[:, k, m * P:(m + 1) * P]
                    o = acc[buf][:, m]
                    nc.tensor.matmul(o, xh, whi[:, s, kt], start=begin, stop=False, skip_group_check=True)
                    nc.tensor.matmul(o, xh, wlo[:, s, kt], start=False, stop=False, skip_group_check=True)
                    mm = nc.tensor.matmul(o, xl, whi[:, s, kt], start=False, stop=end, skip_group_check=True)
            else:
                for m in range(4):
                    o = accv[buf][:, m]
                    wh, wl = whi[:, s, kt, m * P:(m + 1) * P], wlo[:, s, kt, m * P:(m + 1) * P]
                    nc.tensor.matmul(o, wh, xhi[:, k], start=begin and m % 2 == 0, stop=False, skip_group_check=True)
                    nc.tensor.matmul(o, wh, xlo[:, k], start=False, stop=False, skip_group_check=True)
                    mm = nc.tensor.matmul(o, wl, xhi[:, k], start=False, stop=end, skip_group_check=True)
        mm.then_inc(half_used, 1)

    def acc_free(pe, phase, i, buf, n):
        u = use_of(phase, i, buf, n)
        if not (isinstance(u, int) and u == 0):
            pe.wait_ge(acc_read[buf], u)

    def acc_full(eng, phase, i, end):
        eng.wait_ge(half_used, half_of(phase, i, end))

    def carry_wait(eng):
        eng.sem_inc(waits_carried, 1)

    def bc(ap, n):
        return ap.unsqueeze(2).to_broadcast([ap.shape[0], ap.shape[1], n])

    def over(r, n):
        return r.unsqueeze(1).to_broadcast([r.shape[0], n, r.shape[1]])

    def piece(ap, j):
        return ap[:, 2 * j:2 * j + 2]

    def tiles(ap, blk, j):
        return ap[:, ds(4 * blk + 2 * j, 2)]

    with nc.Block() as block:

        @block.sync
        def _(sp):
            sp.dma_start(cols[:], cols_d).then_inc(cols_in, 16)
            for c in range(4):
                sp.dma_start(xT[:, 4 * c:4 * c + 4], xT_d[:, 4 * c:4 * c + 4]).then_inc(x_in[c], 16)
                load_half(sp, win, (BLK_K * HID + c) * P, c, c)
            sp.dma_start(wba_sb[:], wba).then_inc(ba_in, 16)
            sp.dma_start(hv[32:48, 0:2], hv_d).then_inc(ba_in, 16)

            def w_in_block(phase, i, blk, n0, skip=0):
                for n in range(skip, HID):
                    load_half(sp, win, (blk * HID + n) * P, half_of(phase, i, n0 + n), n0 + n)

            w_in_block("qkv", 0, BLK_K, 0, RING)
            w_in_block("qkv", 0, BLK_Q, HID)
            w_in_block("qkv", 0, BLK_DV, 2 * HID)
            with sp.Fori(1, NGROUPS) as g:
                w_in_block("qkv", g, BLK_K + g, 0)
                w_in_block("qkv", g, BLK_Q + g, HID)
                w_in_block("qkv", g, BLK_DV + g, 2 * HID)
            w_in_block("uv", 0, BLK_V, 0)
            w_in_block("uv", 0, BLK_V + 1, HID)
            w_in_block("uv", 0, BLK_U, 2 * HID)
            w_in_block("uv", 0, BLK_U + 1, 3 * HID)
            with sp.Fori(0, 2) as i:
                for b in range(2):
                    w_in_block("z", i, BLK_Z + 2 * i + b, b * HID)
            with sp.Fori(0, NB) as i:
                w_in_block("mix", i, BLK_GA + i, 0)
                w_in_block("mix", i, BLK_GB + i, HID)
                for n in range(HGM):
                    load_half(sp, wa, (i * HGM + n) * P, half_of("mix", i, 2 * HID + n), 2 * HID + n)
                for n in range(HID):
                    load_half(sp, wb, (i * HID + n) * P, half_of("mix", i, 2 * HID + HGM + n), 2 * HID + HGM + n)
            with sp.Fori(0, 2) as i:
                for n in range(2 * HID):
                    load_half(sp, wo, (i * (2 * HID) + n) * P, half_of("out", i, n), n)
            with sp.Fori(0, FB) as i:
                for b in range(2):
                    for n in range(HID):
                        load_half(sp, wgu, ((i + b * FB) * HID + n) * P, half_of("ffn", i, b * HID + n), b * HID + n)
            with sp.Fori(0, 2) as i:
                for n in range(2 * HFF):
                    load_half(sp, wd, (i * (2 * HFF) + n) * P, half_of("down", i, n), n)
            for n in range(NB):
                load_half(sp, wpp, n * P, half_of("proj", 0, n), n)
            with sp.Fori(0, 2) as i:
                for n in range(2 * HID):
                    load_half(sp, wpg, (i * (2 * HID) + n) * P, half_of("ple", i, n), n)
            for c in (0, 1, 6, 2, 3, 7, 4, 5):
                if c >= 6:
                    sp.wait_ge(out_pool, c - 5)
                else:
                    sp.wait_ge(out_dve, c + 1)
                sp.dma_start(out_d[:, 2 * c:2 * c + 2], xT[:, 2 * c:2 * c + 2]).then_inc(stored, 16)
            sp.wait_ge(stored, 128)

        @block.gpsimd
        def _(pool):
            g = nc.gpsimd

            def chain(ins, value):
                ins.then_inc(pool_step, 1)
                pool.wait_ge(pool_step, value)

            g.memset(ones[:], 1.0).then_inc(consts_made, 1)
            chain(g.memset(ident[:], 0.0), 1)
            g.affine_select(out=ident[:], in_=ident[:], compare_op=ALU.not_equal, fill=1.0, base=0,
                            pattern=[[-1, P]], channel_multiplier=1).then_inc(consts_made, 1)
            chain(g.memset(mask_m[:], 0.0), 2)
            g.affine_select(out=mask_m[:], in_=mask_m[:], compare_op=ALU.is_gt, fill=BIG, base=0,
                            pattern=[[-1, P]], channel_multiplier=1).then_inc(consts_made, 1)
            chain(g.memset(mask_q[:], 0.0), 3)
            g.affine_select(out=mask_q[:], in_=mask_q[:], compare_op=ALU.is_ge, fill=-BIG, base=0,
                            pattern=[[1, P]], channel_multiplier=-1).then_inc(consts_made, 1)
            g.memset(bg[:], 0.0).then_inc(consts_made, 1)
            g.memset(pre[:, :, 0:4], 0.0).then_inc(consts_made, 1)
            chain(g.memset(sqsum[:], 0.0), 4)
            g.memset(inv[:], 0.0)
            g.memset(invT[:], 0.0).then_inc(inv_zero, 1)
            g.memset(blk_eye[:], 0.0).then_inc(eye_made, 1)
            pool.wait_ge(eye_made, 1)
            for q in range(4):
                g.memset(blk_eye[32 * q:32 * q + 32].rearrange("p i c -> p (i c)")[:, 8 * q:256:33], 1.0).then_inc(eye_made, 1)
                pool.wait_ge(eye_made, q + 2)
            for q in range(8):
                pool.wait_ge(x0_sq, q + 1)
                g.tensor_tensor(sqsum[:], sqsum[:], piece(t[1], q % 2), ALU.add).then_inc(sq_added, 1)
                pool.wait_ge(sq_added, q + 1)
            pool.wait_ge(cols_in, 16)
            pool.wait_ge(ba_in, 32)
            g.tensor_tensor(wba_sb[:], wba_sb[:], bc(cols[:, C_MIX:C_MIX + KD], 48), ALU.mult).then_inc(wba_scaled, 1)

            INV_STEPS = 63

            def invert(d, v):
                pool.wait_ge(m_stored, 64 * (d + 1))
                carry_wait(pool)
                pool.dma_start(blk_m[:].rearrange("p i j -> p (i j)"),
                               scratch_m.rearrange("x a i j -> (x a) (i j)").unsqueeze(0).to_broadcast([4, 32, 1024])).then_inc(m_in, 16)
                chain(g.tensor_copy(blk_x[:], blk_eye[:]), v + 1)
                pool.wait_ge(m_in, 16 * (d + 1))
                for j in range(31):
                    r, c = 31 - j, j // 4 + 1
                    tmp = blk_t[:, 0:r, 0:c]
                    chain(g.tensor_tensor(tmp, blk_m[:, j + 1:32, j:j + 1].to_broadcast([P, r, c]),
                                          blk_x[:, j:j + 1, 0:c].to_broadcast([P, r, c]), ALU.mult), v + 2 + 2 * j)
                    chain(g.tensor_tensor(blk_x[:, j + 1:32, 0:c], blk_x[:, j + 1:32, 0:c], tmp, ALU.add), v + 3 + 2 * j)
                carry_wait(pool)
                g.tensor_copy(blk_xT[:], blk_x[:].rearrange("p i c -> p c i")).then_inc(x_inv, 1)
                pool.wait_ge(x_inv, d + 1)
                carry_wait(pool)
                pool.dma_start(scratch_x.rearrange("x a c q i -> q (x a) c i"), blk_xT[:]).then_inc(x_stored, 16)
                pool.wait_ge(x_stored, 16 * (d + 1))
                carry_wait(pool)
                pool.dma_start(diagT[:], scratch_x.rearrange("x a c q i -> (a c q) x i")).then_inc(diagT_in, 16)
                pool.wait_ge(diagT_in, 16 * (d + 1))
                carry_wait(pool)
                for a in range(4):
                    g.tensor_copy(invT[32 * a:32 * a + 32, :, 32 * a:32 * a + 32], diagT[32 * a:32 * a + 32]).then_inc(invT_placed, 1)
                    pool.wait_ge(invT_placed, 4 * d + a + 1)
                    carry_wait(pool)

            v0 = 4
            with pool.Fori(0, NGROUPS) as d:
                invert(d, v0 + d * INV_STEPS)
            v0 += NGROUPS * INV_STEPS
            pool.wait_ge(x_stored, 16 * NGROUPS)
            pool.dma_start(gmw[:], gmw_d).then_inc(gm_in, 16)
            pool.dma_start(gmb[:].rearrange("p g n -> p (g n)"), gmb_d.to_broadcast([P, GM])).then_inc(gm_in, 16)
            pool.wait_ge(merge_out, 4 * NGROUPS - 3)
            pool.dma_start(praw[:], pT_d).then_inc(p_in, 16)
            pool.wait_ge(gm_in, 32)
            g.affine_select(out=gmw[:], in_=gmw[:], compare_op=ALU.is_ge, fill=0.0, base=0,
                            pattern=[[0, GMT], [1, P]], channel_multiplier=-1).then_inc(gm_masked, 1)

            def residual(n):
                s = res[n]
                pool.wait_ge(sq_summed, n + 1)
                g.memset(sqsum[:], 0.0).then_inc(s["added"], 1)
                pool.wait_ge(s["added"], 1)
                with pool.Fori(0, 2) as i:
                    for q in range(4):
                        pool.wait_ge(s["sq"], 4 * i + q + 1)
                        g.tensor_tensor(sqsum[:], sqsum[:], piece(t[1], q % 2), ALU.add).then_inc(s["added"], 1)
                        pool.wait_ge(s["added"], 4 * i + q + 2)

            residual(0)
            with pool.Fori(0, FB) as i:
                for j in range(2):
                    pool.wait_ge(ff_silu, 2 * i + j + 1)
                    g.tensor_tensor(piece(t[1], j), piece(t[0], j), over(R[:], 2), ALU.mult).then_inc(ff_gate, 1)
            residual(1)
            pool.wait_ge(sq_summed, 3)
            chain(g.memset(sqsum[:], 0.0), v0 + 1)
            for b in range(NB):
                for j in range(2 if b < NB - 1 else 0):
                    q = 2 * b + j
                    pool.wait_ge(ple_sig, q + 1)
                    if b == 0:
                        pool.wait_ge(pw_done, NB)
                    g.tensor_tensor(piece(t[0], j), piece(t[0], j), tiles(pw, b, j), ALU.mult).then_inc(ple_prod, 1)
                for j in range(2):
                    q = 2 * b + j
                    pool.wait_ge(ple_sq, q + 1)
                    if b < NB - 1:
                        g.tensor_tensor(sqsum[:], sqsum[:], piece(t[1], j), ALU.add).then_inc(sq_added, 1)
                    g.tensor_tensor(tiles(xT, b, j), tiles(xT, b, j),
                                    bc(cols[:, C_FIN + 4 * b + 2 * j:C_FIN + 4 * b + 2 * j + 2], SEQ), ALU.mult).then_inc(ple_gain, 1)
                    if b < NB - 1:
                        pool.wait_ge(sq_added, 9 + q)
            pool.wait_ge(r_done, 4)
            pool.wait_ge(ple_gain, 8)
            for c in range(6, 8):
                g.tensor_tensor(xT[:, 2 * c:2 * c + 2], xT[:, 2 * c:2 * c + 2], over(R[:], 2), ALU.mult).then_inc(out_pool, 1)

        @block.tensor
        def _(pe):
            mm = nc.tensor.matmul

            def gemm(phase, i, n0, halves, buf, use, xhi, xlo, rows=False, after=None):
                acc_free(pe, phase, i, buf, use)
                for n in range(halves):
                    use_half(pe, phase, i, n0 + n, buf, n == 0, n == halves - 1, HALF_K * n, xhi, xlo, rows)
                    if after and n in after:
                        after[n]()

            def sum_squares(n):
                for k in range(2):
                    last = mm(psf[0][:, 0:SEQ], ones[:], sqsum[:, k], start=(k == 0), stop=(k == 1))
                last.then_inc(sq_summed, 1)

            def beta_a():
                pe.wait_ge(wba_scaled, 1)
                for k in range(KD):
                    last = mm(psf[1][0:48, 0:SEQ], wba_sb[:, k], xT[:, k], start=(k == 0), stop=(k == KD - 1))
                last.then_inc(ba_out, 1)
                pe.wait_ge(r_done, 1)
                for m in range(TILES):
                    last = mm(psf[0][:, COLS + m:COLS + m + 1], R[0:1, m * P:(m + 1) * P], ones[0:1, 0:1], start=True, stop=True)
                last.then_inc(rcol_out, 1)

            def tok_columns():
                pe.wait_ge(ba_act, 5)
                pe.wait_ge(ba_dve, 7)
                pe.wait_ge(rcol_done, 1)
                for m in range(TILES):
                    last = nc.tensor.transpose(psf[1][:, m * 80:m * 80 + 80], bg[:, m * P:(m + 1) * P], ident[0:80, 0:80])
                last.then_inc(tok_T, 1)

            def first_sum():
                pe.wait_ge(sq_added, 8)
                sum_squares(0)

            pe.wait_ge(consts_made, 6)
            def x_part(c):
                return lambda: pe.wait_ge(x0_lo, c + 1)
            x_part(0)()
            def tok_tile(ap, h, m):
                return ap[:, h, m * P:(m + 1) * P]

            def columns(src, n, signal):
                for h in range(GROUP):
                    for m in range(TILES):
                        c = 8 * n + 2 * h + m
                        last = mm(psf[0][:, c:c + 1], tok_tile(src, h, m), ones[:, 0:1], start=True, stop=True)
                last.then_inc(signal, 1)

            def rows(src, signal):
                for b in range(2):
                    last = mm(ps[0][:, b], ones[:], piece(src, b).rearrange("p h n -> p (h n)"), start=True, stop=True)
                last.then_inc(signal, 1)

            def k_columns(g):
                pe.wait_ge(qk_sq, 2 * g + 1)
                columns(t[1], 1, qk_len)

            def k_rows(g):
                pe.wait_ge(k_diag_done, g + 1)
                rows(t[1], k_rows_out)

            def q_columns(g):
                pe.wait_ge(qk_sq, 2 * g + 2)
                pe.wait_ge(negm_done, g + 1)
                columns(t[0], 0, qk_len)

            def grams(g):
                pe.wait_ge(ps_free, g + 1)
                pe.wait_ge(sel_done, g + 1)
                for h in range(GROUP):
                    last = mm(psv[1][:, h], selg[32:48, h:h + 1].to_broadcast([16, P]), bg[32:48, :], start=True, stop=True)
                last.then_inc(g_out, 1)
                pe.wait_ge(k_normed, g + 1)
                for m in range(TILES):
                    for h in range(GROUP):
                        last = mm(psq[0][:, 4 * m + h], tok_tile(kn, h, m), tok_tile(kn, h, m), start=True, stop=True)
                last.then_inc(gram_m_out, 1)

            def transpose_k(g):
                pe.wait_ge(diff_done, 2 * g + 2)
                for m in range(TILES):
                    for h in range(GROUP):
                        last = nc.tensor.transpose(psq[1][:, 4 * m + h], tok_tile(kn, h, m), ident[:])
                last.then_inc(kT_out, 1)

            def gram_q(g):
                pe.wait_ge(conv_silu, 2 * g + 2)
                pe.wait_ge(k_scaled, 2 * g + 2)
                for m in range(TILES):
                    for h in range(GROUP):
                        last = mm(psq[1][:, 4 * m + h], tok_tile(kn, h, m), tok_tile(conv[0], h, m), start=True, stop=True)
                last.then_inc(gram_q_out, 1)

            def q_gram_columns(g):
                gram_q(g)
                q_columns(g)

            def transpose_v(d):
                pe.wait_ge(convv_silu, d + 1)
                pe.wait_ge(qkT_done, d + 1)
                for m in range(TILES):
                    for h in range(GROUP):
                        last = nc.tensor.transpose(psq[1][:, 4 * m + h], tok_tile(conv[2], h, m), ident[:])
                last.then_inc(vT_out, 1)

            PAIRS = ((0, 32), (64, 96))

            def merge32_a(d):
                pe.wait_ge(diagT_in, 16 * (d + 1))
                pe.wait_ge(qk_mean, 2 * d + 2)
                carry_wait(pe)
                for a, (top, low) in enumerate(PAIRS):
                    for x in range(8):
                        last = mm(ps[0][top:top + 32, a, 32 * x:32 * x + 32], negm[low:low + 32, x, top:top + 32],
                                  diagT[low:low + 32, x], start=True, stop=True)
                for a, bank in ((0, 1), (1, 1), (2, 0)):
                    part = slice(32 * a, 32 * a + 32)
                    for x in range(8):
                        last = mm(ps[0][part, bank, 256 + 32 * x:288 + 32 * x], diagT[part, x], ident[part, part], start=True, stop=True)
                last.then_inc(merge_out, 1)

            def merge32_b(d):
                pe.wait_ge(merge_act, 6 * d + 5)
                pe.wait_ge(v_scaled, 2 * d + 2)
                carry_wait(pe)
                for a, (top, low) in enumerate(PAIRS):
                    for x in range(8):
                        last = mm(ps[1][top:top + 32, a, 32 * x:32 * x + 32], inv[top:top + 32, x, top:top + 32],
                                  p32[top:top + 32, x], start=True, stop=True)
                for x in range(8):
                    last = mm(ps[1][32:64, 0, 256 + 32 * x:288 + 32 * x], p32[0:32, x], inv[0:32, x, 0:32], start=True, stop=True)
                last.then_inc(merge_out, 1)

            def merge64_a(d):
                pe.wait_ge(invT_placed, 4 * d + 4)
                pe.wait_ge(merge_dve, 4 * d + 2)
                pe.wait_ge(merge_act, 6 * d + 6)
                carry_wait(pe)
                for x in range(8):
                    last = mm(ps[0][0:64, 0, 64 * x:64 * x + 64], negm[64:128, x, 0:64], invT[64:128, x, 64:128], start=True, stop=True)
                last.then_inc(merge_out, 1)

            def merge64_b(d):
                pe.wait_ge(merge_dve, 4 * d + 3)
                carry_wait(pe)
                for x in range(8):
                    last = mm(ps[0][0:64, 1, 64 * x:64 * x + 64], inv[0:64, x, 0:64], p64[:, x], start=True, stop=True)
                last.then_inc(merge_out, 1)

            def first_tile(d):
                pe.wait_ge(merge_dve, 4 * d + 4)
                for h in range(GROUP):
                    last = mm(psq[1][:, h], invT[:, h], vbeta[:, h], start=True, stop=True)
                last.then_inc(delta_out, 1)
                for h in range(GROUP):
                    last = mm(psq[1][:, 4 + h], kbeg[:, h], invT[:, 4 + h], start=True, stop=True)
                last.then_inc(delta_out, 1)

            def carry(d):
                pe.wait_ge(delta_act, 3 * d + 1)
                for h in range(GROUP):
                    last = mm(psq[0][:, h], ktail[:, h], vnew[:, h], start=True, stop=True)
                last.then_inc(delta_out, 1)

            def second_tile(d):
                pe.wait_ge(delta_dve, 2 * d + 2)
                for h in range(GROUP):
                    mm(psq[0][:, 4 + h], invT[:, 4 + h], vbeta[:, 4 + h], start=True, stop=False)
                    last = mm(psq[0][:, 4 + h], nwT[:, h], state[:, h], start=False, stop=True)
                last.then_inc(delta_out, 1)

            def outputs(d):
                pe.wait_ge(delta_act, 3 * d + 2)
                pe.wait_ge(qdec_done, d + 1)
                for h in range(GROUP):
                    mm(psv[1][:, h, 0:P], vnew[:, h], qkT[:, h], start=True, stop=True)
                    mm(psv[1][:, h, P:SEQ], vnew[:, 4 + h], qkT[:, 4 + h], start=True, stop=False)
                    last = mm(psv[1][:, h, P:SEQ], state[:, h], qdec[:, h], start=False, stop=True)
                last.then_inc(delta_out, 1)

            def o_columns(d, g=None):
                pe.wait_ge(delta_act, 3 * d + 3)
                if g is not None:
                    pe.wait_ge(k_normed, g + 1)
                columns(t[2], 2, o_len)

            def o_row(d):
                pe.wait_ge(o_diag, d + 1)
                rows(t[2], o_rows)

            FINISH = {3: transpose_v, 5: merge32_a, 6: merge32_b, 7: merge64_a, 8: merge64_b, 9: first_tile, 10: carry,
                      11: second_tile, 12: outputs}
            START = {15: grams, 18: transpose_k, 22: q_gram_columns}

            def stages(d, g, n0):
                steps = {}

                def put(n, f, *a):
                    if n0 <= n < n0 + HID:
                        steps.setdefault(n - n0, []).append(lambda: f(*a))
                if d is not None:
                    for n, f in FINISH.items():
                        put(n, f, d)
                    put(13, o_columns, d, g)
                    put(14, o_row, d)
                if g is not None:
                    put(11, k_columns, g)
                    put(12, k_rows, g)
                    for n, f in START.items():
                        put(n, f, g)
                return steps

            def group(g, d, extra=({}, {}), last=({}, {})):
                for p, buf, use in ((0, 0, 0), (1, 1, 0), (2, 0, 1)):
                    after = {n: (lambda fs: lambda: [f() for f in fs])(fs) for n, fs in stages(d, g, p * HID).items()}
                    if p < 2:
                        after.update(extra[p])
                        for n, f in last[p].items():
                            after[n] = (lambda a, b: lambda: (a(), b()))(after[n], f) if n in after else f
                    gemm("qkv", g, p * HID, HID, buf, use, ahi, alo, after=after)

            group(0, None, extra=({1: x_part(1), 3: x_part(2), 5: lambda: (x_part(3)(), first_sum()), 6: beta_a},
                                  {}), last=({}, {4: tok_columns}))
            with pe.Fori(1, NGROUPS) as g:
                group(g, g - 1)

            def spatial():
                pe.wait_ge(v_normed, TILES)
                pe.wait_ge(gm_masked, 1)
                pe.wait_ge(ps_free, NGROUPS + 1)
                for x in range(GMT):
                    for m in range(TILES):
                        last = mm(psv[x // 4][:, x % 4, m * P:(m + 1) * P], vg[:, m, x * P:(x + 1) * P], gmw[:, x], start=True, stop=True)
                last.then_inc(sv_out, 1)

            for p, buf in ((0, 0), (1, 1)):
                last_steps = {n: (lambda fs: lambda: [f() for f in fs])(fs) for n, fs in stages(NGROUPS - 1, None, p * HID).items()}
                gemm("uv", 0, p * HID, HID, buf, 0, ahi, alo, rows=True, after=last_steps)
            gemm("uv", 0, 2 * HID, HID, 0, 1, ahi, alo)
            gemm("uv", 0, 3 * HID, HID, 1, 1, ahi, alo, after={4: spatial})

            with pe.Fori(0, 2) as i:
                for b in range(2):
                    gemm("z", i, b * HID, HID, b, 0, ahi, alo)
            with pe.Fori(0, NB) as i:
                gemm("mix", i, 0, HID, 0, 0, ahi, alo)
                gemm("mix", i, HID, HID, 1, 0, ahi, alo)
                pe.wait_ge(ya_lo, 2)
                gemm("mix", i, 2 * HID, HGM, 0, 1, yahi, yalo)
                pe.wait_ge(yb_lo, 8)
                gemm("mix", i, 2 * HID + HGM, HID, 1, 1, ybhi, yblo)

            def operand_ready(done, last):
                return lambda: pe.wait_ge(done, last)

            pe.wait_ge(mix_lo, 6)
            gemm("out", 0, 0, HID, 0, 0, mhi, mlo, after={5: operand_ready(mix_lo, 8)})
            gemm("out", 0, HID, HID, 1, 0, mhi, mlo)
            with pe.Fori(1, 2) as i:
                for b in range(2):
                    gemm("out", i, b * HID, HID, b, 0, mhi, mlo)

            def next_sum(n):
                def f():
                    pe.wait_ge(res[n]["added"], 9)
                    sum_squares(n + 1)
                return f

            pe.wait_ge(res[0]["lo"], 6)
            gemm("ffn", 0, 0, HID, 0, 0, ahi, alo, after={4: next_sum(0), 5: operand_ready(res[0]["lo"], 8)})
            gemm("ffn", 0, HID, HID, 1, 0, ahi, alo)
            with pe.Fori(1, FB) as i:
                for b in range(2):
                    gemm("ffn", i, b * HID, HID, b, 0, ahi, alo)
            pe.wait_ge(ff_lo, 2 * FB - 2)
            gemm("down", 0, 0, HFF, 0, 0, fhi, flo, after={HFF - 3: operand_ready(ff_lo, 2 * FB)})
            gemm("down", 0, HFF, HFF, 1, 0, fhi, flo)
            with pe.Fori(1, 2) as i:
                for b in range(2):
                    gemm("down", i, b * HFF, HFF, b, 0, fhi, flo)
            pe.wait_ge(p_lo, 1)
            for b in range(NB):
                gemm("proj", 0, b, 1, b % 2, b // 2, phi, plo)
            pe.wait_ge(res[1]["lo"], 6)
            gemm("ple", 0, 0, HID, 0, 0, ahi, alo, after={4: next_sum(1), 5: operand_ready(res[1]["lo"], 8)})
            gemm("ple", 0, HID, HID, 1, 0, ahi, alo)
            for b in range(2):
                gemm("ple", 1, b * HID, HID, b, 0, ahi, alo)
            pe.wait_ge(sq_added, 14)
            for k in range(2):
                mm(psf[0][:, 0:SEQ], ones[:], sqsum[:, k], start=(k == 0), stop=False)
            for j in range(2):
                pe.wait_ge(ple_sq, 7 + j)
                for k in range(2):
                    last = mm(psf[0][:, 0:SEQ], ones[:], t[1][:, 2 * j + k], start=False, stop=(j == 1 and k == 1))
            last.then_inc(sq_summed, 1)

        @block.scalar
        def _(act):
            f = nc.scalar.activation

            def split(phase, i, a, b):
                for n in range(a, b):
                    split_hi(act, phase, i, n)

            def root(n):
                act.wait_ge(mean_inv, 2 * n + 2)
                f(R[:], Rt[:], ACT.Sqrt).then_inc(r_done, 1)

            def x_hi(c):
                act.wait_ge(x0_gain, c + 1)
                f(ahi[:, 4 * c:4 * c + 4], t[2 * (c % 2)][:], ACT.Copy).then_inc(x0_hi, 1)

            def x_square(q):
                act.wait_ge(x_in[q // 2], 16)
                if q >= 2:
                    act.wait_ge(sq_added, q - 1)
                f(piece(t[1], q % 2), xT[:, 2 * q:2 * q + 2], ACT.Square).then_inc(x0_sq, 1)

            for n in range(-LEAD, 0):
                split_hi(act, "qkv", 0, n)
                c = n + LEAD
                x_hi(n + LEAD)
            x_hi(3)
            x_square(0)
            x_square(1)

            def silu_qk(c, p, g):
                act.wait_ge(conv_done, 12 * g + 4 * (p + 1))
                f(conv[c][:], conv[c][:], ACT.Silu).then_inc(conv_silu, 1)
                act.wait_ge(conv_silu, 2 * g + p + 1)
                f(t[c][:], conv[c][:], ACT.Square).then_inc(qk_sq, 1)

            def silu_k(g):
                silu_qk(1, 0, g)

            def silu_q(g):
                silu_qk(0, 1, g)

            def k_root(d):
                act.wait_ge(k_inv, d + 1)
                f(length[:, 1], length[:, 1], ACT.Sqrt).then_inc(k_rooted, 1)

            def g_exp(d):
                act.wait_ge(g_out, d + 1)
                f(vnew[:, 4:8], psv[1][:, :, P:SEQ], ACT.Exp).then_inc(decay_done, 1)

            def decay_m(d):
                act.wait_ge(diff_done, 2 * d + 1)
                f(negm[:], negm[:], ACT.Exp, scale=-1.0).then_inc(decay_done, 1)

            def decay_q(d):
                act.wait_ge(diff_done, 2 * d + 2)
                f(qkT[:], qkT[:], ACT.Exp).then_inc(decay_done, 1)

            def silu_v(d):
                act.wait_ge(conv_done, 12 * d + 12)
                f(conv[2][:], conv[2][:], ACT.Silu).then_inc(convv_silu, 1)

            def copy_p32(d):
                act.wait_ge(merge_out, 4 * d + 1)
                for a, top in enumerate((0, 64)):
                    f(p32[top:top + 32], heads(ps[0][top:top + 32, a, 0:256], 32), ACT.Copy).then_inc(merge_act, 1)
                for a, bank in ((0, 1), (1, 1), (2, 0)):
                    part = slice(32 * a, 32 * a + 32)
                    f(inv[part, :, part], heads(ps[0][part, bank, 256:512], 32), ACT.Copy).then_inc(merge_act, 1)

            def copy_inv(d):
                act.wait_ge(merge_out, 4 * d + 2)
                f(inv[32:64, :, 0:32], heads(ps[1][32:64, 0, 256:512], 32), ACT.Copy).then_inc(merge_act, 1)

            def copy_v0(d):
                act.wait_ge(delta_out, 5 * d + 1)
                f(vnew[:, 0:4], psq[1][:, 0:4], ACT.Copy).then_inc(delta_act, 1)

            def copy_v1(d):
                act.wait_ge(delta_out, 5 * d + 4)
                f(vnew[:, 4:8], psq[0][:, 4:8], ACT.Copy).then_inc(delta_act, 1)

            def square_o(d):
                act.wait_ge(delta_out, 5 * d + 5)
                f(t[2][:], psv[1], ACT.Square).then_inc(delta_act, 1)

            def o_rt(d):
                act.wait_ge(o_mean, 2 * d + 2)
                f(length[:, 2], length[:, 2], ACT.Sqrt).then_inc(o_root, 1)

            def store_m(g):
                act.wait_ge(negm_done, g + 1)
                carry_wait(act)
                for a in range(4):
                    act.dma_start(scratch_m[:, a].rearrange("x i j -> i x j"),
                                  negm[32 * a:32 * a + 32, :, 32 * a:32 * a + 32]).then_inc(m_stored, 16)

            FINISH = {2: (silu_v,), 6: (copy_p32,), 7: (copy_inv,), 10: (copy_v0,), 12: (copy_v1,),
                      13: (square_o,), 14: (o_rt,)}
            START = {10: (silu_k,), 12: (k_root,), 16: (g_exp, decay_m, decay_q), 17: (store_m,), 21: (silu_q,)}

            def beta_g():
                act.wait_ge(ba_dve, 1)
                f(bg[0:16, :], g1[0:16, :], ACT.Sigmoid).then_inc(ba_act, 1)
                f(hv[32:48, 2:3], hv[32:48, 1:2], ACT.Exp).then_inc(ba_act, 1)
                act.wait_ge(ba_dve, 3)
                f(g2[32:48, :], g2[32:48, :], ACT.Exp, scale=-1.0).then_inc(ba_act, 1)
                act.wait_ge(ba_act, 3)
                f(g2[32:48, :], g2[32:48, :], ACT.Ln, bias=1.0).then_inc(ba_act, 1)

            def tails():
                act.wait_ge(ba_dve, 7)
                f(bg[64:80, 0:P], bg[32:48, 0:P], ACT.Exp, bias=bg[32:48, P - 1:P], scale=-1.0).then_inc(ba_act, 1)

            def tok_exp():
                act.wait_ge(tok_done, 2)
                f(tok[:, 3], tok[:, 1], ACT.Exp).then_inc(tok_eg, 1)

            for n in range(3 * HID):
                split_hi(act, "qkv", 0, n)
                if n < 3:
                    x_square(2 * n + 2)
                    x_square(2 * n + 3)
                if n == 6:
                    root(0)
                if n == 8:
                    beta_g()
                if n == 11:
                    tails()
                if n == 14:
                    tok_exp()
                for stage in START.get(n, ()):
                    stage(0)
            with act.Fori(1, NGROUPS) as g:
                for n in range(3 * HID):
                    split_hi(act, "qkv", g, n)
                    for stage in FINISH.get(n, ()):
                        stage(g - 1)
                    for stage in START.get(n, ()):
                        stage(g)

            def v_block(b):
                acc_full(act, "uv", 0, HID * (b + 1))
                if b == 0:
                    act.wait_ge(qdec_done, NGROUPS)
                    act.wait_ge(gram_q_out, NGROUPS)
                for m in range(TILES):
                    x = f(vg[:, m, COLS * b:COLS * (b + 1)], acc[b][:, m], ACT.Gelu, scale=rcol[:, m:m + 1])
                    x.then_inc(v_gelu, 1)
                    if m == TILES - 1:
                        act.wait_ge(v_gelu, 4 * b + 3)
                        act.sem_inc(acc_read[b], 1)
                    else:
                        act.wait_ge(v_gelu, 4 * b + 2 * m + 1)
                    f(t[2][:, 0:2].rearrange("p a n -> p (a n)"), vg[:, m, COLS * b:COLS * (b + 1)], ACT.Square,
                      accum_out=vsum[:, b, m:m + 1]).then_inc(v_gelu, 1)
                    act.wait_ge(v_gelu, 4 * b + 2 * m + 2)

            def u_block(b):
                act.wait_ge(ps_free, NGROUPS + 1)
                for j in range(2):
                    act.wait_ge(u_scaled, 2 * b + j + 1)
                    f(uT[:, 4 * b + 2 * j:4 * b + 2 * j + 2], piece(t[0], j), ACT.Gelu).then_inc(u_gelu, 1)

            for n in range(4 * HID):
                split_hi(act, "uv", 0, n)
                for stage in FINISH.get(n, ()):
                    stage(NGROUPS - 1)
                if n in (7, 15):
                    v_block(n // 8)
                if n == 18:
                    act.wait_ge(v_mean, 3)
                    f(vrms[:], vrms[:], ACT.Sqrt).then_inc(v_root, 1)
                if n in (23, 31):
                    u_block(n // 8 - 2)
            for j in range(2):
                act.wait_ge(ya_dve, j + 1)
                f(yahi[:, 4 * j:4 * j + 4], ytmp[:, 4 * j:4 * j + 4], ACT.Copy).then_inc(ya_hi, 1)
            act.wait_ge(p_in, 16)
            f(phi[:], praw[:], ACT.Copy).then_inc(p_hi, 1)

            with act.Fori(0, 2) as i:
                for b in range(2):
                    split("z", i, b * HID, (b + 1) * HID)
                    for j in range(2):
                        act.wait_ge(z_scaled, 4 * i + 2 * b + j + 1)
                        f(piece(t[0], j), piece(t[0], j), ACT.Silu).then_inc(z_silu, 1)
                    for j in range(2):
                        act.wait_ge(z_gated, 4 * i + 2 * b + j + 1)
                        f(tiles(ybhi, 2 * i + b, j), piece(t[1], j), ACT.Copy).then_inc(yb_hi, 1)
            with act.Fori(0, NB) as i:
                for b in range(2):
                    split("mix", i, b * HID, (b + 1) * HID)
                    for j in range(2):
                        act.wait_ge(gate_scaled, 4 * i + 2 * b + j + 1)
                        f(piece(t[b], j), piece(t[b], j), ACT.Sigmoid).then_inc(gate_sig, 1)
                split("mix", i, 2 * HID, PER["mix"])
                for j in range(2):
                    act.wait_ge(mix_prod, 6 * i + 5 + j)
                    f(tiles(mhi, i, j), piece(t[2], j), ACT.Copy).then_inc(mix_hi, 1)

            def residual(n, phase, halves):
                s = res[n]
                with act.Fori(0, 2) as i:
                    for b in range(2):
                        split(phase, i, b * halves, (b + 1) * halves)
                        for j in range(2):
                            q = 4 * i + 2 * b + j
                            act.wait_ge(s["x"], q + 1)
                            act.wait_ge(s["added"], 1 + 4 * i + (0, 0, 1, 2)[2 * b + j])
                            f(piece(t[1], j), tiles(xT, 2 * i + b, j), ACT.Square).then_inc(s["sq"], 1)
                        for j in range(2):
                            act.wait_ge(s["gain"], 4 * i + 2 * b + j + 1)
                            f(tiles(ahi, 2 * i + b, j), piece(t[0], j), ACT.Copy).then_inc(s["hi"], 1)

            residual(0, "out", HID)

            def ffn(i, first=False):
                if first:
                    split("ffn", i, 0, 5)
                    root(1)
                split("ffn", i, 5 if first else 0, HID)
                for j in range(2):
                    act.wait_ge(ff_scaled, 2 * i + j + 1)
                    f(piece(t[0], j), piece(t[0], j), ACT.Silu).then_inc(ff_silu, 1)
                split("ffn", i, HID, 2 * HID)
                for j in range(2):
                    act.wait_ge(ff_prod, 2 * i + j + 1)
                    f(tiles(fhi, i, j), piece(t[2], j), ACT.Copy).then_inc(ff_hi, 1)

            ffn(0, first=True)
            with act.Fori(1, FB) as i:
                ffn(i)
            residual(1, "down", HFF)
            split("proj", 0, 0, NB)
            for i in range(2):
                for b in range(2):
                    if i == 0 and b == 0:
                        split("ple", 0, 0, 5)
                        root(2)
                        split("ple", 0, 5, HID)
                    else:
                        split("ple", i, b * HID, (b + 1) * HID)
                    for j in range(2):
                        act.wait_ge(ple_scaled, 4 * i + 2 * b + j + 1)
                        f(piece(t[0], j), piece(t[0], j), ACT.Sigmoid).then_inc(ple_sig, 1)
                    for j in range(2):
                        q = 4 * i + 2 * b + j
                        act.wait_ge(ple_x, q + 1)
                        if q >= 2:
                            act.wait_ge(sq_added, 8 + q - 1)
                        f(piece(t[1], j), tiles(xT, 2 * i + b, j), ACT.Square).then_inc(ple_sq, 1)
            root(3)

        @block.vector
        def _(dve):
            v = nc.vector

            def split(phase, i, a, b):
                for n in range(a, b):
                    split_lo(dve, phase, i, n)

            def mean(n):
                dve.wait_ge(sq_summed, n + 1)
                v.tensor_scalar(Rt[:], psf[0][:, 0:SEQ], 1.0 / D, EPS, ALU.mult, ALU.add).then_inc(mean_inv, 1)
                dve.wait_ge(mean_inv, 2 * n + 1)
                v.reciprocal(Rt[:], Rt[:]).then_inc(mean_inv, 1)

            def x_gain(c):
                dve.wait_ge(x_in[c], 16)
                if c >= 2:
                    dve.wait_ge(x0_lo, c - 1)
                v.tensor_tensor(t[2 * (c % 2)][:], xT[:, 4 * c:4 * c + 4], bc(cols[:, C_MIX + 4 * c:C_MIX + 4 * c + 4], SEQ),
                                ALU.mult).then_inc(x0_gain, 1)

            def x_lo(c):
                dve.wait_ge(x0_hi, c + 1)
                v.tensor_tensor(alo[:, 4 * c:4 * c + 4], t[2 * (c % 2)][:], ahi[:, 4 * c:4 * c + 4].bitcast(F32),
                                ALU.subtract).then_inc(x0_lo, 1)

            dve.wait_ge(cols_in, 16)
            for n in range(-LEAD, 0):
                c = n + LEAD
                x_gain(c)
                split_lo(dve, "qkv", 0, n)
                x_lo(c)
            x_gain(3)
            x_lo(3)

            def evac(p, g):
                acc_full(dve, "qkv", g, (p + 1) * HID)
                if not (isinstance(g, int) and g == 0 and p == 0):
                    dve.wait_ge(conv_done, 12 * g + 4 * p)
                buf = p % 2
                v.tensor_tensor(pre[:, :, 4:], accv[buf], over(R[:], 4), ALU.mult).then_inc(pre_done, 1)
                dve.wait_ge(pre_done, 3 * g + p + 1)
                dve.sem_inc(acc_read[buf], 1)

            def convolve(c, p, g, pair):
                for tap in range(4):
                    for n in range(2):
                        h = 2 * pair + n
                        y = conv[c][:, h]
                        w = cols[:, ds(C_CONV + tap * 48 + c * HEADS + GROUP * g + h, 1)]
                        src = pre[:, h, 1 + tap:1 + tap + SEQ]
                        if tap == 0:
                            ins = v.tensor_scalar(y, src, w, None, ALU.mult)
                        else:
                            dve.wait_ge(conv_mac, 36 * g + 12 * p + 6 * pair + 2 * (tap - 1) + n + 1)
                            ins = v.scalar_tensor_tensor(y, src, w, y, ALU.mult, ALU.add)
                        ins.then_inc(conv_done if tap == 3 else conv_mac, 1)

            def conv_a(c, p):
                return lambda g: convolve(c, p, g, 0)

            def conv_b(c, p):
                return lambda g: convolve(c, p, g, 1)

            def k_mean(g):
                dve.wait_ge(qk_len, 2 * g + 1)
                x = length[:, 1]
                v.tensor_scalar(x, psf[0][:, 8:16], EPS, None, ALU.add).then_inc(qk_mean, 1)
                dve.wait_ge(qk_mean, 2 * g + 1)
                v.reciprocal(x, x).then_inc(k_inv, 1)

            def q_mean(g):
                dve.wait_ge(qk_len, 2 * g + 2)
                v.tensor_scalar(length[:, 0], psf[0][:, 0:8], EPS, P * EPS, ALU.add, ALU.mult).then_inc(qk_mean, 1)

            def diagonal(c, signal):
                v.tensor_tensor(t[c][:].rearrange("p h (m n) -> p (h m) n", n=P), over(ident[:], 8), bc(length[:, c], P),
                                ALU.mult).then_inc(signal, 1)

            def k_diag(g):
                dve.wait_ge(k_rooted, g + 1)
                diagonal(1, k_diag_done)

            def norm_k(g):
                dve.wait_ge(k_rows_out, g + 1)
                v.tensor_tensor(kn[:], psv[0], conv[1][:], ALU.mult).then_inc(k_normed, 1)

            def decay_q(g):
                dve.wait_ge(conv_silu, 2 * g + 2)
                v.tensor_tensor(qdec[:], conv[0][:, :, P:SEQ], vnew[:, 4:8, :], ALU.mult).then_inc(qdec_done, 1)

            def token(k, m, h, d):
                return tok[:, k, m, ds(GROUP * d + h, 1)]

            def tokens(k, m, d):
                return bc(tok[:, k, m, ds(GROUP * d, GROUP)], P)

            def diff_m(d):
                dve.wait_ge(decay_done, 3 * d + 1)
                for m in range(TILES):
                    for h in range(GROUP):
                        x = v.scalar_tensor_tensor(negm[:, 4 * m + h], psv[1][:, h, m * P:(m + 1) * P], token(1, m, h, d), mask_m[:],
                                                   ALU.subtract, ALU.max)
                x.then_inc(diff_done, 1)

            def diff_q(d):
                for m in range(TILES):
                    for h in range(GROUP):
                        x = v.scalar_tensor_tensor(qkT[:, 4 * m + h], psv[1][:, h, m * P:(m + 1) * P], token(1, m, h, d), mask_q[:],
                                                   ALU.subtract, ALU.min)
                x.then_inc(diff_done, 1)

            def make_negm(d):
                dve.wait_ge(gram_m_out, d + 1)
                dve.wait_ge(decay_done, 3 * d + 2)
                for m in range(TILES):
                    for h in range(GROUP):
                        x = v.scalar_tensor_tensor(negm[:, 4 * m + h], psq[0][:, 4 * m + h], token(4, m, h, d), negm[:, 4 * m + h],
                                                   ALU.mult, ALU.mult)
                x.then_inc(negm_done, 1)

            def scale_v(d):
                dve.wait_ge(vT_out, d + 1)
                for m in range(TILES):
                    v.tensor_tensor(vbeta[:, 4 * m:4 * m + 4], psq[1][:, 4 * m:4 * m + 4], tokens(0, m, d), ALU.mult).then_inc(v_scaled, 1)

            def scale_k(d):
                dve.wait_ge(kT_out, d + 1)
                v.tensor_tensor(ktail[:], psq[1][:, 0:4], tokens(2, 0, d), ALU.mult).then_inc(k_scaled, 1)
                v.tensor_tensor(kbeg[:], psq[1][:, 4:8], tokens(3, 1, d), ALU.mult).then_inc(k_scaled, 1)

            def make_qkT(d):
                dve.wait_ge(gram_q_out, d + 1)
                dve.wait_ge(decay_done, 3 * d + 3)
                v.tensor_tensor(qkT[:], psq[1], qkT[:], ALU.mult).then_inc(qkT_done, 1)

            def copy_invT32(d):
                dve.wait_ge(merge_out, 4 * d + 2)
                for a, (top, low) in enumerate(((0, 32), (64, 96))):
                    v.tensor_copy(invT[top:top + 32, :, low:low + 32], heads(ps[1][top:top + 32, a, 0:256], 32)).then_inc(merge_dve, 1)

            def copy_p64(d):
                dve.wait_ge(merge_out, 4 * d + 3)
                v.tensor_copy(p64[:], heads(ps[0][0:64, 0], 64)).then_inc(merge_dve, 1)

            def copy_invT64(d):
                dve.wait_ge(merge_out, 4 * d + 4)
                v.tensor_copy(invT[0:64, :, 64:128], heads(ps[0][0:64, 1], 64)).then_inc(merge_dve, 1)

            def copy_nwT(d):
                dve.wait_ge(delta_out, 5 * d + 2)
                v.tensor_scalar(nwT[:], psq[1][:, 4:8], -1.0, None, ALU.mult).then_inc(delta_dve, 1)

            def copy_state(d):
                dve.wait_ge(delta_out, 5 * d + 3)
                v.tensor_copy(state[:], psq[0][:, 0:4]).then_inc(delta_dve, 1)

            def o_inv(d):
                dve.wait_ge(o_len, d + 1)
                v.scalar_tensor_tensor(length[:, 2], psf[0][:, 16:24], 1.0 / P, length[:, 0], ALU.mult, ALU.add).then_inc(o_mean, 1)
                dve.wait_ge(o_mean, 2 * d + 1)
                v.reciprocal(length[:, 2], length[:, 2]).then_inc(o_mean, 1)
                dve.wait_ge(delta_act, 3 * d + 3)
                v.tensor_scalar(oT[:, ds(GROUP * d, GROUP)], psv[1], cols[:, C_DNO:C_DNO + 1], None, ALU.mult).then_inc(o_gained, 1)

            def o_diagonal(d):
                dve.wait_ge(o_root, d + 1)
                diagonal(2, o_diag)

            def norm_o(d):
                dve.wait_ge(o_gained, d + 1)
                dve.wait_ge(o_rows, d + 1)
                o = oT[:, ds(GROUP * d, GROUP)]
                v.tensor_tensor(o, o, psv[0], ALU.mult).then_inc(ps_free, 1)

            def select_heads(g):
                v.tensor_copy(selg[32:48, :], ident[32:48, ds(32 + GROUP * g, GROUP)]).then_inc(sel_done, 1)

            FINISH = {0: (make_qkT, conv_a(2, 2)), 1: (conv_b(2, 2),), 4: (scale_v,), 7: (copy_invT32,), 8: (copy_p64,),
                      9: (copy_invT64,), 10: (copy_nwT,), 11: (copy_state,), 14: (o_inv, o_diagonal), 15: (norm_o,)}
            START = {11: (select_heads,), 12: (k_mean, k_diag), 13: (norm_k,), 16: (diff_m, diff_q, make_negm),
                     18: (conv_a(0, 1),), 19: (conv_b(0, 1),), 20: (scale_k,), 21: (decay_q,), 23: (q_mean,)}
            CONV_K = {8: conv_a(1, 0), 9: conv_b(1, 0)}

            def steps(n, d, g):
                if g is not None:
                    for stage in START.get(n, ()):
                        stage(g)
                if d is not None:
                    for stage in FINISH.get(n, ()):
                        stage(d)
                if g is not None and n in CONV_K:
                    CONV_K[n](g)

            def beta_a():
                dve.wait_ge(ba_out, 1)
                v.tensor_tensor(g1[:], psf[1][0:48, 0:SEQ], R[0:48, :], ALU.mult).then_inc(ba_dve, 1)
                dve.wait_ge(ba_dve, 1)
                v.tensor_scalar(g1[32:48, :], g1[32:48, :], hv[32:48, 0:1], None, ALU.add).then_inc(ba_dve, 1)
                dve.wait_ge(ba_dve, 2)
                v.scalar_tensor_tensor(g2[32:48, :], g1[32:48, :], -1.0, g1[32:48, :], ALU.mult, ALU.max).then_inc(ba_dve, 1)
                dve.wait_ge(rcol_out, 1)
                v.tensor_copy(rcol[:], psf[0][:, COLS:COLS + TILES]).then_inc(rcol_done, 1)

            def sum_g():
                dve.wait_ge(ba_act, 4)
                v.scalar_tensor_tensor(g1[32:48, :], g1[32:48, :], 0.0, g2[32:48, :], ALU.max, ALU.add).then_inc(ba_dve, 1)
                dve.wait_ge(ba_dve, 4)
                v.tensor_scalar(g2[32:48, :], g1[32:48, :], hv[32:48, 2:3], -1.0, ALU.mult, ALU.mult).then_inc(ba_dve, 1)
                dve.wait_ge(ba_dve, 5)
                for m in range(TILES):
                    v.tensor_tensor_scan(bg[32:48, m * P:(m + 1) * P], ones[32:48, :], g2[32:48, m * P:(m + 1) * P], 0.0,
                                         ALU.mult, ALU.add).then_inc(ba_dve, 1)

            def tok_copy():
                dve.wait_ge(tok_T, 1)
                src = psf[1][:, 0:160].rearrange("p (m c) -> p m c", m=TILES)
                for k in (1, 0, 2):
                    v.tensor_copy(tok[:, k], src[:, :, 32 * k:32 * k + 16]).then_inc(tok_done, 1)
                dve.wait_ge(tok_done, 3)
                v.tensor_scalar(tok[:, 4], tok[:, 0], -1.0, None, ALU.mult).then_inc(tok_done, 1)
                dve.wait_ge(tok_eg, 1)
                v.tensor_tensor(tok[:, 3], tok[:, 3], tok[:, 0], ALU.mult).then_inc(tok_done, 1)
                dve.wait_ge(tok_done, 5)
                dve.sem_inc(ps_free, 1)

            for n in range(3 * HID):
                split_lo(dve, "qkv", 0, n)
                if n == 6:
                    mean(0)
                if n == 7:
                    beta_a()
                if n == 9:
                    sum_g()
                if n == 14:
                    tok_copy()
                steps(n, None, 0)
                if n in (7, 15, 23):
                    evac(n // 8, 0)
            with dve.Fori(1, NGROUPS) as g:
                for n in range(3 * HID):
                    split_lo(dve, "qkv", g, n)
                    steps(n, g - 1, g)
                    if n in (7, 15, 23):
                        evac(n // 8, g)

            def v_norm():
                dve.wait_ge(v_gelu, 8)
                v.tensor_tensor(vrms[:], vsum[:, 0], vsum[:, 1], ALU.add).then_inc(v_mean, 1)
                dve.wait_ge(v_mean, 1)
                v.tensor_scalar(vrms[:], vrms[:], 1.0 / GM, EPS, ALU.mult, ALU.add).then_inc(v_mean, 1)
                dve.wait_ge(v_mean, 2)
                v.reciprocal(vrms[:], vrms[:]).then_inc(v_mean, 1)

            def v_scale():
                dve.wait_ge(v_root, 1)
                for m in range(TILES):
                    v.tensor_scalar(vg[:, m], vg[:, m], vrms[:, m:m + 1], None, ALU.mult).then_inc(v_normed, 1)

            def u_block(b):
                acc_full(dve, "uv", 0, (b + 3) * HID)
                for j in range(2):
                    if b:
                        dve.wait_ge(u_gelu, j + 1)
                    v.tensor_tensor(piece(t[0], j), piece(accv[b], j), over(R[:], 2), ALU.mult).then_inc(u_scaled, 1)
                dve.wait_ge(u_scaled, 2 * b + 2)
                dve.sem_inc(acc_read[b], 1)

            def sv_bias():
                dve.wait_ge(sv_out, 1)
                for x in range(GMT):
                    ins = v.scalar_tensor_tensor(ytmp[:, x].rearrange("p (m t) -> p m t", m=TILES),
                                                 psv[x // 4][:, x % 4].rearrange("p (m t) -> p m t", m=TILES), cols[:, C_GMV + x:C_GMV + x + 1],
                                                 over(gmb[:, x], TILES), ALU.mult, ALU.add)
                ins.then_inc(sv_biased, 1)

            for n in range(4 * HID):
                split_lo(dve, "uv", 0, n)
                steps(n, NGROUPS - 1, None)
                if n == 16:
                    v_norm()
                if n == 19:
                    v_scale()
                if n == 23:
                    u_block(0)
                if n == 29:
                    sv_bias()
            u_block(1)
            dve.wait_ge(sv_biased, 1)
            for j in range(2):
                dve.wait_ge(u_gelu, 2 * j + 2)
                v.tensor_tensor(ytmp[:, 4 * j:4 * j + 4], ytmp[:, 4 * j:4 * j + 4], uT[:, 4 * j:4 * j + 4], ALU.mult).then_inc(ya_dve, 1)
            for j in range(2):
                dve.wait_ge(ya_hi, j + 1)
                v.tensor_tensor(yalo[:, 4 * j:4 * j + 4], ytmp[:, 4 * j:4 * j + 4], yahi[:, 4 * j:4 * j + 4].bitcast(F32), ALU.subtract).then_inc(ya_lo, 1)
            dve.wait_ge(p_hi, 1)
            v.tensor_tensor(plo[:], praw[:], phi[:].bitcast(F32), ALU.subtract).then_inc(p_lo, 1)

            def times_row(phase, i, end, buf, dst, signal, value):
                acc_full(dve, phase, i, end)
                for j in range(2):
                    x = v.tensor_tensor(piece(dst, j), piece(accv[buf], j), over(R[:], 2), ALU.mult)
                    x.then_inc(signal, 1)
                dve.wait_ge(signal, value + 2)
                dve.sem_inc(acc_read[buf], 1)

            def take_lo(hi, lo, src, blk, done, signal, value):
                for j in range(2):
                    dve.wait_ge(done, value + j + 1)
                    v.tensor_tensor(tiles(lo, blk, j), piece(src, j), tiles(hi, blk, j).bitcast(F32), ALU.subtract).then_inc(signal, 1)

            with dve.Fori(0, 2) as i:
                for b in range(2):
                    split("z", i, b * HID, (b + 1) * HID)
                    times_row("z", i, (b + 1) * HID, b, t[0], z_scaled, 4 * i + 2 * b)
                    for j in range(2):
                        dve.wait_ge(z_silu, 4 * i + 2 * b + j + 1)
                        v.tensor_tensor(piece(t[1], j), tiles(oT, 2 * i + b, j), piece(t[0], j), ALU.mult).then_inc(z_gated, 1)
                    take_lo(ybhi, yblo, t[1], 2 * i + b, yb_hi, yb_lo, 4 * i + 2 * b)
            with dve.Fori(0, NB) as i:
                for b in range(2):
                    split("mix", i, b * HID, (b + 1) * HID)
                    times_row("mix", i, (b + 1) * HID, b, t[b], gate_scaled, 4 * i + 2 * b)
                split("mix", i, 2 * HID, 2 * HID + HGM)
                for b in range(2):
                    if b:
                        split("mix", i, 2 * HID + HGM, PER["mix"])
                    acc_full(dve, "mix", i, 2 * HID + HGM + b * HID)
                    for j in range(2):
                        dve.wait_ge(gate_sig, 4 * i + 2 * b + j + 1)
                        v.tensor_tensor(piece(t[b], j), piece(accv[b], j), piece(t[b], j), ALU.mult).then_inc(mix_prod, 1)
                    dve.wait_ge(mix_prod, 6 * i + 2 * b + 2)
                    dve.sem_inc(acc_read[b], 1)
                for j in range(2):
                    v.tensor_tensor(piece(t[2], j), piece(t[0], j), piece(t[1], j), ALU.add).then_inc(mix_prod, 1)
                take_lo(mhi, mlo, t[2], i, mix_hi, mix_lo, 2 * i)

            def residual(n, phase, halves, gain):
                s = res[n]
                with dve.Fori(0, 2) as i:
                    for b in range(2):
                        split(phase, i, b * halves, (b + 1) * halves)
                        acc_full(dve, phase, i, (b + 1) * halves)
                        q = 4 * i + 2 * b
                        for j in range(2):
                            v.tensor_tensor(tiles(xT, 2 * i + b, j), piece(accv[b], j), tiles(xT, 2 * i + b, j), ALU.add).then_inc(s["x"], 1)
                        dve.wait_ge(s["x"], q + 2)
                        dve.sem_inc(acc_read[b], 1)
                        for j in range(2):
                            v.tensor_tensor(piece(t[0], j), tiles(xT, 2 * i + b, j),
                                            bc(cols[:, ds(gain + 4 * (2 * i + b) + 2 * j, 2)], SEQ), ALU.mult).then_inc(s["gain"], 1)
                        take_lo(ahi, alo, t[0], 2 * i + b, s["hi"], s["lo"], q)

            residual(0, "out", HID, C_FFN)

            def ffn(i, first=False):
                if first:
                    split("ffn", i, 0, 5)
                    mean(1)
                split("ffn", i, 5 if first else 0, HID)
                if first:
                    dve.wait_ge(r_done, 2)
                times_row("ffn", i, HID, 0, t[0], ff_scaled, 2 * i)
                split("ffn", i, HID, 2 * HID)
                acc_full(dve, "ffn", i, 2 * HID)
                for j in range(2):
                    dve.wait_ge(ff_gate, 2 * i + j + 1)
                    v.tensor_tensor(piece(t[2], j), piece(accv[1], j), piece(t[1], j), ALU.mult).then_inc(ff_prod, 1)
                dve.wait_ge(ff_prod, 2 * i + 2)
                dve.sem_inc(acc_read[1], 1)
                take_lo(fhi, flo, t[2], i, ff_hi, ff_lo, 2 * i)

            ffn(0, first=True)
            with dve.Fori(1, FB) as i:
                ffn(i)
            residual(1, "down", HFF, C_PLE)
            for b in range(NB):
                split("proj", 0, b, b + 1)
                acc_full(dve, "proj", 0, b + 1)
                v.tensor_copy(pw[:, 4 * b:4 * b + 4], accv[b % 2]).then_inc(pw_done, 1)
                dve.wait_ge(pw_done, b + 1)
                dve.sem_inc(acc_read[b % 2], 1)
            for i in range(2):
                for b in range(2):
                    if i == 0 and b == 0:
                        split("ple", 0, 0, 5)
                        mean(2)
                        split("ple", 0, 5, HID)
                        dve.wait_ge(r_done, 3)
                    else:
                        split("ple", i, b * HID, (b + 1) * HID)
                    times_row("ple", i, (b + 1) * HID, b, t[0], ple_scaled, 4 * i + 2 * b)
                    for j in range(2):
                        if i == 1 and b == 1:
                            dve.wait_ge(ple_sig, 7 + j)
                            v.tensor_tensor(piece(t[0], j), piece(t[0], j), tiles(pw, 3, j), ALU.mult).then_inc(ple_prod, 1)
                        dve.wait_ge(ple_prod, 4 * i + 2 * b + j + 1)
                        v.tensor_tensor(tiles(xT, 2 * i + b, j), tiles(xT, 2 * i + b, j), piece(t[0], j), ALU.add).then_inc(ple_x, 1)
            mean(3)
            dve.wait_ge(r_done, 4)
            dve.wait_ge(ple_gain, 8)
            for c in range(6):
                v.tensor_tensor(xT[:, 2 * c:2 * c + 2], xT[:, 2 * c:2 * c + 2], over(R[:], 2), ALU.mult).then_inc(out_dve, 1)


def halves(w):
    k, n = w.shape
    x = w.reshape(k // (HALF_K * P), HALF_K, P, n // COLS, COLS).transpose(3, 0, 2, 1, 4)
    return np.ascontiguousarray(x.reshape(-1, HALF_K * COLS))


def features(a, n):
    return np.ascontiguousarray(a.reshape(SEQ, n, P).transpose(2, 1, 0))


def kernel(**inputs):
    from concourse import bacc
    from concourse.bass_utils import run_bass_kernel_spmd

    a = {k: np.asarray(v) for k, v in inputs.items()}
    w_in = a["w_in"][0]
    ba0 = 2 * GM + 4 * D
    wba = np.zeros((D, 48), np.float32)
    wba[:, 0:16] = w_in[:, ba0:ba0 + HEADS]
    wba[:, 32:48] = w_in[:, ba0 + HEADS:ba0 + 2 * HEADS]

    def per_feature(x):
        return x.reshape(-1, P).T

    conv_w = a["dn_conv_w"][0]
    arrays = {
        "win": halves(np.concatenate([w_in[:, :ba0], w_in[:, ba0 + 2 * HEADS:]], axis=1)),
        "wba": np.ascontiguousarray(wba.reshape(KD, P, 48).transpose(1, 0, 2)),
        "wa": halves(a["w_branch_a"][0]), "wb": halves(a["w_branch_b"][0]), "wo": halves(a["w_out"][0]),
        "wgu": halves(a["w_gate_up"][0]), "wd": halves(a["w_down"][0]), "wpg": halves(a["w_ple_gate"][0]),
        "wpp": halves(a["w_ple_proj"][0]),
        "xT": features(a["x"][0], KD), "pT": features(a["p"][0, 0], PLE // P),
        "cols": np.ascontiguousarray(np.concatenate([
            per_feature(a["norm_mix"][0]), per_feature(a["norm_ffn"][0]), per_feature(a["ple_norm"][0]),
            per_feature(a["norm_final"]), per_feature(a["gm_v_norm"][0]), per_feature(a["dn_out_norm"][0])]
            + [per_feature(conv_w[t]) for t in range(4)], axis=1)),
        "hv": np.ascontiguousarray(np.stack([a["dn_dt_bias"][0], a["dn_a_log"][0]], axis=1)),
        "gmw": np.ascontiguousarray(a["gm_w_s"][0].transpose(2, 0, 1)),
        "gmb": np.ascontiguousarray(a["gm_b_s"][0].reshape(1, GM)),
    }
    nc = bacc.Bacc("TRN2", target_bir_lowering=False, num_devices=1)
    args = [nc.dram_tensor(f"in_{k}", x.shape, mybir.dt.from_np(x.dtype), kind="ExternalInput").ap() for k, x in arrays.items()]
    out = nc.dram_tensor("out_T", (P, KD, SEQ), F32, kind="ExternalOutput").ap()
    build(nc, *args, out)
    r = run_bass_kernel_spmd(nc, [{f"in_{k}": x for k, x in arrays.items()}], core_ids=[0])
    got = np.asarray(r.results[0]["out_T"])
    return np.ascontiguousarray(got.transpose(2, 1, 0)).reshape(1, SEQ, D)
```
